# Optimizing a Trainium2 kernel written in Bass

```python
import math
import jax, jax.numpy as jnp
from jax import lax
import numpy as np

D_MODEL = 1024
BATCH = 1
SEQ = 256
DEPTH = 2

N_MIXERS = 2
N_CONV_LAYERS = (DEPTH + 1) // 2
N_SSD_LAYERS = DEPTH // 2
RMS_EPS = 1e-6
FFN_RESIDUAL_WEIGHT = 0.5
D_FF = 2816
SC_WIDTH = 3
SSD_EXPAND = 2
D_INNER = SSD_EXPAND * D_MODEL
SSD_HEAD_DIM = 64
SSD_HEADS = D_INNER // SSD_HEAD_DIM
SSD_GROUPS = 8
SSD_HPG = SSD_HEADS // SSD_GROUPS
D_STATE = 128
SSD_CONV_WIDTH = 4
SSD_CONV_DIM = D_INNER + 2 * SSD_GROUPS * D_STATE
SSD_IN_DIM = D_INNER + SSD_CONV_DIM + SSD_HEADS
SSD_CHUNK = 128
N_MEM = 256
XA_HEADS = 4
XA_HEAD_DIM = D_MODEL // XA_HEADS

kernel_name = "hybrid_shortconv_ssd_macaron_memxattn"

def _rmsnorm(x, g):
    xf = x.astype(jnp.float32)
    y = xf * lax.rsqrt(jnp.mean(xf * xf, axis=-1, keepdims=True) + RMS_EPS)
    return (y * g.astype(jnp.float32)).astype(x.dtype)

def _swiglu(h, w_gate_up, w_down):
    g, u = jnp.split(h @ w_gate_up, 2, axis=-1)
    return (jax.nn.silu(g) * u) @ w_down

def _causal_depthwise_conv(x, kernel):
    k = kernel.shape[0]
    return lax.conv_general_dilated(
        x, kernel[:, None, :].astype(x.dtype), window_strides=(1,),
        padding=[(k - 1, 0)], dimension_numbers=("NWC", "WIO", "NWC"),
        feature_group_count=x.shape[-1])

def _short_conv_mixer(h, w_in, kernel, w_out):
    b_gate, c_gate, v = jnp.split(h @ w_in, 3, axis=-1)
    return (b_gate * _causal_depthwise_conv(c_gate * v, kernel)) @ w_out

def _segsum_exp(a_cum):
    q = a_cum.shape[-1]
    diff = a_cum[..., :, None] - a_cum[..., None, :]
    mask = jnp.tril(jnp.ones((q, q), dtype=bool))
    return jnp.exp(jnp.where(mask, diff, -jnp.inf))

def _ssd_mixer(h, w_in, conv_kernel, conv_bias, dt_bias, a_log, d_skip, gate_norm, w_out):
    f32 = jnp.float32
    bsz, seq, _ = h.shape
    nc = seq // SSD_CHUNK
    z, xbc, dt = jnp.split(h @ w_in, [D_INNER, D_INNER + SSD_CONV_DIM], axis=-1)
    xbc = jax.nn.silu(_causal_depthwise_conv(xbc, conv_kernel) + conv_bias)
    xs, bm, cm = jnp.split(xbc, [D_INNER, D_INNER + SSD_GROUPS * D_STATE], axis=-1)

    dt = jax.nn.softplus(dt.astype(f32) + dt_bias.astype(f32))
    a = -jnp.exp(a_log.astype(f32))
    da = (dt * a).reshape(bsz, nc, SSD_CHUNK, SSD_GROUPS, SSD_HPG)
    da = da.transpose(0, 3, 4, 1, 2)
    a_cum = jnp.cumsum(da, axis=-1)

    x = xs.astype(f32).reshape(bsz, nc, SSD_CHUNK, SSD_GROUPS, SSD_HPG, SSD_HEAD_DIM)
    xdt = x * dt.reshape(bsz, nc, SSD_CHUNK, SSD_GROUPS, SSD_HPG)[..., None]
    bm = bm.astype(f32).reshape(bsz, nc, SSD_CHUNK, SSD_GROUPS, D_STATE)
    cm = cm.astype(f32).reshape(bsz, nc, SSD_CHUNK, SSD_GROUPS, D_STATE)

    decay = _segsum_exp(a_cum)
    cb = jnp.einsum("bclgn,bcsgn->bgcls", cm, bm)
    y_diag = jnp.einsum("bgcls,bgrcls,bcsgrp->bclgrp", cb, decay, xdt)

    decay_states = jnp.exp(a_cum[..., -1:] - a_cum)
    states = jnp.einsum("bcsgn,bgrcs,bcsgrp->bcgrpn", bm, decay_states, xdt)
    chunk_decay = jnp.exp(a_cum[..., -1])

    def step(prev, inp):
        st, dec = inp
        return prev * dec[..., None, None] + st, prev

    init = jnp.zeros((bsz, SSD_GROUPS, SSD_HPG, SSD_HEAD_DIM, D_STATE), f32)
    _, prev_states = lax.scan(step, init, (jnp.moveaxis(states, 1, 0),
                                           jnp.moveaxis(chunk_decay, -1, 0)))

    y_off = jnp.einsum("bclgn,cbgrpn,bgrcl->bclgrp", cm, prev_states, jnp.exp(a_cum))
    y = y_diag + y_off + x * d_skip.astype(f32).reshape(SSD_GROUPS, SSD_HPG)[:, :, None]
    y = y.reshape(bsz, seq, D_INNER) * jax.nn.silu(z.astype(f32))

    yg = y.reshape(bsz, seq, SSD_GROUPS, D_INNER // SSD_GROUPS)
    yg = yg * lax.rsqrt(jnp.mean(yg * yg, axis=-1, keepdims=True) + RMS_EPS)
    y = yg.reshape(bsz, seq, D_INNER) * gate_norm.astype(f32)
    return y.astype(h.dtype) @ w_out

def _memory_cross_attn(h, mem_n, w_q, w_kv, w_o):
    f32 = jnp.float32
    bsz, seq, _ = h.shape
    q = (h @ w_q).reshape(bsz, seq, XA_HEADS, XA_HEAD_DIM)
    k, v = jnp.split(mem_n @ w_kv, 2, axis=-1)
    k = k.reshape(bsz, N_MEM, XA_HEADS, XA_HEAD_DIM)
    v = v.reshape(bsz, N_MEM, XA_HEADS, XA_HEAD_DIM)
    s = jnp.einsum("bshd,bmhd->bhsm", q.astype(f32), k.astype(f32)) * (XA_HEAD_DIM ** -0.5)
    p = jax.nn.softmax(s, axis=-1)
    o = jnp.einsum("bhsm,bmhd->bshd", p, v.astype(f32)).reshape(bsz, seq, D_MODEL)
    return o.astype(h.dtype) @ w_o

def setup_inputs(seed: int = 0) -> dict:
    key = jax.random.key(seed)
    ks = iter(jax.random.split(key, 32))
    f32 = jnp.float32

    def nrm(shape, fan_in):
        return jax.random.normal(next(ks), shape, f32) * (fan_in ** -0.5)

    def gain(shape):
        return 1.0 + 0.02 * jax.random.normal(next(ks), shape, f32)

    x = jax.random.normal(next(ks), (BATCH, SEQ, D_MODEL), f32)
    mem = jax.random.normal(next(ks), (BATCH, N_MEM, D_MODEL), f32)

    ffn_norm = gain((DEPTH, 2, D_MODEL))
    ffn_w_gate_up = nrm((DEPTH, 2, D_MODEL, 2 * D_FF), D_MODEL)
    ffn_w_down = nrm((DEPTH, 2, D_FF, D_MODEL), D_FF)
    mix_norm = gain((DEPTH, D_MODEL))

    conv_w_in = nrm((N_CONV_LAYERS, D_MODEL, 3 * D_MODEL), D_MODEL)
    conv_kernel = nrm((N_CONV_LAYERS, SC_WIDTH, D_MODEL), SC_WIDTH)
    conv_w_out = nrm((N_CONV_LAYERS, D_MODEL, D_MODEL), D_MODEL)

    ssd_w_in = nrm((N_SSD_LAYERS, D_MODEL, SSD_IN_DIM), D_MODEL)
    ssd_conv_kernel = nrm((N_SSD_LAYERS, SSD_CONV_WIDTH, SSD_CONV_DIM), SSD_CONV_WIDTH)
    ssd_conv_bias = 0.02 * jax.random.normal(next(ks), (N_SSD_LAYERS, SSD_CONV_DIM), f32)
    dt0 = jnp.exp(jax.random.uniform(next(ks), (N_SSD_LAYERS, SSD_HEADS), f32)
                  * (math.log(0.1) - math.log(0.001)) + math.log(0.001))
    dt0 = jnp.maximum(dt0, 1e-4)
    ssd_dt_bias = dt0 + jnp.log(-jnp.expm1(-dt0))
    ssd_a_log = jnp.log(jax.random.uniform(next(ks), (N_SSD_LAYERS, SSD_HEADS), f32, 1.0, 16.0))
    ssd_d_skip = gain((N_SSD_LAYERS, SSD_HEADS))
    ssd_gate_norm = gain((N_SSD_LAYERS, D_INNER))
    ssd_w_out = nrm((N_SSD_LAYERS, D_INNER, D_MODEL), D_INNER)

    xa_norm = gain((DEPTH, D_MODEL))
    xa_mem_norm = gain((DEPTH, D_MODEL))
    xa_w_q = nrm((DEPTH, D_MODEL, D_MODEL), D_MODEL)
    xa_w_kv = nrm((DEPTH, D_MODEL, 2 * D_MODEL), D_MODEL)
    xa_w_o = nrm((DEPTH, D_MODEL, D_MODEL), D_MODEL)

    final_norm = gain((D_MODEL,))

    return {
        "x": x, "mem": mem,
        "ffn_norm": ffn_norm, "ffn_w_gate_up": ffn_w_gate_up, "ffn_w_down": ffn_w_down,
        "mix_norm": mix_norm,
        "conv_w_in": conv_w_in, "conv_kernel": conv_kernel, "conv_w_out": conv_w_out,
        "ssd_w_in": ssd_w_in, "ssd_conv_kernel": ssd_conv_kernel, "ssd_conv_bias": ssd_conv_bias,
        "ssd_dt_bias": ssd_dt_bias, "ssd_a_log": ssd_a_log, "ssd_d_skip": ssd_d_skip,
        "ssd_gate_norm": ssd_gate_norm, "ssd_w_out": ssd_w_out,
        "xa_norm": xa_norm, "xa_mem_norm": xa_mem_norm, "xa_w_q": xa_w_q,
        "xa_w_kv": xa_w_kv, "xa_w_o": xa_w_o,
        "final_norm": final_norm,
    }

def reference(x, mem, ffn_norm, ffn_w_gate_up, ffn_w_down, mix_norm,
              conv_w_in, conv_kernel, conv_w_out,
              ssd_w_in, ssd_conv_kernel, ssd_conv_bias, ssd_dt_bias, ssd_a_log,
              ssd_d_skip, ssd_gate_norm, ssd_w_out,
              xa_norm, xa_mem_norm, xa_w_q, xa_w_kv, xa_w_o, final_norm):
    for i in range(DEPTH):
        x = x + FFN_RESIDUAL_WEIGHT * _swiglu(_rmsnorm(x, ffn_norm[i, 0]),
                                              ffn_w_gate_up[i, 0], ffn_w_down[i, 0])
        h = _rmsnorm(x, mix_norm[i])
        j = i // N_MIXERS
        if i % N_MIXERS == 0:
            y = _short_conv_mixer(h, conv_w_in[j], conv_kernel[j], conv_w_out[j])
        else:
            y = _ssd_mixer(h, ssd_w_in[j], ssd_conv_kernel[j], ssd_conv_bias[j],
                           ssd_dt_bias[j], ssd_a_log[j], ssd_d_skip[j],
                           ssd_gate_norm[j], ssd_w_out[j])
        x = x + y
        x = x + _memory_cross_attn(_rmsnorm(x, xa_norm[i]), _rmsnorm(mem, xa_mem_norm[i]),
                                   xa_w_q[i], xa_w_kv[i], xa_w_o[i])
        x = x + FFN_RESIDUAL_WEIGHT * _swiglu(_rmsnorm(x, ffn_norm[i, 1]),
                                              ffn_w_gate_up[i, 1], ffn_w_down[i, 1])
    return _rmsnorm(x, final_norm)


_drawn_inputs = setup_inputs


def setup_inputs(seed=0):
    import zlib

    import numpy as np

    out = dict(_drawn_inputs(seed))
    spreads = {}
    factors = {'ffn_norm': 3.138,
     'ssd_conv_bias': 3.611,
     'ssd_d_skip': 8.0,
     'ssd_gate_norm': 4.805,
     'xa_norm': 8.0,
     'xa_mem_norm': 8.0,
     'final_norm': 2.825}
    for name, (base, spread) in spreads.items():
        noise = np.random.default_rng([zlib.crc32(name.encode()), seed]).standard_normal(out[name].shape)
        drawn = base * np.exp(spread * noise) if base else spread * noise
        out[name] = __import__('jax').numpy.asarray(drawn.astype(out[name].dtype))
    for name, factor in factors.items():
        out[name] = (out[name] * factor).astype(out[name].dtype)
    return out
```

```python
from contextlib import ExitStack

import numpy as np

import concourse.bass as bass
from concourse import mybir

F32 = mybir.dt.float32
F32R = mybir.dt.float32r
ALU = mybir.AluOpType
ACT = mybir.ActivationFunctionType
AX = mybir.AxisListType

P = 128
SEQ = 256
D_MODEL = 1024
KT = D_MODEL // P
D_FF = 2816
FT = D_FF // P
N_MEM = 256
HEADS = 4
HEAD_W = D_MODEL // HEADS
GROUPS = 8
HPG = 4
HD = 64
SSD_HEADS = GROUPS * HPG
CHUNK = 128
D_INNER = SSD_HEADS * HD
IT = D_INNER // P
GW = D_INNER // GROUPS
EPS = 1e-6
MASKED = -1e30

UNIT_W = KT * P
DOWN_W = FT // 2 * P
SLOTS = 4
AHEAD = 3

N_NORMS = 11
C_GAIN = 0
C_CONVK = C_GAIN + N_NORMS * KT
C_SSDK = C_CONVK + KT * 3
C_SSDB = C_SSDK + 32 * 4
C_GATE = C_SSDB + 32
C_DTB = C_GATE + IT
C_ALOG = C_DTB + SSD_HEADS
C_DSKIP = C_ALOG + SSD_HEADS
C_EYE = C_DSKIP + SSD_HEADS
C_TRI = C_EYE + P
C_MASK = C_TRI + P
C_ALL = C_MASK + P
NORM_MIX0, NORM_XA0, NORM_MIX1, NORM_XA1, NORM_FINAL, NORM_MEM = 1, 2, 5, 6, 8, 9

PHASES = [
    ("gu0", 44, UNIT_W), ("down0", 16, DOWN_W), ("conv_in", 24, UNIT_W), ("conv_out", 8, UNIT_W),
    ("q0", 8, UNIT_W), ("k0", 8, UNIT_W), ("v0", 8, UNIT_W), ("o0", 8, UNIT_W),
    ("gu1", 44, UNIT_W), ("down1", 16, DOWN_W), ("gu2", 44, UNIT_W), ("down2", 16, DOWN_W),
    ("z", 16, UNIT_W), ("xbc", 32, UNIT_W), ("ssd_out", 16, UNIT_W),
    ("q1", 8, UNIT_W), ("k1", 8, UNIT_W), ("v1", 8, UNIT_W), ("o1", 8, UNIT_W),
    ("gu3", 44, UNIT_W), ("down3", 16, DOWN_W),
]
LAST_NORM = 8


def plan():
    first, uses, n, used = {}, {}, 0, [0] * 4
    for name, units, _ in PHASES:
        first[name], uses[name] = n, list(used)
        n += units
        tiles = units // 2 if name[:4] == "down" or name == "ssd_out" else units
        banks = 2 if name[:4] == "down" else 4
        for b in range(banks):
            used[b] += tiles // banks
    return first, uses, n


def trunk(nc, x_t, mem_t, small, w_gu, w_down, w_conv_in, w_conv_out, w_z, w_xbc, w_dt, w_ssd_out,
          w_q, w_k, w_v, w_o, out_t):
    first, uses, n_units = plan()
    width = []
    for _, units, w in PHASES:
        width += [w] * units

    with ExitStack() as ctx:
        def sb(name, shape, dt=F32):
            return ctx.enter_context(nc.sbuf_tensor(name, shape, dt))

        def sem(name):
            return ctx.enter_context(nc.semaphore(name))

        x = sb("x", [P, KT, SEQ])
        h_hi, h_lo = sb("h_hi", [P, KT, SEQ], F32R), sb("h_lo", [P, KT, SEQ], F32R)
        a_hi, a_lo = sb("a_hi", [P, FT, SEQ], F32R), sb("a_lo", [P, FT, SEQ], F32R)
        raw = sb("raw", [P, SLOTS, DOWN_W])
        w_hi = [sb(f"w_hi{s}", [P, DOWN_W], F32R) for s in range(SLOTS)]
        w_lo = [sb(f"w_lo{s}", [P, DOWN_W], F32R) for s in range(SLOTS)]
        mark = nc.sbuf_base
        mn_hi, mn_lo = sb("mn_hi", [P, KT, N_MEM], F32R), sb("mn_lo", [P, KT, N_MEM], F32R)
        z = nc.alloc_sbuf_tensor_at("z", [P, 2, D_INNER], F32, offset=mark + (-mark) % 32)
        mark = nc.sbuf_base
        k_hi, k_lo = sb("k_hi", [P, KT, N_MEM], F32R), sb("k_lo", [P, KT, N_MEM], F32R)
        v_hi, v_lo = sb("v_hi", [P, 2, D_MODEL], F32R), sb("v_lo", [P, 2, D_MODEL], F32R)
        decay = nc.alloc_sbuf_tensor_at("decay", [P, GROUPS, 2, HPG * CHUNK], F32, offset=mark + (-mark) % 32)
        mark = nc.sbuf_base
        mem = sb("mem", [P, KT, N_MEM])
        at = [mark + (-mark) % 32]

        def over(name, shape, dt=F32):
            t = nc.alloc_sbuf_tensor_at(name, shape, dt, offset=at[0])
            at[0] += 4 * int(np.prod(shape[1:]))
            return t

        probs_all = nc.alloc_sbuf_tensor_at("probs", [P, HEADS, 2, N_MEM], F32, offset=at[0])
        probs = [probs_all[:, h] for h in range(HEADS)]
        m = over("m", [P, 2 * HPG * CHUNK])
        wdt = over("wdt", [P, KT, SSD_HEADS])
        wdt_hi, wdt_lo = over("wdt_hi", [P, KT, SSD_HEADS], F32R), over("wdt_lo", [P, KT, SSD_HEADS], F32R)
        assert at[0] <= nc.sbuf_base
        cst = sb("cst", [P, C_ALL])
        ones = sb("ones", [P, P])
        ones_r, eye_r, tri_r, mask_r = (sb(n, [P, P], F32R) for n in ("ones_r", "eye_r", "tri_r", "mask_r"))
        ssq, sq = sb("ssq", [P, SEQ]), sb("sq", [P, SEQ])
        root, var, rms, rms_k, rms_mem = sb("root", [P, SEQ]), sb("var", [P, SEQ]), sb("rms", [P, SEQ]), sb("rms_k", [P, SEQ]), sb("rms_mem", [P, SEQ])
        t1_all, t2_all, gate_all = (sb(n, [P, 2, SEQ]) for n in ("t1", "t2", "gate"))
        t1, t2, gate = ([t[:, i] for i in range(2)] for t in (t1_all, t2_all, gate_all))
        padded = sb("padded", [P, 4 + SEQ])
        acc = [sb(f"acc{i}", [P, SEQ]) for i in range(2)]
        pt_hi, pt_lo = a_hi[:, 16:18, :], a_lo[:, 16:18, :]
        m_hi, m_lo = (a[:, 16:20, :].rearrange("p a n -> p (a n)") for a in (a_hi, a_lo))
        c_hi, c_lo = a_hi[:, 20:22, :], a_lo[:, 20:22, :]
        mx, neg_mx, tot, inv_tot = (sb(n, [P, 2]) for n in ("mx", "neg_mx", "tot", "inv_tot"))
        act_xbc = [raw[:, s, UNIT_W:UNIT_W + SEQ] for s in range(4)]
        b_hi, b_lo = (w[0][:, UNIT_W:UNIT_W + SEQ] for w in (w_hi, w_lo))
        bn_hi, bn_lo = (w[0][:, UNIT_W + SEQ:DOWN_W] for w in (w_hi, w_lo))
        xs_hi, xs_lo = (w[1][:, UNIT_W:UNIT_W + GW] for w in (w_hi, w_lo))
        st_hi, st_lo = (w[2][:, UNIT_W:UNIT_W + GW] for w in (w_hi, w_lo))
        xn_hi, xn_lo = sb("xn_hi", [P, 2, GW], F32R), sb("xn_lo", [P, 2, GW], F32R)
        xd, y = sb("xd", [P, 2, GW]), sb("y", [P, 2, GW])
        y_off, xs = t1
        sq_y, zs = t2_all, gate_all
        var_y, rms_y = sb("var_y", [P, 2]), sb("rms_y", [P, 2])
        rms_n, var_n, root_n, sum_y = (sb(n, [P, 2]) for n in ("rms_n", "var_n", "root_n", "sum_y"))
        H = SSD_HEADS
        d = {n: sb("dt_" + n, [P, 2, H]) for n in ("sp", "nacum")}
        for i, n in enumerate(("x", "abs", "e", "u", "ln", "c", "inv", "da")):
            c0 = UNIT_W + SEQ + i % 2 * 2 * H
            d[n] = raw[:, i // 2, c0:c0 + 2 * H].rearrange("p (c h) -> p c h", c=2)
        da_hi, da_lo = sb("da_hi", [P, 2, H], F32R), sb("da_lo", [P, 2, H], F32R)
        a_exp, e_acum, dsd, rest = (sb(n, [P, H]) for n in ("a_exp", "e_acum", "dsd", "rest"))

        bank = [ctx.enter_context(nc.psum_tensor(f"bank{i}", [P, 512], F32)) for i in range(8)]

        x_in, mem_in, cst_in, dt_in = sem("x_in"), sem("mem_in"), sem("cst_in"), sem("dt_in")
        landed = [sem(f"landed{s}") for s in range(SLOTS)]
        hi_ready, lo_ready = sem("hi_ready"), sem("lo_ready")
        unit_done = sem("unit_done")
        evac = [sem(f"evac{b}") for b in range(4)]
        silu_ready = sem("silu_ready")
        ahi_ready, a_ready = sem("ahi_ready"), sem("a_ready")
        x_ready = sem("x_ready")
        hhi_ready, h_ready = sem("hhi_ready"), sem("h_ready")
        ssq_step, ss_done = sem("ssq_step"), sem("ss_done")
        consts = sem("consts")
        var_ready, root_ready = sem("var_ready"), sem("root_ready")
        small_var_ready, small_root_ready = sem("small_var_ready"), sem("small_root_ready")
        ones_set, pads_set = sem("ones_set"), sem("pads_set")
        dve_step, act_step, pool_step = sem("dve_step"), sem("act_step"), sem("pool_step")
        mem_val, mem_hi, mem_lo = sem("mem_val"), sem("mem_hi"), sem("mem_lo")
        kv_hi = sem("kv_hi")
        s_done, max_ready, exp_ready, probs_ready = sem("s_done"), sem("max_ready"), sem("exp_ready"), sem("probs_ready")
        pt_done, pthi_ready, pt_ready = sem("pt_done"), sem("pthi_ready"), sem("pt_ready")
        o_done, ohi_ready, o_ready = sem("o_done"), sem("ohi_ready"), sem("o_ready")
        dt_done, dt_x, dt_e, dt_u, dt_ln, dt_a = (sem(n) for n in ("dt_done", "dt_x", "dt_e", "dt_u", "dt_ln", "dt_a"))
        wdt_hi_ready, wdt_ready = sem("wdt_hi_ready"), sem("wdt_ready")
        da_val, dahi_ready, da_ready = sem("da_val"), sem("dahi_ready"), sem("da_ready")
        acum_done, acum_ready, acum_exp, dsd_ready = sem("acum_done"), sem("acum_ready"), sem("acum_exp"), sem("dsd_ready")
        l_done, decay_ready = sem("l_done"), sem("decay_ready")
        conv_ready, xbc_ready = sem("conv_ready"), sem("xbc_ready")
        bhi_ready, b_ready = sem("bhi_ready"), sem("b_ready")
        cb_done, bnhi_ready, bn_ready = sem("cb_done"), sem("bnhi_ready"), sem("bn_ready")
        m_ready, mhi_ready, mlo_ready = sem("m_ready"), sem("mhi_ready"), sem("mlo_ready")
        xt_done, xnhi_ready, xn_ready, xd_ready = sem("xt_done"), sem("xnhi_ready"), sem("xn_ready"), sem("xd_ready")
        xs_ready, xshi_ready, xslo_ready = sem("xs_ready"), sem("xshi_ready"), sem("xslo_ready")
        state_done, sthi_ready, st_ready = sem("state_done"), sem("sthi_ready"), sem("st_ready")
        y_done, yo_done, zs_ready, y_ready, ysq_ready, yn_ready = (
            sem(n) for n in ("y_done", "yo_done", "zs_ready", "y_ready", "ysq_ready", "yn_ready"))
        yt_done, yhi_ready, yt_ready = sem("yt_done"), sem("yhi_ready"), sem("yt_ready")
        out_ready, out_landed = sem("out_ready"), sem("out_landed")

        def at_least(eng, s, value):
            if isinstance(value, int) and value <= 0:
                return
            eng.wait_ge(s, value)

        def gain(b, k):
            return cst[:, C_GAIN + b * KT + k:C_GAIN + b * KT + k + 1]

        def col(c0, i):
            return cst[:, c0 + i:c0 + i + 1]

        def bank_use(phase, t, banks=4):
            return t % banks, uses[phase][t % banks] + t // banks

        FFN_A = {0: 0, 1: FT + KT + KT, 2: 2 * FT + 2 * KT, 3: 3 * FT + 3 * KT}
        CONV_A, Q_A = FT, {0: FT + KT, 1: 3 * FT + 2 * KT}
        X_COUNT = {"down0": 0, "conv_out": KT, "down1": 2 * KT, "down2": 3 * KT, "down3": 4 * KT}
        OUT_NORM = {"down0": 1, "conv_out": 2, "o0": 3, "down1": 4, "down2": 5, "ssd_out": 6, "o1": 7, "down3": 8}
        SS_INDEX = {0: 0, "mem": 1, 1: 2, 2: 3, 3: 4, 4: 5, 5: 6, 6: 7, 7: 8, 8: 9}

        def ssq_count(b):
            return (SS_INDEX[b] + 1) * (2 * KT - 1)

        def x_signal(phase, k):
            if phase in X_COUNT:
                return x_ready, X_COUNT[phase] + k + 1
            b, use = bank_use(phase, k)
            return evac[b], use + 1

        def a_out(k):
            return mem[:, k, :]

        block = ctx.enter_context(nc.Block())

        @block.sync
        def _(sp):
            sp.dma_start(cst[:, :], small).then_inc(cst_in, 16)
            sp.dma_start(x[:, :, :], x_t).then_inc(x_in, 16)

            def load(n, src, i=0):
                at_least(sp, lo_ready, n - SLOTS + 1 + SLOTS * i)
                sp.dma_start(raw[:, n % SLOTS, 0:width[n]], src).then_inc(landed[n % SLOTS], 16)

            def load_phase(name, w, units):
                n0 = first[name]
                for s in range(SLOTS):
                    load(n0 + s, w[s])
                if name == "gu0":
                    sp.dma_start(mem[:, :, :], mem_t).then_inc(mem_in, 16)
                if units == 2 * SLOTS:
                    for s in range(SLOTS, units):
                        load(n0 + s, w[s])
                else:
                    with sp.Fori(1, units // SLOTS) as i:
                        for s in range(SLOTS):
                            load(n0 + s, w[bass.ds(i * SLOTS + s, 1)].rearrange("a p n -> p (a n)"), i)

            sources = {"gu": w_gu, "down": w_down, "q": w_q, "k": w_k, "v": w_v, "o": w_o}
            whole = {"conv_in": w_conv_in, "conv_out": w_conv_out, "z": w_z, "xbc": w_xbc, "ssd_out": w_ssd_out}
            for name, units, _ in PHASES:
                if name in whole:
                    load_phase(name, whole[name], units)
                else:
                    load_phase(name, sources[name[:-1]][int(name[-1])], units)
                if name == "ssd_out":
                    sp.dma_start(mem[:, :, :], mem_t).then_inc(mem_in, 16)
                if name == "down1":
                    sp.dma_start(wdt[:, :, :], w_dt).then_inc(dt_in, 16)
            for k in range(KT):
                sp.wait_ge(out_ready, k + 1)
                sp.dma_start(out_t[:, k, :], a_out(k)).then_inc(out_landed, 16)
            sp.wait_ge(out_landed, 16 * KT)

        @block.scalar
        def _(act):
            def copy(out, in_, scale=1.0):
                return nc.scalar.activation(out, in_, ACT.Copy, scale=scale)

            def split(n, i=0):
                if n >= n_units:
                    return
                s = n % SLOTS
                act.wait_ge(landed[s], 16 * (n // SLOTS + 1) + 16 * i)
                at_least(act, unit_done, n - SLOTS + 1 + SLOTS * i)
                copy(w_hi[s][:, 0:width[n]], raw[:, s, 0:width[n]]).then_inc(hi_ready, 1)

            def norm(b):
                act.wait_ge(var_ready, SS_INDEX[b] + 1)
                nc.scalar.activation(root[:, :], var[:, :], ACT.Sqrt).then_inc(root_ready, 1)

            def new_h(b, k):
                copy(h_hi[:, k, :], x[:, k, :], gain(b, k)).then_inc(hhi_ready, 1)

            def a_part(j, count, src, signal, i=None):
                act.wait_ge(*signal)
                copy(a_hi[:, j, :], src).then_inc(ahi_ready, 1)

            def ffn_unit(f, n, s, i, j_of, opening=False):
                split(n + AHEAD, i)
                q, up = s // 2, s % 2
                if opening:
                    norm({0: 0, 1: 3, 2: 4, 3: 7}[f])
                b, use = bank_use(f"gu{f}", n - first[f"gu{f}"])
                act.wait_ge(evac[b], use + 1 + i)
                if not up:
                    b_up, use_up = bank_use(f"gu{f}", n + 1 - first[f"gu{f}"])
                    at_least(act, evac[b_up], use_up + i)
                    nc.scalar.activation(gate[q][:, :], t1[q][:, :], ACT.Silu).then_inc(silu_ready, 1)
                else:
                    copy(j_of(a_hi), t2[q][:, :]).then_inc(ahi_ready, 1)

            def ffn(f):
                n0 = first[f"gu{f}"]
                turns = FT // 2
                for s in range(4):
                    ffn_unit(f, n0 + s, s, 0, lambda t, s=s: t[:, s // 2, :], opening=s == 0)
                with act.Fori(1, turns - 1) as i:
                    for s in range(4):
                        ffn_unit(f, n0 + s, s, i, lambda t, s=s: t[:, bass.ds(2 * i + s // 2, 1), :].rearrange("p a n -> p (a n)"))
                for s in range(4):
                    n = n0 + 4 * (turns - 1) + s
                    ffn_unit(f, n, s, 0, lambda t, s=s: t[:, 2 * (turns - 1) + s // 2, :])
                project_out(f"down{f}", 2)

            def project_out(phase, per_tile):
                n0 = first[phase]
                for k in range(KT):
                    for u in range(per_tile):
                        split(n0 + per_tile * k + u + AHEAD)
                    b = OUT_NORM[phase]
                    if b <= 7:
                        act.wait_ge(*x_signal(phase, k))
                        new_h(b, k)

            def conv():
                n0 = first["conv_in"]
                for t in range(3 * KT):
                    split(n0 + t + AHEAD)
                    if t == 0:
                        norm(NORM_MIX0)
                    if t % 3 == 2:
                        b, use = bank_use("conv_in", t)
                        act.wait_ge(evac[b], use + 1)
                        copy(a_hi[:, t // 3, :], t2[t // 3 % 2][:, :]).then_inc(ahi_ready, 1)
                project_out("conv_out", 1)

            def attention(layer):
                n0 = first[f"q{layer}"]
                for s in range(24):
                    split(n0 + s + AHEAD)
                    if s == 0:
                        norm(2 if layer == 0 else 6)
                    if s < KT:
                        act.wait_ge(mem_val, KT * layer + s + 1)
                        copy(mn_hi[:, s, :], gate[s % 2][:, :]).then_inc(mem_hi, 1)
                        b, use = bank_use(f"q{layer}", s)
                        act.wait_ge(evac[b], use + 1)
                        copy(a_hi[:, KT + s, :], t2[s % 2][:, :]).then_inc(ahi_ready, 1)
                    elif s < 2 * KT:
                        act.wait_ge(unit_done, n0 + s + 1)
                        copy(k_hi[:, s - KT, :], bank[s % 4][:, 0:N_MEM]).then_inc(kv_hi, 1)
                    elif s % 2:
                        act.wait_ge(unit_done, n0 + s + 1)
                        c = (s - 2 * KT) // 2
                        for mt in range(2):
                            copy(v_hi[:, mt, c * 256:c * 256 + 256], bank[2 * (c % 2) + mt][:, 0:256]).then_inc(kv_hi, 1)
                    for h in range(HEADS):
                        if s == 11 + 2 * h:
                            act.wait_ge(max_ready, HEADS * layer + h + 1)
                            for tt in range(2):
                                nc.scalar.activation(probs[h][:, tt, :], bank[5][:, tt * 256:tt * 256 + 256], ACT.Exp,
                                                     bias=neg_mx[:, tt:tt + 1], accum_out=tot[:, tt:tt + 1]).then_inc(exp_ready, 1)
                        if s == 18 + 2 * h:
                            pt_part(layer, h)
                        if s == 19 + 2 * h:
                            o_part(layer, h)
                pt_part(layer, 3)
                o_part(layer, 3)
                project_out(f"o{layer}", 1)

            def pt_part(layer, h):
                act.wait_ge(pt_done, HEADS * layer + h + 1)
                at_least(act, o_done, HEADS * layer + h)
                copy(pt_hi[:, :, :], bank[6][:, 0:512].rearrange("p (a n) -> p a n", a=2)).then_inc(pthi_ready, 1)

            def o_part(layer, h):
                act.wait_ge(o_done, HEADS * layer + h + 1)
                copy(a_hi[:, 2 * h:2 * h + 2, :], bank[7][:, 0:512].rearrange("p (a n) -> p a n", a=2)).then_inc(ohi_ready, 1)

            def decays(l):
                g, c = l // 2, l % 2
                act.wait_ge(l_done, l + 1)
                for r in range(HPG):
                    hd = g * HPG + r
                    ins = nc.scalar.activation(decay[:, g, c, r * P:r * P + P], bank[5 + l % 2][:, r * P:r * P + P],
                                               ACT.Exp, bias=d["nacum"][:, c, hd:hd + 1])
                ins.then_inc(decay_ready, 1)

            def ssd():
                nz = first["z"]
                lcount = 0
                for s in range(16):
                    split(nz + s + AHEAD)
                    if s == 0:
                        norm(NORM_MIX1)
                        act.wait_ge(small_var_ready, 1)
                        nc.scalar.activation(root_n[:, :], var_n[:, :], ACT.Sqrt).then_inc(small_root_ready, 1)
                    if s == 1:
                        act.wait_ge(dt_x, 1)
                        nc.scalar.activation(d["e"][:, :, :], d["abs"][:, :, :], ACT.Exp, scale=-1.0).then_inc(dt_e, 1)
                        nc.scalar.activation(a_exp[:, :], cst[:, C_ALOG:C_ALOG + H], ACT.Exp).then_inc(dt_e, 1)
                        act.wait_ge(dt_u, 1)
                        nc.scalar.activation(d["ln"][:, :, :], d["u"][:, :, :], ACT.Ln).then_inc(dt_ln, 1)
                        act.wait_ge(da_val, 1)
                        copy(da_hi[:, :, :], d["da"][:, :, :]).then_inc(dahi_ready, 1)
                    if s % 2:
                        act.wait_ge(unit_done, nz + s + 1)
                        g = s // 2
                        for tt in range(2):
                            b = 2 * (g % 2) + tt
                            copy(z[:, tt, g * GW:g * GW + GW], bank[b][:, 0:GW], rms_n[:, tt:tt + 1]).then_inc(evac[b], 1)
                    if s == 2:
                        act.wait_ge(acum_ready, 2)
                        nc.scalar.activation(e_acum[:, :], d["nacum"][:, 1, :], ACT.Exp, scale=-1.0).then_inc(acum_exp, 1)
                        nc.scalar.activation(dsd[:, :], rest[:, :], ACT.Exp).then_inc(acum_exp, 1)
                    if s >= 3:
                        while lcount < min(16, (s - 2) * 16 // 12):
                            decays(lcount)
                            lcount += 1
                nx = first["xbc"]
                for G in range(GROUPS + 1):
                    g = G - 1
                    for q in range(4):
                        if G < GROUPS:
                            split(nx + 4 * G + q + AHEAD)
                            i = 4 * G + q
                            act.wait_ge(conv_ready, i + 1)
                            if q < 2:
                                at_least(act, b_ready, 2 * G)
                                at_least(act, cb_done, 2 * G)
                            else:
                                at_least(act, xt_done, G)
                            nc.scalar.activation(act_xbc[q][:, :], acc[i % 2][:, :], ACT.Silu).then_inc(xbc_ready, 1)
                            act.wait_ge(xbc_ready, i + 1)
                            if q == 0:
                                copy(b_hi[:, :], act_xbc[0][:, :]).then_inc(bhi_ready, 1)
                            if q == 1:
                                copy(c_hi[:, G % 2, :], act_xbc[1][:, :]).then_inc(bhi_ready, 1)
                            if q == 3:
                                act.wait_ge(cb_done, 2 * G + 2)
                                at_least(act, state_done, G)
                                copy(bn_hi[:, :], bank[6][:, 256:384]).then_inc(bnhi_ready, 1)
                                for c in range(2):
                                    act.wait_ge(m_ready, 2 * G + c + 1)
                                    if c == 0:
                                        at_least(act, y_done, G)
                                    copy(m_hi[:, c * 512:c * 512 + 512], m[:, c * 512:c * 512 + 512]).then_inc(mhi_ready, 1)
                        if g >= 0:
                            if q == 0:
                                act.wait_ge(xt_done, G)
                                copy(xn_hi[:, :, :], bank[5][:, :].rearrange("p (a n) -> p a n", a=2)).then_inc(xnhi_ready, 1)
                                act.wait_ge(xs_ready, G)
                                copy(xs_hi[:, :], xs[:, :]).then_inc(xshi_ready, 1)
                                nc.scalar.activation(zs[:, :, :], z[:, :, g * GW:g * GW + GW], ACT.Silu).then_inc(zs_ready, 1)
                            if q == 1:
                                act.wait_ge(state_done, G)
                                copy(st_hi[:, :], bank[4][:, 0:GW]).then_inc(sthi_ready, 1)
                            if q == 2:
                                act.wait_ge(y_ready, G)
                                for c in range(2):
                                    nc.scalar.activation(sq_y[:, c, :], y[:, c, :], ACT.Square,
                                                         accum_out=sum_y[:, c:c + 1]).then_inc(ysq_ready, 1)
                                act.wait_ge(small_var_ready, G + 1)
                                nc.scalar.activation(root_n[:, :], var_y[:, :], ACT.Sqrt).then_inc(small_root_ready, 1)
                            if q == 3:
                                act.wait_ge(yt_done, G)
                                for t in range(2):
                                    j = 2 * g + t
                                    copy(a_hi[:, j, :], bank[5][:, t * SEQ:t * SEQ + SEQ], col(C_GATE, j)).then_inc(yhi_ready, 1)
                project_out("ssd_out", 2)

            act.wait_ge(cst_in, 16)
            act.wait_ge(x_in, 16)
            for k in range(KT):
                new_h(0, k)
            for n in range(AHEAD):
                split(n)
            copy(eye_r[:, :], cst[:, C_EYE:C_EYE + P]).then_inc(consts, 1)
            copy(tri_r[:, :], cst[:, C_TRI:C_TRI + P]).then_inc(consts, 1)
            copy(mask_r[:, :], cst[:, C_MASK:C_MASK + P]).then_inc(consts, 1)
            act.wait_ge(ones_set, 1)
            copy(ones_r[:, :], ones[:, :]).then_inc(consts, 1)
            ffn(0)
            norm("mem")
            conv()
            attention(0)
            ffn(1)
            act.wait_ge(dt_in, 16)
            copy(wdt_hi[:, :, :], wdt[:, :, :]).then_inc(wdt_hi_ready, 1)
            ffn(2)
            ssd()
            attention(1)
            ffn(3)
            norm(NORM_FINAL)

        @block.vector
        def _(dve):
            chain = [0]

            def step(ins):
                chain[0] += 1
                ins.then_inc(dve_step, 1)
                dve.wait_ge(dve_step, chain[0])

            def tt(out, a, b, op=ALU.mult):
                return nc.vector.tensor_tensor(out, a, b, op)

            def stt(out, a, scalar, b, op0=ALU.mult, op1=ALU.mult):
                return nc.vector.scalar_tensor_tensor(out=out, in0=a, scalar=scalar, in1=b, op0=op0, op1=op1)

            def rest_of(lo, value, hi):
                return tt(lo, value, hi.bitcast(F32), ALU.subtract)

            def split(n, i=0):
                if n >= n_units:
                    return
                s = n % SLOTS
                dve.wait_ge(hi_ready, n + 1 + SLOTS * i)
                rest_of(w_lo[s][:, 0:width[n]], raw[:, s, 0:width[n]], w_hi[s][:, 0:width[n]]).then_inc(lo_ready, 1)

            def new_h(b, k):
                dve.wait_ge(hhi_ready, KT * b + k + 1)
                stt(h_lo[:, k, :], x[:, k, :], gain(b, k), h_hi[:, k, :].bitcast(F32), op1=ALU.subtract).then_inc(h_ready, 1)

            def norm(b, out=None):
                dve.wait_ge(ss_done, SS_INDEX[b] + 1)
                out = (rms if out is None else out)[:, :]
                nc.vector.tensor_scalar(var[:, :], bank[4][:, 0:SEQ], 1.0 / D_MODEL, EPS, ALU.mult, ALU.add).then_inc(var_ready, 1)
                inverse_root(out, var[:, :], root[:, :], SS_INDEX[b] + 1)

            def inverse_root(out, v, root_v, count):
                dve.wait_ge(root_ready, count)
                step(nc.vector.reciprocal(out, root_v))
                step(tt(root_v, v, out))
                step(tt(root_v, root_v, out))
                step(nc.vector.tensor_scalar(root_v, root_v, -0.5, 1.5, ALU.mult, ALU.add))
                step(tt(out, out, root_v))

            def scaled(factor):
                step(nc.vector.tensor_scalar(rms_k[:, :], rms[:, :], factor, None, ALU.mult))

            def ffn_unit(f, n, s, i, j, opening=False):
                if opening:
                    split(n + AHEAD)
                    norm({0: 0, 1: 3, 2: 4, 3: 7}[f])
                    scaled(0.5)
                q, up = s // 2, s % 2
                b, use = bank_use(f"gu{f}", n - first[f"gu{f}"])
                dve.wait_ge(unit_done, n + 1 + 4 * i)
                if not up:
                    at_least(dve, silu_ready, FT * f + j - 1)
                    tt(t1[q][:, :], bank[b][:, 0:SEQ], rms[:, :]).then_inc(evac[b], 1)
                else:
                    dve.wait_ge(silu_ready, FT * f + j + 1)
                    at_least(dve, a_ready, FFN_A[f] + j - 1)
                    tt(t2[q][:, :], bank[b][:, 0:SEQ], gate[q][:, :]).then_inc(evac[b], 1)
                if not opening:
                    split(n + AHEAD, i)

            def ffn(f):
                n0 = first[f"gu{f}"]
                turns = FT // 2
                for s in range(4):
                    ffn_unit(f, n0 + s, s, 0, s // 2, opening=s == 0)
                with dve.Fori(1, turns - 1) as i:
                    for s in range(4):
                        ffn_unit(f, n0 + s, s, i, 2 * i + s // 2)
                for s in range(4):
                    ffn_unit(f, n0 + 4 * (turns - 1) + s, s, 0, 2 * (turns - 1) + s // 2)
                project_out(f"down{f}", 2, 2, True)

            def project_out(phase, per_tile, banks, with_scale):
                n0 = first[phase]
                for k in range(KT):
                    if per_tile == 2:
                        split(n0 + 2 * k + AHEAD)
                    dve.wait_ge(unit_done, n0 + per_tile * (k + 1))
                    b, use = bank_use(phase, k, banks)
                    if with_scale:
                        tt(acc[k % 2][:, :], bank[b][:, 0:SEQ], rms_k[:, :]).then_inc(evac[b], 1)
                        dve.wait_ge(evac[b], use + 1)
                        tt(x[:, k, :], x[:, k, :], acc[k % 2][:, :], ALU.add).then_inc(x_ready, 1)
                    else:
                        tt(x[:, k, :], bank[b][:, 0:SEQ], x[:, k, :], ALU.add).then_inc(evac[b], 1)
                    if k < KT - 1 or OUT_NORM[phase] > 7:
                        split(n0 + per_tile * (k + 1) - 1 + AHEAD)
                    if OUT_NORM[phase] <= 7:
                        new_h(OUT_NORM[phase], k)
                    if k == KT - 1 and OUT_NORM[phase] <= 7:
                        split(n0 + per_tile * (k + 1) - 1 + AHEAD)

            def conv():
                n0 = first["conv_in"]
                for t in range(3 * KT):
                    if t == 0:
                        split(n0 + t + AHEAD)
                        norm(NORM_MIX0)
                        step(tt(rms_k[:, :], rms[:, :], rms[:, :]))
                    j, q = t // 3, t % 3
                    b, use = bank_use("conv_in", t)
                    dve.wait_ge(unit_done, n0 + t + 1)
                    if q == 0:
                        tt(t1[0][:, :], bank[b][:, 0:SEQ], rms_k[:, :]).then_inc(evac[b], 1)
                        if t:
                            split(n0 + t + AHEAD)
                        dve.wait_ge(evac[b], use + 1)
                    elif q == 1:
                        tt(padded[:, 2:2 + SEQ], bank[b][:, 0:SEQ], t1[0][:, :]).then_inc(evac[b], 1)
                        split(n0 + t + AHEAD)
                        dve.wait_ge(evac[b], use + 1)
                        step(nc.vector.tensor_scalar(acc[0][:, :], padded[:, 0:SEQ], col(C_CONVK, 3 * j), None, ALU.mult))
                        for w in range(1, 3):
                            step(stt(acc[0][:, :], padded[:, w:w + SEQ], col(C_CONVK, 3 * j + w), acc[0][:, :], op1=ALU.add))
                    else:
                        at_least(dve, a_ready, CONV_A + j - 1)
                        tt(t2[j % 2][:, :], bank[b][:, 0:SEQ], acc[0][:, :]).then_inc(evac[b], 1)
                        split(n0 + t + AHEAD)
                step(nc.vector.tensor_copy(rms_k[:, :], rms[:, :]))
                project_out("conv_out", 1, 4, True)

            def softmax_max(layer, h):
                dve.wait_ge(s_done, HEADS * layer + h + 1)
                if h:
                    dve.wait_ge(exp_ready, 2 * (HEADS * layer + h))
                step(nc.vector.tensor_reduce(mx[:, :], bank[5][:, :].rearrange("p (a n) -> p a n", a=2), AX.X, ALU.max))
                nc.vector.tensor_scalar(neg_mx[:, :], mx[:, :], -1.0, None, ALU.mult).then_inc(max_ready, 1)

            def softmax_norm(layer, h):
                dve.wait_ge(exp_ready, 2 * (HEADS * layer + h) + 2)
                step(nc.vector.reciprocal(inv_tot[:, :], tot[:, :]))
                for t in range(2):
                    nc.vector.tensor_scalar(probs[h][:, t, :], probs[h][:, t, :], inv_tot[:, t:t + 1], None,
                                            ALU.mult).then_inc(probs_ready, 1)

            def pt_part(layer, h):
                dve.wait_ge(pthi_ready, HEADS * layer + h + 1)
                rest_of(pt_lo[:, :, :], bank[6][:, :].rearrange("p (a n) -> p a n", a=2), pt_hi[:, :, :]).then_inc(pt_ready, 1)

            def o_part(layer, h):
                dve.wait_ge(ohi_ready, HEADS * layer + h + 1)
                rest_of(a_lo[:, 2 * h:2 * h + 2, :], bank[7][:, :].rearrange("p (a n) -> p a n", a=2),
                        a_hi[:, 2 * h:2 * h + 2, :]).then_inc(o_ready, 1)

            def attention(layer):
                n0 = first[f"q{layer}"]
                for s in range(24):
                    if s == 0:
                        split(n0 + s + AHEAD)
                        norm(2 if layer == 0 else 6)
                        scaled(HEAD_W ** -0.5)
                    if s < KT:
                        if s == 0:
                            dve.wait_ge(mem_in, 16 * layer + 16)
                        if s >= 2:
                            dve.wait_ge(mem_hi, KT * layer + s - 1)
                        stt(gate[s % 2][:, :], mem[:, s, :], gain(NORM_MEM + layer, s), rms_mem[:, :]).then_inc(mem_val, 1)
                        dve.wait_ge(unit_done, n0 + s + 1)
                        b, use = bank_use(f"q{layer}", s)
                        at_least(dve, a_ready, Q_A[layer] + s - 1)
                        tt(t2[s % 2][:, :], bank[b][:, 0:SEQ], rms_k[:, :]).then_inc(evac[b], 1)
                        if s:
                            split(n0 + s + AHEAD)
                        dve.wait_ge(mem_hi, KT * layer + s + 1)
                        rest_of(mn_lo[:, s, :], gate[s % 2][:, :], mn_hi[:, s, :]).then_inc(mem_lo, 1)
                    elif s < 2 * KT:
                        dve.wait_ge(kv_hi, 16 * layer + s - KT + 1)
                        b = s % 4
                        rest_of(k_lo[:, s - KT, :], bank[b][:, 0:N_MEM], k_hi[:, s - KT, :]).then_inc(evac[b], 1)
                        split(n0 + s + AHEAD)
                    elif s % 2 == 0:
                        split(n0 + s + AHEAD)
                    else:
                        c = (s - 2 * KT) // 2
                        for mt in range(2):
                            dve.wait_ge(kv_hi, 16 * layer + KT + 2 * c + mt + 1)
                            b = 2 * (c % 2) + mt
                            cols = slice(c * 256, c * 256 + 256)
                            rest_of(v_lo[:, mt, cols], bank[b][:, 0:256], v_hi[:, mt, cols]).then_inc(evac[b], 1)
                        split(n0 + s + AHEAD)
                    for h in range(HEADS):
                        if s == 11 + 2 * h:
                            softmax_max(layer, h)
                            softmax_norm(layer, h)
                        if s == 18 + 2 * h:
                            pt_part(layer, h)
                        if s == 19 + 2 * h:
                            o_part(layer, h)
                pt_part(layer, 3)
                o_part(layer, 3)
                project_out(f"o{layer}", 1, 4, False)

            def heads_over(t, g):
                return t[:, g * HPG:g * HPG + HPG].unsqueeze(2).broadcast_to((P, HPG, HD))

            def dt_chain():
                dve.wait_ge(dt_done, 1)
                for c in range(2):
                    step(stt(d["x"][:, c, :], bank[7][:, c * H:c * H + H], rms_n[:, c:c + 1],
                             cst[:, C_DTB:C_DTB + H], op1=ALU.add))
                stt(d["abs"][:, :, :], d["x"][:, :, :], -1.0, d["x"][:, :, :], op1=ALU.max).then_inc(dt_x, 1)
                dve.wait_ge(dt_e, 2)
                nc.vector.tensor_scalar(d["u"][:, :, :], d["e"][:, :, :], 1.0, None, ALU.add).then_inc(dt_u, 1)
                dve.wait_ge(dt_u, 1)
                step(stt(d["c"][:, :, :], d["u"][:, :, :], -1.0, d["e"][:, :, :], op0=ALU.add, op1=ALU.subtract))
                step(nc.vector.reciprocal(d["inv"][:, :, :], d["u"][:, :, :]))
                step(tt(d["c"][:, :, :], d["c"][:, :, :], d["inv"][:, :, :]))
                dve.wait_ge(dt_ln, 1)
                step(tt(d["c"][:, :, :], d["ln"][:, :, :], d["c"][:, :, :], ALU.subtract))
                step(stt(d["sp"][:, :, :], d["x"][:, :, :], 0.0, d["c"][:, :, :], op0=ALU.max, op1=ALU.add))
                for c in range(2):
                    ins = stt(d["da"][:, c, :], d["sp"][:, c, :], -1.0, a_exp[:, :])
                ins.then_inc(da_val, 1)
                dve.wait_ge(dahi_ready, 1)
                rest_of(da_lo[:, :, :], d["da"][:, :, :], da_hi[:, :, :]).then_inc(da_ready, 1)

            def acum_chain():
                dve.wait_ge(acum_done, 1)
                nc.vector.tensor_scalar(d["nacum"][:, :, :], bank[7][:, 64:64 + 2 * H].rearrange("p (c h) -> p c h", c=2),
                                        -1.0, None, ALU.mult).then_inc(acum_ready, 1)
                dve.wait_ge(acum_ready, 1)
                tt(rest[:, :], bank[7][:, 128:128 + H], d["nacum"][:, 0, :], ALU.add).then_inc(acum_ready, 1)

            def ssd():
                nz = first["z"]
                for s in range(16):
                    split(nz + s + AHEAD)
                    if s == 0:
                        norm(NORM_MIX1)
                        nc.vector.tensor_scalar(var_n[:, :], bank[4][:, 256:260].rearrange("p (a b) -> p a b", a=2)[:, :, 0],
                                                1.0 / D_MODEL, EPS, ALU.mult, ALU.add).then_inc(small_var_ready, 1)
                        dve.wait_ge(small_root_ready, 1)
                        inverse_root(rms_n[:, :], var_n[:, :], root_n[:, :], 1)
                    if s == 1:
                        dt_chain()
                    if s == 2:
                        acum_chain()
                    if s == 3:
                        dve.wait_ge(acum_exp, 2)
                        tt(dsd[:, :], dsd[:, :], d["sp"][:, 0, :]).then_inc(dsd_ready, 1)
                        dve.wait_ge(dsd_ready, 1)
                nx = first["xbc"]
                for G in range(GROUPS + 1):
                    g = G - 1
                    for q in range(4):
                        if G < GROUPS:
                            i = 4 * G + q
                            dve.wait_ge(unit_done, nx + i + 1)
                            b, use = bank_use("xbc", i)
                            at_least(dve, conv_ready, i)
                            tt(padded[:, 3:3 + SEQ], bank[b][:, 0:SEQ], rms[:, :]).then_inc(evac[b], 1)
                            split(nx + i + AHEAD)
                            dve.wait_ge(evac[b], use + 1)
                            at_least(dve, xbc_ready, i - 1)
                            o = acc[i % 2]
                            step(nc.vector.tensor_scalar(o[:, :], padded[:, 0:SEQ], col(C_SSDK, 4 * i), col(C_SSDB, i), ALU.mult, ALU.add))
                            for w in range(1, 3):
                                step(stt(o[:, :], padded[:, w:w + SEQ], col(C_SSDK, 4 * i + w), o[:, :], op1=ALU.add))
                            stt(o[:, :], padded[:, 3:3 + SEQ], col(C_SSDK, 4 * i + 3), o[:, :], op1=ALU.add).then_inc(conv_ready, 1)
                            if q == 3:
                                dve.wait_ge(bnhi_ready, G + 1)
                                rest_of(bn_lo[:, :], bank[6][:, 256:384], bn_hi[:, :]).then_inc(bn_ready, 1)
                                dve.wait_ge(decay_ready, 2 * G + 2)
                                at_least(dve, mlo_ready, 2 * G)
                                for c in range(2):
                                    for r in range(HPG):
                                        hd = G * HPG + r
                                        cols = slice(r * P, r * P + P)
                                        ins = stt(m[:, c * 512 + r * P:c * 512 + r * P + P], decay[:, G, c, cols],
                                                  d["sp"][:, c, hd:hd + 1], bank[6][:, c * P:c * P + P])
                                    ins.then_inc(m_ready, 1)
                        if g >= 0:
                            if q == 0:
                                dve.wait_ge(xnhi_ready, G)
                                tt(xs[:, :].rearrange("p (r n) -> p r n", r=HPG),
                                   bank[5][:, 0:GW].rearrange("p (r n) -> p r n", r=HPG), heads_over(dsd, g)).then_inc(xs_ready, 1)
                                for c in range(2):
                                    ins = tt(xd[:, c, :].rearrange("p (r n) -> p r n", r=HPG),
                                             bank[5][:, c * GW:c * GW + GW].rearrange("p (r n) -> p r n", r=HPG),
                                             heads_over(cst[:, C_DSKIP:C_DSKIP + H], g))
                                ins.then_inc(xd_ready, 1)
                                rest_of(xn_lo[:, :, :], bank[5][:, :].rearrange("p (a n) -> p a n", a=2), xn_hi[:, :, :]).then_inc(xn_ready, 1)
                                dve.wait_ge(xshi_ready, G)
                                rest_of(xs_lo[:, :], xs[:, :], xs_hi[:, :]).then_inc(xslo_ready, 1)
                            if q == 1:
                                dve.wait_ge(sthi_ready, G)
                                rest_of(st_lo[:, :], bank[4][:, 0:GW], st_hi[:, :]).then_inc(st_ready, 1)
                                dve.wait_ge(y_done, G)
                                dve.wait_ge(xd_ready, G)
                                step(tt(y[:, :, :], bank[7][:, :].rearrange("p (a n) -> p a n", a=2), xd[:, :, :], ALU.add))
                            if q == 2:
                                dve.wait_ge(yo_done, G)
                                step(tt(y_off[:, :].rearrange("p (r n) -> p r n", r=HPG),
                                        bank[4][:, 256:512].rearrange("p (r n) -> p r n", r=HPG), heads_over(e_acum, g)))
                                step(tt(y[:, 1, :], y[:, 1, :], y_off[:, :], ALU.add))
                                dve.wait_ge(zs_ready, G)
                                tt(y[:, :, :], y[:, :, :], zs[:, :, :]).then_inc(y_ready, 1)
                                dve.wait_ge(ysq_ready, 2 * G)
                                nc.vector.tensor_scalar(var_y[:, :], sum_y[:, :], 1.0 / GW, EPS, ALU.mult, ALU.add).then_inc(small_var_ready, 1)
                                dve.wait_ge(small_root_ready, G + 1)
                                inverse_root(rms_y[:, :], var_y[:, :], root_n[:, :], 1)
                                for c in range(2):
                                    nc.vector.tensor_scalar(y[:, c, :], y[:, c, :], rms_y[:, c:c + 1], None, ALU.mult).then_inc(yn_ready, 1)
                            if q == 3:
                                dve.wait_ge(yhi_ready, 2 * G)
                                for t in range(2):
                                    j = 2 * g + t
                                    stt(a_lo[:, j, :], bank[5][:, t * SEQ:t * SEQ + SEQ], col(C_GATE, j),
                                        a_hi[:, j, :].bitcast(F32), op1=ALU.subtract).then_inc(yt_ready, 1)
                project_out("ssd_out", 2, 4, False)

            nc.vector.memset(ones[:, :], 1.0).then_inc(ones_set, 1)
            step(nc.vector.memset(padded[:, 0:4], 0.0))
            dve.wait_ge(cst_in, 16)
            for k in range(KT):
                new_h(0, k)
            for n in range(AHEAD):
                split(n)
            ffn(0)
            norm("mem", rms_mem)
            conv()
            attention(0)
            ffn(1)
            dve.wait_ge(wdt_hi_ready, 1)
            rest_of(wdt_lo[:, :, :], wdt[:, :, :], wdt_hi[:, :, :]).then_inc(wdt_ready, 1)
            ffn(2)
            step(nc.vector.memset(padded[:, 0:4], 0.0))
            ssd()
            attention(1)
            ffn(3)
            norm(NORM_FINAL)
            for k in range(KT):
                stt(a_out(k), x[:, k, :], gain(NORM_FINAL, k), rms[:, :]).then_inc(out_ready, 1)

        @block.gpsimd
        def _(pool):
            steps = [0]

            def square_sum(src, k):
                if k == 0:
                    nc.gpsimd.tensor_tensor(ssq[:, :], src, src, ALU.mult).then_inc(ssq_step, 1)
                    steps[0] += 1
                    return
                nc.gpsimd.tensor_tensor(sq[:, :], src, src, ALU.mult).then_inc(ssq_step, 1)
                steps[0] += 1
                pool.wait_ge(ssq_step, steps[0])
                nc.gpsimd.tensor_tensor(ssq[:, :], ssq[:, :], sq[:, :], ALU.add).then_inc(ssq_step, 1)
                steps[0] += 1
                pool.wait_ge(ssq_step, steps[0])

            def a_part(j, count, src):
                pool.wait_ge(ahi_ready, count + 1)
                nc.gpsimd.tensor_tensor(j(a_lo), src, j(a_hi).bitcast(F32), ALU.subtract).then_inc(a_ready, 1)

            def ffn(f):
                for j in range(2):
                    a_part(lambda t, j=j: t[:, j, :], FFN_A[f] + j, t2[j][:, :])
                with pool.Fori(1, FT // 2) as i:
                    for q in range(2):
                        a_part(lambda t, q=q: t[:, bass.ds(2 * i + q, 1), :].rearrange("p a n -> p (a n)"),
                               FFN_A[f] + 2 * i + q, t2[q][:, :])
                if f == 0:
                    pool.wait_ge(mem_in, 16)
                    pool.wait_ge(ss_done, 1)
                    for k in range(KT):
                        square_sum(mem[:, k, :], k)
                    pool.wait_ge(ss_done, 2)
                project_out(f"down{f}")

            def project_out(phase):
                for k in range(KT):
                    pool.wait_ge(*x_signal(phase, k))
                    square_sum(x[:, k, :], k)

            def attention(layer):
                for k in range(KT):
                    a_part(lambda t, k=k: t[:, KT + k, :], Q_A[layer] + k, t2[k % 2][:, :])
                project_out(f"o{layer}")

            def ssd():
                for G in range(GROUPS):
                    for half in range(2):
                        pool.wait_ge(bhi_ready, 2 * G + half + 1)
                        if half == 0:
                            at_least(pool, cb_done, 2 * G)
                            nc.gpsimd.tensor_tensor(b_lo[:, :], act_xbc[0][:, :], b_hi[:, :].bitcast(F32), ALU.subtract).then_inc(b_ready, 1)
                        else:
                            at_least(pool, yo_done, G - 1)
                            nc.gpsimd.tensor_tensor(c_lo[:, G % 2, :], act_xbc[1][:, :], c_hi[:, G % 2, :].bitcast(F32),
                                                    ALU.subtract).then_inc(b_ready, 1)
                    for c in range(2):
                        pool.wait_ge(mhi_ready, 2 * G + c + 1)
                        at_least(pool, y_done, G)
                        cols = slice(c * 512, c * 512 + 512)
                        nc.gpsimd.tensor_tensor(m_lo[:, cols], m[:, cols], m_hi[:, cols].bitcast(F32), ALU.subtract).then_inc(mlo_ready, 1)
                project_out("ssd_out")

            pool.wait_ge(x_in, 16)
            for k in range(KT):
                square_sum(x[:, k, :], k)
            ffn(0)
            for k in range(KT):
                a_part(lambda t, k=k: t[:, k, :], CONV_A + k, t2[k % 2][:, :])
            project_out("conv_out")
            attention(0)
            ffn(1)
            ffn(2)
            ssd()
            attention(1)
            ffn(3)

        @block.tensor
        def _(pe):
            def mm(out, lhs, rhs, start, stop, check=False):
                return nc.tensor.matmul(out, lhs, rhs, start=start, stop=stop, skip_group_check=check)

            def three(out, lh, ll, rh, rl, start, stop, check=False):
                mm(out, lh, rh, start, False, check)
                mm(out, lh, rl, False, False, check)
                return mm(out, ll, rh, False, stop, check)

            def unit(n, out, blocks, k0, r_hi, r_lo, start, stop, i=0, ready=None):
                s = n % SLOTS
                pe.wait_ge(lo_ready, n + 1 + SLOTS * i)
                for k in range(blocks):
                    if ready:
                        pe.wait_ge(ready[0], ready[1] + k0 + k + 1)
                    w = slice(k * P, k * P + P)
                    ins = three(out[:, 0:SEQ], w_hi[s][:, w], w_lo[s][:, w], r_hi[:, k0 + k, :], r_lo[:, k0 + k, :],
                                start and k == 0, stop and k == blocks - 1)
                ins.then_inc(unit_done, 1)

            def norm(b):
                pe.wait_ge(ssq_step, ssq_count(b))
                at_least(pe, var_ready, SS_INDEX[b])
                ins = mm(bank[4][:, 0:SEQ], ones[:, :], ssq[:, :], True, True)
                if b == NORM_MIX1:
                    for t in range(2):
                        ins = mm(bank[4][:, 256 + 2 * t:258 + 2 * t], ssq[:, t * P:t * P + P], ones[:, 0:2], True, True)
                ins.then_inc(ss_done, 1)

            def free(phase, t, banks=4, i=0):
                b, use = bank_use(phase, t, banks)
                at_least(pe, evac[b], use + i)
                return bank[b]

            def ffn(f):
                b = {0: 0, 1: 3, 2: 4, 3: 7}[f]
                n0, name = first[f"gu{f}"], f"gu{f}"
                for s in range(4):
                    unit(n0 + s, free(name, s), KT, 0, h_hi, h_lo, True, True, ready=(h_ready, KT * b) if s == 0 else None)
                    if s == 0:
                        norm(b)
                with pe.Fori(1, FT // 2) as i:
                    for s in range(4):
                        unit(n0 + s, free(name, s, i=i), KT, 0, h_hi, h_lo, True, True, i)
                name = f"down{f}"
                n0 = first[name]
                half = FT // 2

                def pair(i, ready):
                    for t in range(2):
                        out = free(name, t, 2, i)
                        for u in range(2):
                            unit(n0 + 2 * t + u, out, half, u * half, a_hi, a_lo, u == 0, u == 1, i, ready if t == 0 else None)

                pair(0, (a_ready, FFN_A[f]))
                if f == 0:
                    norm("mem")
                with pe.Fori(1, KT // 2) as i:
                    pair(i, None)

            def project(name, b, tiles=KT, extra=None):
                for t in range(tiles):
                    unit(first[name] + t, free(name, t), KT, 0, h_hi, h_lo, True, True, ready=(h_ready, KT * b) if t == 0 else None)
                    if t == 0:
                        norm(b)

            def scores(h):
                for t in range(2):
                    for k in range(2):
                        lq = slice(t * P, t * P + P)
                        ins = three(bank[5][:, t * 256:t * 256 + 256], a_hi[:, KT + 2 * h + k, lq], a_lo[:, KT + 2 * h + k, lq],
                                    k_hi[:, 2 * h + k, :], k_lo[:, 2 * h + k, :], k == 0, k == 1)
                ins.then_inc(s_done, 1)

            def turn(layer, h):
                pe.wait_ge(probs_ready, 2 * (HEADS * layer + h) + 2)
                at_least(pe, pt_ready, HEADS * layer + h)
                for mt in range(2):
                    for t in range(2):
                        ins = nc.tensor.transpose(bank[6][:, mt * 256 + t * P:mt * 256 + t * P + P],
                                                  probs[h][:, t, mt * P:mt * P + P], cst[:, C_EYE:C_EYE + P])
                ins.then_inc(pt_done, 1)

            def values(layer, h):
                pe.wait_ge(pt_ready, HEADS * layer + h + 1)
                at_least(pe, o_ready, HEADS * layer + h)
                for t in range(2):
                    cols = slice(h * HEAD_W + t * P, h * HEAD_W + t * P + P)
                    for mt in range(2):
                        ins = three(bank[7][:, t * SEQ:t * SEQ + SEQ], v_hi[:, mt, cols], v_lo[:, mt, cols],
                                    pt_hi[:, mt, :], pt_lo[:, mt, :], mt == 0, mt == 1)
                ins.then_inc(o_done, 1)

            def natural_unit(n, outs, k0, l_hi, l_lo, start, stop):
                s = n % SLOTS
                pe.wait_ge(lo_ready, n + 1)
                for k in range(4):
                    w = slice(k * 256, k * 256 + 256)
                    for t in range(2):
                        lt = slice(t * P, t * P + P)
                        ins = three(outs[t][:, 0:256], l_hi[:, k0 + k, lt], l_lo[:, k0 + k, lt], w_hi[s][:, w], w_lo[s][:, w],
                                    start and k == 0, stop and k == 3)
                ins.then_inc(unit_done, 1)

            def attention(layer):
                n0 = first[f"q{layer}"]
                b = 2 if layer == 0 else 6
                project(f"q{layer}", b)
                for s in range(KT, 24):
                    if s < 2 * KT:
                        t = s - KT
                        unit(n0 + s, free(f"k{layer}", t), KT, 0, mn_hi, mn_lo, True, True,
                             ready=(mem_lo, KT * layer) if t == 0 else None)
                    else:
                        c, u = divmod(s - 2 * KT, 2)
                        if u == 0:
                            outs = [free(f"v{layer}", 2 * c + t) for t in range(2)]
                        natural_unit(n0 + s, outs, 4 * u, mn_hi, mn_lo, u == 0, u == 1)
                    for h in range(HEADS):
                        if s == 10 + 2 * h:
                            pe.wait_ge(a_ready, Q_A[layer] + 2 * h + 2)
                            for t in range(2 * h, 2 * h + 2):
                                kb, use = bank_use(f"k{layer}", t)
                                pe.wait_ge(evac[kb], use + 1)
                            at_least(pe, exp_ready, 2 * (HEADS * layer + h))
                            scores(h)
                        if s == 17 + 2 * h:
                            turn(layer, h)
                        if s == 18 + 2 * h:
                            wait_v(layer, h)
                            values(layer, h)
                wait_v(layer, 3)
                values(layer, 3)
                for t in range(KT):
                    out = free(f"o{layer}", t)
                    s = (first[f"o{layer}"] + t) % SLOTS
                    pe.wait_ge(lo_ready, first[f"o{layer}"] + t + 1)
                    for k in range(KT):
                        if t == 0 and k % 2 == 0:
                            pe.wait_ge(o_ready, HEADS * layer + k // 2 + 1)
                        w = slice(k * P, k * P + P)
                        ins = three(out[:, 0:SEQ], w_hi[s][:, w], w_lo[s][:, w], a_hi[:, k, :], a_lo[:, k, :], k == 0, k == KT - 1)
                    ins.then_inc(unit_done, 1)

            def wait_v(layer, h):
                for mt in range(2):
                    vb, use = bank_use(f"v{layer}", 2 * h + mt)
                    pe.wait_ge(evac[vb], use + 1)

            def decays(l):
                g, c = l // 2, l % 2
                at_least(pe, decay_ready, l - 1)
                out = bank[5 + l % 2]
                mm(out[:, :].rearrange("p (r n) -> p r n", r=HPG), eye_r[:, :], mask_r[:, :].unsqueeze(1).broadcast_to((P, HPG, CHUNK)), True, False, True)
                for r in range(HPG):
                    hd = g * HPG + r
                    for part in (da_hi, da_lo):
                        ins = mm(out[:, r * P:r * P + P], part[:, c, hd:hd + 1].broadcast_to((P, P)), tri_r[:, :],
                                 False, r == HPG - 1 and part is da_lo, True)
                ins.then_inc(l_done, 1)

            def ssd():
                nz = first["z"]
                lcount = 0
                for s in range(16):
                    c, u = divmod(s, 2)
                    if u == 0:
                        outs = [free("z", 2 * c + t) for t in range(2)]
                    if s == 0:
                        for k in range(KT):
                            pe.wait_ge(h_ready, KT * NORM_MIX1 + k + 1)
                    natural_unit(nz + s, outs, 4 * u, h_hi, h_lo, u == 0, u == 1)
                    if s == 0:
                        norm(NORM_MIX1)
                        pe.wait_ge(wdt_ready, 1)
                        for t in range(2):
                            lt = slice(t * P, t * P + P)
                            for k in range(KT):
                                ins = three(bank[7][:, t * H:t * H + H], h_hi[:, k, lt], h_lo[:, k, lt], wdt_hi[:, k, :], wdt_lo[:, k, :],
                                            k == 0, k == KT - 1)
                        ins.then_inc(dt_done, 1)
                    if s == 2:
                        pe.wait_ge(da_ready, 1)
                        for cc in range(2):
                            mm(bank[7][:, 64 + cc * H:64 + cc * H + H], tri_r[:, :], da_hi[:, cc, :], True, False)
                            mm(bank[7][:, 64 + cc * H:64 + cc * H + H], tri_r[:, :], da_lo[:, cc, :], False, True)
                        mm(bank[7][:, 128:128 + H], ones_r[:, :], da_hi[:, 0, :], True, False)
                        mm(bank[7][:, 128:128 + H], ones_r[:, :], da_lo[:, 0, :], False, True).then_inc(acum_done, 1)
                    if s >= 3:
                        while lcount < min(16, (s - 2) * 16 // 12):
                            decays(lcount)
                            lcount += 1
                nx = first["xbc"]
                for G in range(GROUPS + 1):
                    g = G - 1
                    for q in range(4):
                        if G < GROUPS:
                            unit(nx + 4 * G + q, free("xbc", 4 * G + q), KT, 0, h_hi, h_lo, True, True)
                        if G < GROUPS and q == 2:
                            pe.wait_ge(b_ready, 2 * G + 2)
                            at_least(pe, m_ready, 2 * G)
                            at_least(pe, bn_ready, G)
                            if G == 0:
                                pe.wait_ge(decay_ready, 16)
                            for c in range(2):
                                lc = slice(c * P, c * P + P)
                                ins = three(bank[6][:, c * P:c * P + P], b_hi[:, lc], b_lo[:, lc], c_hi[:, G % 2, lc], c_lo[:, G % 2, lc],
                                            True, True)
                            ins.then_inc(cb_done, 1)
                            nc.tensor.transpose(bank[6][:, 256:384], act_xbc[0][:, 0:P], cst[:, C_EYE:C_EYE + P]).then_inc(cb_done, 1)
                        if g >= 0:
                            if q == 0:
                                pe.wait_ge(xbc_ready, 4 * g + 4)
                                at_least(pe, yt_ready, 2 * g)
                                if g == 0:
                                    pe.wait_ge(decay_ready, 16)
                                for c in range(2):
                                    for t in range(2):
                                        ins = nc.tensor.transpose(bank[5][:, c * 256 + t * P:c * 256 + t * P + P],
                                                                  act_xbc[2 + t][:, c * P:c * P + P], cst[:, C_EYE:C_EYE + P])
                                ins.then_inc(xt_done, 1)
                            if q == 1:
                                pe.wait_ge(bn_ready, G)
                                pe.wait_ge(xslo_ready, G)
                                at_least(pe, y_ready, g)
                                pe.wait_ge(small_var_ready, g + 1)
                                three(bank[4][:, 0:GW], bn_hi[:, :], bn_lo[:, :], xs_hi[:, :], xs_lo[:, :], True, True).then_inc(state_done, 1)
                                pe.wait_ge(mlo_ready, 2 * G)
                                pe.wait_ge(xn_ready, G)
                                for c in range(2):
                                    for r in range(HPG):
                                        mc = slice(c * 512 + r * P, c * 512 + r * P + P)
                                        xc = slice(r * HD, r * HD + HD)
                                        ins = three(bank[7][:, c * GW + r * HD:c * GW + r * HD + HD], m_hi[:, mc], m_lo[:, mc],
                                                    xn_hi[:, c, xc], xn_lo[:, c, xc], True, True)
                                ins.then_inc(y_done, 1)
                            if q == 2:
                                pe.wait_ge(st_ready, G)
                                three(bank[4][:, 256:512], c_hi[:, g % 2, P:2 * P], c_lo[:, g % 2, P:2 * P], st_hi[:, :], st_lo[:, :],
                                      True, True).then_inc(yo_done, 1)
                            if q == 3:
                                pe.wait_ge(yn_ready, 2 * G)
                                for t in range(2):
                                    for c in range(2):
                                        ins = nc.tensor.transpose(bank[5][:, t * SEQ + c * P:t * SEQ + c * P + P],
                                                                  y[:, c, t * P:t * P + P], cst[:, C_EYE:C_EYE + P])
                                ins.then_inc(yt_done, 1)
                for t in range(KT):
                    out = free("ssd_out", t)
                    for u in range(2):
                        unit(first["ssd_out"] + 2 * t + u, out, KT, KT * u, a_hi, a_lo, u == 0, u == 1,
                             ready=(yt_ready, 0) if t == 0 else None)

            pe.wait_ge(cst_in, 16)
            pe.wait_ge(ones_set, 1)
            ffn(0)
            pe.wait_ge(consts, 4)
            project_conv = first["conv_in"]
            project("conv_in", NORM_MIX0, 3 * KT)
            for t in range(KT):
                unit(first["conv_out"] + t, free("conv_out", t), KT, 0, a_hi, a_lo, True, True,
                     ready=(a_ready, CONV_A) if t == 0 else None)
            attention(0)
            ffn(1)
            ffn(2)
            ssd()
            attention(1)
            ffn(3)
            norm(NORM_FINAL)


def _units(w):
    k, m = w.shape
    return w.reshape(k // P, P, m // P, P).transpose(2, 1, 0, 3).reshape(m // P, P, k)


def _halves(w, parts):
    u = _units(w)
    m, _, k = u.shape
    return u.reshape(m, P, parts, k // parts).transpose(0, 2, 1, 3).reshape(m * parts, P, k // parts)


def _natural(w):
    k, m = w.shape
    return w.reshape(2, 4, P, m // 256, 256).transpose(3, 0, 2, 1, 4).reshape(m // 128, P, 1024)


def _tiles(v):
    return v.reshape(-1, P).T


def _rows(v):
    return np.broadcast_to(v.reshape(1, -1), (P, v.size))


def kernel(**inputs):
    import concourse.bacc as bacc
    from concourse.bass_utils import run_bass_kernel_spmd

    t = {k: np.asarray(v) for k, v in inputs.items()}
    gu = t["ffn_w_gate_up"].reshape(4, D_MODEL, 2, FT, P).transpose(0, 1, 3, 2, 4).reshape(4, D_MODEL, 2 * D_FF)
    conv_in = t["conv_w_in"][0].reshape(D_MODEL, 3, KT, P)[:, [1, 2, 0]].transpose(0, 2, 1, 3).reshape(D_MODEL, 3 * D_MODEL)
    ssd_in = t["ssd_w_in"][0]
    xbc = ssd_in[:, D_INNER:D_INNER + 4096].reshape(D_MODEL, 32, P)
    order = [i for g in range(GROUPS) for i in (16 + g, 24 + g, 2 * g, 2 * g + 1)]
    ones = np.ones((P, P), np.float32)
    upper = np.triu(ones)
    gains = [t["ffn_norm"][0, 0], t["mix_norm"][0], t["xa_norm"][0], t["ffn_norm"][0, 1], t["ffn_norm"][1, 0],
             t["mix_norm"][1], t["xa_norm"][1], t["ffn_norm"][1, 1], t["final_norm"], t["xa_mem_norm"][0], t["xa_mem_norm"][1]]
    small = np.concatenate([
        *[_tiles(g) for g in gains],
        t["conv_kernel"][0].reshape(3, KT, P).transpose(2, 1, 0).reshape(P, KT * 3),
        t["ssd_conv_kernel"][0].reshape(4, 32, P)[:, order].transpose(2, 1, 0).reshape(P, 128),
        t["ssd_conv_bias"][0].reshape(32, P)[order].T,
        _tiles(t["ssd_gate_norm"][0]),
        _rows(t["ssd_dt_bias"][0]), _rows(t["ssd_a_log"][0]), _rows(t["ssd_d_skip"][0]),
        np.eye(P, dtype=np.float32), upper, np.tril(np.full((P, P), MASKED, np.float32), -1)], axis=1)
    arrays = {
        "x_t": t["x"][0].T.reshape(KT, P, SEQ).transpose(1, 0, 2),
        "mem_t": t["mem"][0].T.reshape(KT, P, N_MEM).transpose(1, 0, 2),
        "small": small,
        "w_gu": np.stack([_units(w) for w in gu]),
        "w_down": np.stack([_halves(w, 2) for w in t["ffn_w_down"].reshape(4, D_FF, D_MODEL)]),
        "w_conv_in": _units(conv_in),
        "w_conv_out": _units(t["conv_w_out"][0]),
        "w_z": _natural(ssd_in[:, :D_INNER]),
        "w_xbc": _units(xbc[:, order].reshape(D_MODEL, 4096)),
        "w_dt": ssd_in[:, D_INNER + 4096:].reshape(KT, P, SSD_HEADS).transpose(1, 0, 2),
        "w_ssd_out": _halves(t["ssd_w_out"][0], 2),
        "w_q": np.stack([_units(w) for w in t["xa_w_q"]]),
        "w_k": np.stack([_units(w[:, :D_MODEL]) for w in t["xa_w_kv"]]),
        "w_v": np.stack([_natural(w[:, D_MODEL:]) for w in t["xa_w_kv"]]),
        "w_o": np.stack([_units(w) for w in t["xa_w_o"]]),
    }
    arrays = {k: np.ascontiguousarray(v) for k, v in arrays.items()}
    nc = bacc.Bacc("TRN2", target_bir_lowering=False, num_devices=1, dynamic_dma_scratch_size=1024)
    args = [nc.dram_tensor(k, v.shape, F32, kind="ExternalInput").ap() for k, v in arrays.items()]
    out = nc.dram_tensor("out_t", (P, KT, SEQ), F32, kind="ExternalOutput").ap()
    trunk(nc, *args, out)
    got = run_bass_kernel_spmd(nc, [arrays], core_ids=[0]).results[0]["out_t"]
    return np.asarray(got).transpose(2, 1, 0).reshape(1, SEQ, D_MODEL)
```

```python
from contextlib import ExitStack

import numpy as np

import concourse.bass as bass
from concourse import mybir

F32 = mybir.dt.float32
F32R = mybir.dt.float32r
ALU = mybir.AluOpType
ACT = mybir.ActivationFunctionType
AX = mybir.AxisListType

P = 128
SEQ = 256
D_MODEL = 1024
KT = D_MODEL // P
D_FF = 2816
FT = D_FF // P
N_MEM = 256
HEADS = 4
HEAD_W = D_MODEL // HEADS
GROUPS = 8
HPG = 4
HD = 64
SSD_HEADS = GROUPS * HPG
CHUNK = 128
D_INNER = SSD_HEADS * HD
IT = D_INNER // P
GW = D_INNER // GROUPS
EPS = 1e-6
MASKED = -1e30

UNIT_W = KT * P
DOWN_W = FT // 2 * P
SLOTS = 4
AHEAD = 3

N_NORMS = 11
C_GAIN = 0
C_CONVK = C_GAIN + N_NORMS * KT
C_SSDK = C_CONVK + KT * 3
C_SSDB = C_SSDK + 32 * 4
C_GATE = C_SSDB + 32
C_DTB = C_GATE + IT
C_ALOG = C_DTB + SSD_HEADS
C_DSKIP = C_ALOG + SSD_HEADS
C_EYE = C_DSKIP + SSD_HEADS
C_TRI = C_EYE + P
C_MASK = C_TRI + P
C_ALL = C_MASK + P
NORM_MIX0, NORM_XA0, NORM_MIX1, NORM_XA1, NORM_FINAL, NORM_MEM = 1, 2, 5, 6, 8, 9

PHASES = [
    ("gu0", 44, UNIT_W), ("down0", 16, DOWN_W), ("conv_in", 24, UNIT_W), ("conv_out", 8, UNIT_W),
    ("q0", 8, UNIT_W), ("k0", 8, UNIT_W), ("v0", 8, UNIT_W), ("o0", 8, UNIT_W),
    ("gu1", 44, UNIT_W), ("down1", 16, DOWN_W), ("gu2", 44, UNIT_W), ("down2", 16, DOWN_W),
    ("z", 16, UNIT_W), ("xbc", 32, UNIT_W), ("ssd_out", 16, UNIT_W),
    ("q1", 8, UNIT_W), ("k1", 8, UNIT_W), ("v1", 8, UNIT_W), ("o1", 8, UNIT_W),
    ("gu3", 44, UNIT_W), ("down3", 16, DOWN_W),
]
LAST_NORM = 8


def plan():
    first, uses, n, used = {}, {}, 0, [0] * 4
    for name, units, _ in PHASES:
        first[name], uses[name] = n, list(used)
        n += units
        tiles = units // 2 if name[:4] == "down" or name == "ssd_out" else units
        banks = 2 if name[:4] == "down" else 4
        for b in range(banks):
            used[b] += tiles // banks
    return first, uses, n


def trunk(nc, x_t, mem_t, small, w_gu, w_down, w_conv_in, w_conv_out, w_z, w_xbc, w_dt, w_ssd_out,
          w_q, w_k, w_v, w_o, out_t):
    first, uses, n_units = plan()
    width = []
    for _, units, w in PHASES:
        width += [w] * units

    with ExitStack() as ctx:
        def sb(name, shape, dt=F32):
            return ctx.enter_context(nc.sbuf_tensor(name, shape, dt))

        def sem(name):
            return ctx.enter_context(nc.semaphore(name))

        x = sb("x", [P, KT, SEQ])
        h_hi, h_lo = sb("h_hi", [P, KT, SEQ], F32R), sb("h_lo", [P, KT, SEQ], F32R)
        a_hi, a_lo = sb("a_hi", [P, FT, SEQ], F32R), sb("a_lo", [P, FT, SEQ], F32R)
        raw = sb("raw", [P, SLOTS, DOWN_W])
        w_hi = [sb(f"w_hi{s}", [P, DOWN_W], F32R) for s in range(SLOTS)]
        w_lo = [sb(f"w_lo{s}", [P, DOWN_W], F32R) for s in range(SLOTS)]
        mark = nc.sbuf_base
        mn_hi, mn_lo = sb("mn_hi", [P, KT, N_MEM], F32R), sb("mn_lo", [P, KT, N_MEM], F32R)
        z = nc.alloc_sbuf_tensor_at("z", [P, 2, D_INNER], F32, offset=mark + (-mark) % 32)
        mark = nc.sbuf_base
        k_hi, k_lo = sb("k_hi", [P, KT, N_MEM], F32R), sb("k_lo", [P, KT, N_MEM], F32R)
        v_hi, v_lo = sb("v_hi", [P, 2, D_MODEL], F32R), sb("v_lo", [P, 2, D_MODEL], F32R)
        decay = nc.alloc_sbuf_tensor_at("decay", [P, GROUPS, 2, HPG * CHUNK], F32, offset=mark + (-mark) % 32)
        mark = nc.sbuf_base
        mem = sb("mem", [P, KT, N_MEM])
        at = [mark + (-mark) % 32]

        def over(name, shape, dt=F32):
            t = nc.alloc_sbuf_tensor_at(name, shape, dt, offset=at[0])
            at[0] += 4 * int(np.prod(shape[1:]))
            return t

        probs_all = nc.alloc_sbuf_tensor_at("probs", [P, HEADS, 2, N_MEM], F32, offset=at[0])
        probs = [probs_all[:, h] for h in range(HEADS)]
        m = over("m", [P, 2 * HPG * CHUNK])
        wdt = over("wdt", [P, KT, SSD_HEADS])
        wdt_hi, wdt_lo = over("wdt_hi", [P, KT, SSD_HEADS], F32R), over("wdt_lo", [P, KT, SSD_HEADS], F32R)
        assert at[0] <= nc.sbuf_base
        cst = sb("cst", [P, C_ALL])
        ones = sb("ones", [P, P])
        ones_r, eye_r, tri_r, mask_r = (sb(n, [P, P], F32R) for n in ("ones_r", "eye_r", "tri_r", "mask_r"))
        ssq, sq = sb("ssq", [P, SEQ]), sb("sq", [P, SEQ])
        root, var, rms, rms_k, rms_mem = sb("root", [P, SEQ]), sb("var", [P, SEQ]), sb("rms", [P, SEQ]), sb("rms_k", [P, SEQ]), sb("rms_mem", [P, SEQ])
        t1_all, t2_all, gate_all = (sb(n, [P, 2, SEQ]) for n in ("t1", "t2", "gate"))
        t1, t2, gate = ([t[:, i] for i in range(2)] for t in (t1_all, t2_all, gate_all))
        padded = sb("padded", [P, 4 + SEQ])
        acc = [sb(f"acc{i}", [P, SEQ]) for i in range(2)]
        pt_hi, pt_lo = a_hi[:, 16:18, :], a_lo[:, 16:18, :]
        m_hi, m_lo = (a[:, 16:20, :].rearrange("p a n -> p (a n)") for a in (a_hi, a_lo))
        c_hi, c_lo = a_hi[:, 20:22, :], a_lo[:, 20:22, :]
        mx, neg_mx, tot, inv_tot = (sb(n, [P, 2]) for n in ("mx", "neg_mx", "tot", "inv_tot"))
        act_xbc = [raw[:, s, UNIT_W:UNIT_W + SEQ] for s in range(4)]
        b_hi, b_lo = (w[0][:, UNIT_W:UNIT_W + SEQ] for w in (w_hi, w_lo))
        bn_hi, bn_lo = (w[0][:, UNIT_W + SEQ:DOWN_W] for w in (w_hi, w_lo))
        xs_hi, xs_lo = (w[1][:, UNIT_W:UNIT_W + GW] for w in (w_hi, w_lo))
        st_hi, st_lo = (w[2][:, UNIT_W:UNIT_W + GW] for w in (w_hi, w_lo))
        xn_hi, xn_lo = sb("xn_hi", [P, 2, GW], F32R), sb("xn_lo", [P, 2, GW], F32R)
        xd = sb("xd", [P, 2, GW])
        normed = [t[:, i] for t in (t1_all, t2_all, gate_all, xd) for i in range(2)]
        y_off, xs = t1
        y = [t2_all, sb("y1", [P, 2, GW])]
        sq_y, zs = sq, gate_all
        var_y, rms_y = sb("var_y", [P, 2]), sb("rms_y", [P, 2])
        rms_n, var_n, root_n, sum_y = (sb(n, [P, 2]) for n in ("rms_n", "var_n", "root_n", "sum_y"))
        H = SSD_HEADS
        d = {n: sb("dt_" + n, [P, 2, H]) for n in ("sp", "nacum")}
        for i, n in enumerate(("x", "abs", "e", "u", "ln", "c", "inv", "da")):
            c0 = UNIT_W + SEQ + i % 2 * 2 * H
            d[n] = raw[:, i // 2, c0:c0 + 2 * H].rearrange("p (c h) -> p c h", c=2)
        da_hi, da_lo = sb("da_hi", [P, 2, H], F32R), sb("da_lo", [P, 2, H], F32R)
        a_exp, e_acum, dsd, rest = (sb(n, [P, H]) for n in ("a_exp", "e_acum", "dsd", "rest"))

        bank = [ctx.enter_context(nc.psum_tensor(f"bank{i}", [P, 512], F32)) for i in range(8)]

        x_in, mem_in, cst_in, dt_in = sem("x_in"), sem("mem_in"), sem("cst_in"), sem("dt_in")
        landed = [sem(f"landed{s}") for s in range(SLOTS)]
        hi_ready, lo_ready = sem("hi_ready"), sem("lo_ready")
        unit_done = sem("unit_done")
        evac = [sem(f"evac{b}") for b in range(4)]
        silu_ready = sem("silu_ready")
        ahi_ready, a_ready = sem("ahi_ready"), sem("a_ready")
        x_ready = sem("x_ready")
        hhi_ready, h_ready = sem("hhi_ready"), sem("h_ready")
        ssq_step, ss_done = sem("ssq_step"), sem("ss_done")
        consts = sem("consts")
        var_ready, root_ready = sem("var_ready"), sem("root_ready")
        small_var_ready, small_root_ready = sem("small_var_ready"), sem("small_root_ready")
        ones_set, pads_set = sem("ones_set"), sem("pads_set")
        dve_step, act_step, pool_step = sem("dve_step"), sem("act_step"), sem("pool_step")
        mem_val, mem_hi, mem_lo = sem("mem_val"), sem("mem_hi"), sem("mem_lo")
        kv_hi = sem("kv_hi")
        s_done, max_ready, exp_ready, probs_ready = sem("s_done"), sem("max_ready"), sem("exp_ready"), sem("probs_ready")
        pt_done, pthi_ready, pt_ready = sem("pt_done"), sem("pthi_ready"), sem("pt_ready")
        o_done, ohi_ready, o_ready = sem("o_done"), sem("ohi_ready"), sem("o_ready")
        dt_done, dt_x, dt_e, dt_u, dt_ln, dt_a = (sem(n) for n in ("dt_done", "dt_x", "dt_e", "dt_u", "dt_ln", "dt_a"))
        wdt_hi_ready, wdt_ready = sem("wdt_hi_ready"), sem("wdt_ready")
        da_val, dahi_ready, da_ready = sem("da_val"), sem("dahi_ready"), sem("da_ready")
        acum_done, acum_ready, acum_exp, dsd_ready = sem("acum_done"), sem("acum_ready"), sem("acum_exp"), sem("dsd_ready")
        l_done, decay_ready = sem("l_done"), sem("decay_ready")
        normed_ready, conv_begun, xbc_ready, y_added = (sem(n) for n in ("normed_ready", "conv_begun", "xbc_ready", "y_added"))
        bhi_ready, b_ready = sem("bhi_ready"), sem("b_ready")
        cb_done, bnhi_ready, bn_ready = sem("cb_done"), sem("bnhi_ready"), sem("bn_ready")
        m_ready, mhi_ready, mlo_ready = sem("m_ready"), sem("mhi_ready"), sem("mlo_ready")
        xt_done, xnhi_ready, xn_ready, xd_ready = sem("xt_done"), sem("xnhi_ready"), sem("xn_ready"), sem("xd_ready")
        xs_ready, xshi_ready, xslo_ready = sem("xs_ready"), sem("xshi_ready"), sem("xslo_ready")
        state_done, sthi_ready, st_ready = sem("state_done"), sem("sthi_ready"), sem("st_ready")
        yoff_ready, ysum_ready = sem("yoff_ready"), sem("ysum_ready")
        y_done, yo_done, zs_ready, y_ready, ysq_ready, yn_ready = (
            sem(n) for n in ("y_done", "yo_done", "zs_ready", "y_ready", "ysq_ready", "yn_ready"))
        yt_done, yhi_ready, yt_ready = sem("yt_done"), sem("yhi_ready"), sem("yt_ready")
        out_ready, out_landed = sem("out_ready"), sem("out_landed")

        def at_least(eng, s, value):
            if isinstance(value, int) and value <= 0:
                return
            eng.wait_ge(s, value)

        def gain(b, k):
            return cst[:, C_GAIN + b * KT + k:C_GAIN + b * KT + k + 1]

        def col(c0, i):
            return cst[:, c0 + i:c0 + i + 1]

        def bank_use(phase, t, banks=4):
            return t % banks, uses[phase][t % banks] + t // banks

        FFN_A = {0: 0, 1: FT + KT + KT, 2: 2 * FT + 2 * KT, 3: 3 * FT + 3 * KT}
        CONV_A, Q_A = FT, {0: FT + KT, 1: 3 * FT + 2 * KT}
        X_COUNT = {"down0": 0, "conv_out": KT, "down1": 2 * KT, "down2": 3 * KT, "down3": 4 * KT}
        OUT_NORM = {"down0": 1, "conv_out": 2, "o0": 3, "down1": 4, "down2": 5, "ssd_out": 6, "o1": 7, "down3": 8}
        SS_INDEX = {0: 0, "mem": 1, 1: 2, 2: 3, 3: 4, 4: 5, 5: 6, 6: 7, 7: 8, 8: 9}

        def ssq_count(b):
            return (SS_INDEX[b] + 1) * (2 * KT - 1)

        def x_signal(phase, k):
            if phase in X_COUNT:
                return x_ready, X_COUNT[phase] + k + 1
            b, use = bank_use(phase, k)
            return evac[b], use + 1

        def a_out(k):
            return mem[:, k, :]

        H_FIRST = [KT * (b + (b > NORM_MIX1)) for b in range(LAST_NORM)]
        H_EXTRA = KT * (NORM_MIX1 + 1)
        SSD_STEPS = 4 * (GROUPS + 3) + 1

        def ssd_out_unit(k):
            return first["ssd_out"] + (4 + k if k < 4 else 1 + 2 * k)

        def ssd_out_splits(k):
            n = ssd_out_unit(k) + AHEAD
            return [n] if k < 4 else [n - 1, n]

        block = ctx.enter_context(nc.Block())

        @block.sync
        def _(sp):
            sp.dma_start(cst[:, :], small).then_inc(cst_in, 16)
            sp.dma_start(x[:, :, :], x_t).then_inc(x_in, 16)

            def load(n, src, i=0):
                at_least(sp, lo_ready, n - SLOTS + 1 + SLOTS * i)
                sp.dma_start(raw[:, n % SLOTS, 0:width[n]], src).then_inc(landed[n % SLOTS], 16)

            def load_phase(name, w, units):
                n0 = first[name]
                for s in range(SLOTS):
                    load(n0 + s, w[s])
                if name == "gu0":
                    sp.dma_start(mem[:, :, :], mem_t).then_inc(mem_in, 16)
                if units == 2 * SLOTS:
                    for s in range(SLOTS, units):
                        load(n0 + s, w[s])
                else:
                    with sp.Fori(1, units // SLOTS) as i:
                        for s in range(SLOTS):
                            load(n0 + s, w[bass.ds(i * SLOTS + s, 1)].rearrange("a p n -> p (a n)"), i)

            sources = {"gu": w_gu, "down": w_down, "q": w_q, "k": w_k, "v": w_v, "o": w_o}
            whole = {"conv_in": w_conv_in, "conv_out": w_conv_out, "z": w_z, "xbc": w_xbc, "ssd_out": w_ssd_out}
            for name, units, _ in PHASES:
                if name in whole:
                    load_phase(name, whole[name], units)
                else:
                    load_phase(name, sources[name[:-1]][int(name[-1])], units)
                if name == "ssd_out":
                    sp.dma_start(mem[:, :, :], mem_t).then_inc(mem_in, 16)
                if name == "down1":
                    sp.dma_start(wdt[:, :, :], w_dt).then_inc(dt_in, 16)
            for k in range(KT):
                sp.wait_ge(out_ready, k + 1)
                sp.dma_start(out_t[:, k, :], a_out(k)).then_inc(out_landed, 16)
            sp.wait_ge(out_landed, 16 * KT)

        @block.scalar
        def _(act):
            def copy(out, in_, scale=1.0):
                return nc.scalar.activation(out, in_, ACT.Copy, scale=scale)

            def split(n, i=0):
                if n >= n_units:
                    return
                s = n % SLOTS
                act.wait_ge(landed[s], 16 * (n // SLOTS + 1) + 16 * i)
                at_least(act, unit_done, n - SLOTS + 1 + SLOTS * i)
                copy(w_hi[s][:, 0:width[n]], raw[:, s, 0:width[n]]).then_inc(hi_ready, 1)

            def norm(b):
                act.wait_ge(var_ready, SS_INDEX[b] + 1)
                nc.scalar.activation(root[:, :], var[:, :], ACT.Sqrt).then_inc(root_ready, 1)

            def new_h(b, k):
                copy(h_hi[:, k, :], x[:, k, :], gain(b, k)).then_inc(hhi_ready, 1)

            def a_part(j, count, src, signal, i=None):
                act.wait_ge(*signal)
                copy(a_hi[:, j, :], src).then_inc(ahi_ready, 1)

            def ffn_unit(f, n, s, i, j_of, opening=False):
                split(n + AHEAD, i)
                q, up = s // 2, s % 2
                if opening:
                    norm({0: 0, 1: 3, 2: 4, 3: 7}[f])
                b, use = bank_use(f"gu{f}", n - first[f"gu{f}"])
                act.wait_ge(evac[b], use + 1 + i)
                if not up:
                    b_up, use_up = bank_use(f"gu{f}", n + 1 - first[f"gu{f}"])
                    at_least(act, evac[b_up], use_up + i)
                    nc.scalar.activation(gate[q][:, :], t1[q][:, :], ACT.Silu).then_inc(silu_ready, 1)
                else:
                    copy(j_of(a_hi), t2[q][:, :]).then_inc(ahi_ready, 1)

            def ffn(f):
                n0 = first[f"gu{f}"]
                turns = FT // 2
                for s in range(4):
                    ffn_unit(f, n0 + s, s, 0, lambda t, s=s: t[:, s // 2, :], opening=s == 0)
                with act.Fori(1, turns - 1) as i:
                    for s in range(4):
                        ffn_unit(f, n0 + s, s, i, lambda t, s=s: t[:, bass.ds(2 * i + s // 2, 1), :].rearrange("p a n -> p (a n)"))
                for s in range(4):
                    n = n0 + 4 * (turns - 1) + s
                    ffn_unit(f, n, s, 0, lambda t, s=s: t[:, 2 * (turns - 1) + s // 2, :])
                project_out(f"down{f}", 2)

            def project_out(phase, per_tile):
                n0 = first[phase]
                for k in range(KT):
                    for u in range(per_tile):
                        split(n0 + per_tile * k + u + AHEAD)
                    b = OUT_NORM[phase]
                    if b <= 7:
                        act.wait_ge(*x_signal(phase, k))
                        new_h(b, k)

            def conv():
                n0 = first["conv_in"]
                for t in range(3 * KT):
                    split(n0 + t + AHEAD)
                    if t == 0:
                        norm(NORM_MIX0)
                    if t % 3 == 2:
                        b, use = bank_use("conv_in", t)
                        act.wait_ge(evac[b], use + 1)
                        copy(a_hi[:, t // 3, :], t2[t // 3 % 2][:, :]).then_inc(ahi_ready, 1)
                project_out("conv_out", 1)

            def attention(layer):
                n0 = first[f"q{layer}"]
                for s in range(24):
                    split(n0 + s + AHEAD)
                    if s == 0:
                        norm(2 if layer == 0 else 6)
                    if s < KT:
                        act.wait_ge(mem_val, KT * layer + s + 1)
                        copy(mn_hi[:, s, :], gate[s % 2][:, :]).then_inc(mem_hi, 1)
                        b, use = bank_use(f"q{layer}", s)
                        act.wait_ge(evac[b], use + 1)
                        copy(a_hi[:, KT + s, :], t2[s % 2][:, :]).then_inc(ahi_ready, 1)
                    elif s < 2 * KT:
                        act.wait_ge(unit_done, n0 + s + 1)
                        copy(k_hi[:, s - KT, :], bank[s % 4][:, 0:N_MEM]).then_inc(kv_hi, 1)
                    elif s % 2:
                        act.wait_ge(unit_done, n0 + s + 1)
                        c = (s - 2 * KT) // 2
                        for mt in range(2):
                            copy(v_hi[:, mt, c * 256:c * 256 + 256], bank[2 * (c % 2) + mt][:, 0:256]).then_inc(kv_hi, 1)
                    for h in range(HEADS):
                        if s == 11 + 2 * h:
                            act.wait_ge(max_ready, HEADS * layer + h + 1)
                            for tt in range(2):
                                nc.scalar.activation(probs[h][:, tt, :], bank[5][:, tt * 256:tt * 256 + 256], ACT.Exp,
                                                     bias=neg_mx[:, tt:tt + 1], accum_out=tot[:, tt:tt + 1]).then_inc(exp_ready, 1)
                        if s == 18 + 2 * h:
                            pt_part(layer, h)
                        if s == 19 + 2 * h:
                            o_part(layer, h)
                pt_part(layer, 3)
                o_part(layer, 3)
                project_out(f"o{layer}", 1)

            def pt_part(layer, h):
                act.wait_ge(pt_done, HEADS * layer + h + 1)
                at_least(act, o_done, HEADS * layer + h)
                copy(pt_hi[:, :, :], bank[6][:, 0:512].rearrange("p (a n) -> p a n", a=2)).then_inc(pthi_ready, 1)

            def o_part(layer, h):
                act.wait_ge(o_done, HEADS * layer + h + 1)
                copy(a_hi[:, 2 * h:2 * h + 2, :], bank[7][:, 0:512].rearrange("p (a n) -> p a n", a=2)).then_inc(ohi_ready, 1)

            def decays(l):
                g, c = l // 2, l % 2
                act.wait_ge(l_done, l + 1)
                for r in range(HPG):
                    hd = g * HPG + r
                    ins = nc.scalar.activation(decay[:, g, c, r * P:r * P + P], bank[5 + l % 2][:, r * P:r * P + P],
                                               ACT.Exp, bias=d["nacum"][:, c, hd:hd + 1])
                ins.then_inc(decay_ready, 1)

            def ssd():
                nz = first["z"]
                lcount = 0
                for s in range(16):
                    split(nz + s + AHEAD)
                    if s == 0:
                        norm(NORM_MIX1)
                        act.wait_ge(small_var_ready, 1)
                        nc.scalar.activation(root_n[:, :], var_n[:, :], ACT.Sqrt).then_inc(small_root_ready, 1)
                    if s == 1:
                        act.wait_ge(dt_x, 1)
                        nc.scalar.activation(d["e"][:, :, :], d["abs"][:, :, :], ACT.Exp, scale=-1.0).then_inc(dt_e, 1)
                        nc.scalar.activation(a_exp[:, :], cst[:, C_ALOG:C_ALOG + H], ACT.Exp).then_inc(dt_e, 1)
                        act.wait_ge(dt_u, 1)
                        nc.scalar.activation(d["ln"][:, :, :], d["u"][:, :, :], ACT.Ln).then_inc(dt_ln, 1)
                        act.wait_ge(da_val, 1)
                        copy(da_hi[:, :, :], d["da"][:, :, :]).then_inc(dahi_ready, 1)
                    if s % 2:
                        act.wait_ge(unit_done, nz + s + 1)
                        g = s // 2
                        for tt in range(2):
                            b = 2 * (g % 2) + tt
                            copy(z[:, tt, g * GW:g * GW + GW], bank[b][:, 0:GW], rms_n[:, tt:tt + 1]).then_inc(evac[b], 1)
                    if s == 2:
                        act.wait_ge(acum_ready, 2)
                        nc.scalar.activation(e_acum[:, :], d["nacum"][:, 1, :], ACT.Exp, scale=-1.0).then_inc(acum_exp, 1)
                        nc.scalar.activation(dsd[:, :], rest[:, :], ACT.Exp).then_inc(acum_exp, 1)
                    if s >= 3:
                        while lcount < min(16, (s - 2) * 16 // 12):
                            decays(lcount)
                            lcount += 1
                act.wait_ge(unit_done, nz + 16)
                for k in range(KT):
                    act.wait_ge(normed_ready, k + 1)
                    copy(h_hi[:, k, :], normed[k]).then_inc(hhi_ready, 1)
                nx = first["xbc"]
                for t in range(SSD_STEPS):
                    G, q = divmod(t, 4)
                    if t < 36:
                        split(nx + t + AHEAD)
                    if G < GROUPS:
                        act.wait_ge(unit_done, nx + t + 1)
                        at_least(act, xbc_ready, t - 1)
                        nc.scalar.activation(acc[t % 2][:, :], bank[q][:, 0:SEQ], ACT.Identity, bias=col(C_SSDB, t),
                                             scale=col(C_SSDK, 4 * t + 3)).then_inc(conv_begun, 1)
                    if 0 < t <= 4 * GROUPS:
                        silu_xbc(*divmod(t - 1, 4))
                    g = G - 1
                    if 0 <= g < GROUPS:
                        if q == 0:
                            act.wait_ge(cb_done, 2 * g + 2)
                            at_least(act, state_done, g)
                            copy(bn_hi, bank[6][:, 256:384]).then_inc(bnhi_ready, 1)
                        if q == 1:
                            at_least(act, y_done, g)
                            for c in range(2):
                                act.wait_ge(m_ready, 2 * g + c + 1)
                                copy(m_hi[:, c * 512:c * 512 + 512], m[:, c * 512:c * 512 + 512]).then_inc(mhi_ready, 1)
                        if q == 2:
                            act.wait_ge(xt_done, g + 1)
                            copy(xn_hi[:, :, :], bank[5][:, :].rearrange("p (a n) -> p a n", a=2)).then_inc(xnhi_ready, 1)
                        if q == 3:
                            act.wait_ge(xs_ready, g + 1)
                            copy(xs_hi, xs).then_inc(xshi_ready, 1)
                    g = G - 2
                    if 0 <= g < GROUPS:
                        if q == 0:
                            at_least(act, y_ready, g)
                            nc.scalar.activation(zs[:, :, :], z[:, :, g * GW:g * GW + GW], ACT.Silu).then_inc(zs_ready, 1)
                        if q == 1:
                            act.wait_ge(state_done, g + 1)
                            at_least(act, yo_done, g)
                            copy(st_hi, bank[4][:, 0:GW]).then_inc(sthi_ready, 1)
                    g = G - 3
                    if 0 <= g < GROUPS:
                        if q == 0:
                            act.wait_ge(y_ready, g + 1)
                            for c in range(2):
                                if g or c:
                                    act.wait_ge(ysq_ready, 2 * g + c)
                                nc.scalar.activation(sq_y[:, :], y[g % 2][:, c, :], ACT.Square,
                                                     accum_out=sum_y[:, c:c + 1]).then_inc(ysq_ready, 1)
                        if q == 1:
                            act.wait_ge(small_var_ready, g + 2)
                            nc.scalar.activation(root_n[:, :], var_y[:, :], ACT.Sqrt).then_inc(small_root_ready, 1)
                    g = G - 4
                    if 0 <= g < GROUPS and q == 0:
                        act.wait_ge(yt_done, g + 1)
                        for u in range(2):
                            j = 2 * g + u
                            copy(a_hi[:, j, :], bank[5][:, u * SEQ:u * SEQ + SEQ], col(C_GATE, j)).then_inc(yhi_ready, 1)
                for k in range(KT):
                    for n in ssd_out_splits(k):
                        split(n)
                    act.wait_ge(*x_signal("ssd_out", k))
                    new_h(OUT_NORM["ssd_out"], k)

            def silu_xbc(G, q):
                b, use = bank_use("xbc", q)
                act.wait_ge(evac[b], use + G + 1)
                if q < 2:
                    at_least(act, b_ready, 2 * G)
                    at_least(act, cb_done, 2 * G)
                else:
                    at_least(act, xt_done, G)
                nc.scalar.activation(act_xbc[q], acc[q % 2][:, :], ACT.Silu).then_inc(xbc_ready, 1)
                if q < 2:
                    act.wait_ge(xbc_ready, 4 * G + q + 1)
                if q == 0:
                    copy(b_hi, act_xbc[0]).then_inc(bhi_ready, 1)
                if q == 1:
                    at_least(act, yo_done, G - 1)
                    copy(c_hi[:, G % 2, :], act_xbc[1]).then_inc(bhi_ready, 1)

            act.wait_ge(cst_in, 16)
            act.wait_ge(x_in, 16)
            for k in range(KT):
                new_h(0, k)
            for n in range(AHEAD):
                split(n)
            copy(eye_r[:, :], cst[:, C_EYE:C_EYE + P]).then_inc(consts, 1)
            copy(tri_r[:, :], cst[:, C_TRI:C_TRI + P]).then_inc(consts, 1)
            copy(mask_r[:, :], cst[:, C_MASK:C_MASK + P]).then_inc(consts, 1)
            act.wait_ge(ones_set, 1)
            copy(ones_r[:, :], ones[:, :]).then_inc(consts, 1)
            ffn(0)
            norm("mem")
            conv()
            attention(0)
            ffn(1)
            act.wait_ge(dt_in, 16)
            copy(wdt_hi[:, :, :], wdt[:, :, :]).then_inc(wdt_hi_ready, 1)
            ffn(2)
            ssd()
            attention(1)
            ffn(3)
            norm(NORM_FINAL)

        @block.vector
        def _(dve):
            chain = [0]

            def step(ins):
                chain[0] += 1
                ins.then_inc(dve_step, 1)
                dve.wait_ge(dve_step, chain[0])

            def tt(out, a, b, op=ALU.mult):
                return nc.vector.tensor_tensor(out, a, b, op)

            def stt(out, a, scalar, b, op0=ALU.mult, op1=ALU.mult):
                return nc.vector.scalar_tensor_tensor(out=out, in0=a, scalar=scalar, in1=b, op0=op0, op1=op1)

            def rest_of(lo, value, hi):
                return tt(lo, value, hi.bitcast(F32), ALU.subtract)

            def split(n, i=0):
                if n >= n_units:
                    return
                s = n % SLOTS
                dve.wait_ge(hi_ready, n + 1 + SLOTS * i)
                rest_of(w_lo[s][:, 0:width[n]], raw[:, s, 0:width[n]], w_hi[s][:, 0:width[n]]).then_inc(lo_ready, 1)

            def new_h(b, k):
                dve.wait_ge(hhi_ready, H_FIRST[b] + k + 1)
                stt(h_lo[:, k, :], x[:, k, :], gain(b, k), h_hi[:, k, :].bitcast(F32), op1=ALU.subtract).then_inc(h_ready, 1)

            def norm(b, out=None):
                dve.wait_ge(ss_done, SS_INDEX[b] + 1)
                out = (rms if out is None else out)[:, :]
                nc.vector.tensor_scalar(var[:, :], bank[4][:, 0:SEQ], 1.0 / D_MODEL, EPS, ALU.mult, ALU.add).then_inc(var_ready, 1)
                dve.wait_ge(root_ready, SS_INDEX[b] + 1)
                inverse_root(out, var[:, :], root[:, :])

            def inverse_root(out, v, root_v):
                step(nc.vector.reciprocal(out, root_v))
                step(tt(root_v, v, out))
                step(tt(root_v, root_v, out))
                step(nc.vector.tensor_scalar(root_v, root_v, -0.5, 1.5, ALU.mult, ALU.add))
                step(tt(out, out, root_v))

            def scaled(factor):
                step(nc.vector.tensor_scalar(rms_k[:, :], rms[:, :], factor, None, ALU.mult))

            def ffn_unit(f, n, s, i, j, opening=False):
                if opening:
                    split(n + AHEAD)
                    norm({0: 0, 1: 3, 2: 4, 3: 7}[f])
                    scaled(0.5)
                q, up = s // 2, s % 2
                b, use = bank_use(f"gu{f}", n - first[f"gu{f}"])
                dve.wait_ge(unit_done, n + 1 + 4 * i)
                if not up:
                    at_least(dve, silu_ready, FT * f + j - 1)
                    tt(t1[q][:, :], bank[b][:, 0:SEQ], rms[:, :]).then_inc(evac[b], 1)
                else:
                    dve.wait_ge(silu_ready, FT * f + j + 1)
                    at_least(dve, a_ready, FFN_A[f] + j - 1)
                    tt(t2[q][:, :], bank[b][:, 0:SEQ], gate[q][:, :]).then_inc(evac[b], 1)
                if not opening:
                    split(n + AHEAD, i)

            def ffn(f):
                n0 = first[f"gu{f}"]
                turns = FT // 2
                for s in range(4):
                    ffn_unit(f, n0 + s, s, 0, s // 2, opening=s == 0)
                with dve.Fori(1, turns - 1) as i:
                    for s in range(4):
                        ffn_unit(f, n0 + s, s, i, 2 * i + s // 2)
                for s in range(4):
                    ffn_unit(f, n0 + 4 * (turns - 1) + s, s, 0, 2 * (turns - 1) + s // 2)
                project_out(f"down{f}", 2, 2, True)

            def project_out(phase, per_tile, banks, with_scale):
                n0 = first[phase]
                for k in range(KT):
                    if per_tile == 2:
                        split(n0 + 2 * k + AHEAD)
                    dve.wait_ge(unit_done, n0 + per_tile * (k + 1))
                    b, use = bank_use(phase, k, banks)
                    if with_scale:
                        tt(acc[k % 2][:, :], bank[b][:, 0:SEQ], rms_k[:, :]).then_inc(evac[b], 1)
                        dve.wait_ge(evac[b], use + 1)
                        tt(x[:, k, :], x[:, k, :], acc[k % 2][:, :], ALU.add).then_inc(x_ready, 1)
                    else:
                        tt(x[:, k, :], bank[b][:, 0:SEQ], x[:, k, :], ALU.add).then_inc(evac[b], 1)
                    if k < KT - 1 or OUT_NORM[phase] > 7:
                        split(n0 + per_tile * (k + 1) - 1 + AHEAD)
                    if OUT_NORM[phase] <= 7:
                        new_h(OUT_NORM[phase], k)
                    if k == KT - 1 and OUT_NORM[phase] <= 7:
                        split(n0 + per_tile * (k + 1) - 1 + AHEAD)

            def conv():
                n0 = first["conv_in"]
                for t in range(3 * KT):
                    if t == 0:
                        split(n0 + t + AHEAD)
                        norm(NORM_MIX0)
                        step(tt(rms_k[:, :], rms[:, :], rms[:, :]))
                    j, q = t // 3, t % 3
                    b, use = bank_use("conv_in", t)
                    dve.wait_ge(unit_done, n0 + t + 1)
                    if q == 0:
                        tt(t1[0][:, :], bank[b][:, 0:SEQ], rms_k[:, :]).then_inc(evac[b], 1)
                        if t:
                            split(n0 + t + AHEAD)
                        dve.wait_ge(evac[b], use + 1)
                    elif q == 1:
                        tt(padded[:, 2:2 + SEQ], bank[b][:, 0:SEQ], t1[0][:, :]).then_inc(evac[b], 1)
                        split(n0 + t + AHEAD)
                        dve.wait_ge(evac[b], use + 1)
                        step(nc.vector.tensor_scalar(acc[0][:, :], padded[:, 0:SEQ], col(C_CONVK, 3 * j), None, ALU.mult))
                        for w in range(1, 3):
                            step(stt(acc[0][:, :], padded[:, w:w + SEQ], col(C_CONVK, 3 * j + w), acc[0][:, :], op1=ALU.add))
                    else:
                        at_least(dve, a_ready, CONV_A + j - 1)
                        tt(t2[j % 2][:, :], bank[b][:, 0:SEQ], acc[0][:, :]).then_inc(evac[b], 1)
                        split(n0 + t + AHEAD)
                step(nc.vector.tensor_copy(rms_k[:, :], rms[:, :]))
                project_out("conv_out", 1, 4, True)

            def softmax_max(layer, h):
                dve.wait_ge(s_done, HEADS * layer + h + 1)
                if h:
                    dve.wait_ge(exp_ready, 2 * (HEADS * layer + h))
                step(nc.vector.tensor_reduce(mx[:, :], bank[5][:, :].rearrange("p (a n) -> p a n", a=2), AX.X, ALU.max))
                nc.vector.tensor_scalar(neg_mx[:, :], mx[:, :], -1.0, None, ALU.mult).then_inc(max_ready, 1)

            def softmax_norm(layer, h):
                dve.wait_ge(exp_ready, 2 * (HEADS * layer + h) + 2)
                step(nc.vector.reciprocal(inv_tot[:, :], tot[:, :]))
                for t in range(2):
                    nc.vector.tensor_scalar(probs[h][:, t, :], probs[h][:, t, :], inv_tot[:, t:t + 1], None,
                                            ALU.mult).then_inc(probs_ready, 1)

            def pt_part(layer, h):
                dve.wait_ge(pthi_ready, HEADS * layer + h + 1)
                rest_of(pt_lo[:, :, :], bank[6][:, :].rearrange("p (a n) -> p a n", a=2), pt_hi[:, :, :]).then_inc(pt_ready, 1)

            def o_part(layer, h):
                dve.wait_ge(ohi_ready, HEADS * layer + h + 1)
                rest_of(a_lo[:, 2 * h:2 * h + 2, :], bank[7][:, :].rearrange("p (a n) -> p a n", a=2),
                        a_hi[:, 2 * h:2 * h + 2, :]).then_inc(o_ready, 1)

            def attention(layer):
                n0 = first[f"q{layer}"]
                for s in range(24):
                    if s == 0:
                        split(n0 + s + AHEAD)
                        norm(2 if layer == 0 else 6)
                        scaled(HEAD_W ** -0.5)
                    if s < KT:
                        if s == 0:
                            dve.wait_ge(mem_in, 16 * layer + 16)
                        if s >= 2:
                            dve.wait_ge(mem_hi, KT * layer + s - 1)
                        stt(gate[s % 2][:, :], mem[:, s, :], gain(NORM_MEM + layer, s), rms_mem[:, :]).then_inc(mem_val, 1)
                        dve.wait_ge(unit_done, n0 + s + 1)
                        b, use = bank_use(f"q{layer}", s)
                        at_least(dve, a_ready, Q_A[layer] + s - 1)
                        tt(t2[s % 2][:, :], bank[b][:, 0:SEQ], rms_k[:, :]).then_inc(evac[b], 1)
                        if s:
                            split(n0 + s + AHEAD)
                        dve.wait_ge(mem_hi, KT * layer + s + 1)
                        rest_of(mn_lo[:, s, :], gate[s % 2][:, :], mn_hi[:, s, :]).then_inc(mem_lo, 1)
                    elif s < 2 * KT:
                        dve.wait_ge(kv_hi, 16 * layer + s - KT + 1)
                        b = s % 4
                        rest_of(k_lo[:, s - KT, :], bank[b][:, 0:N_MEM], k_hi[:, s - KT, :]).then_inc(evac[b], 1)
                        split(n0 + s + AHEAD)
                    elif s % 2 == 0:
                        split(n0 + s + AHEAD)
                    else:
                        c = (s - 2 * KT) // 2
                        for mt in range(2):
                            dve.wait_ge(kv_hi, 16 * layer + KT + 2 * c + mt + 1)
                            b = 2 * (c % 2) + mt
                            cols = slice(c * 256, c * 256 + 256)
                            rest_of(v_lo[:, mt, cols], bank[b][:, 0:256], v_hi[:, mt, cols]).then_inc(evac[b], 1)
                        split(n0 + s + AHEAD)
                    for h in range(HEADS):
                        if s == 11 + 2 * h:
                            softmax_max(layer, h)
                            softmax_norm(layer, h)
                        if s == 18 + 2 * h:
                            pt_part(layer, h)
                        if s == 19 + 2 * h:
                            o_part(layer, h)
                pt_part(layer, 3)
                o_part(layer, 3)
                project_out(f"o{layer}", 1, 4, False)

            def heads_over(t, g):
                return t[:, g * HPG:g * HPG + HPG].unsqueeze(2).broadcast_to((P, HPG, HD))

            def dt_chain():
                dve.wait_ge(dt_done, 1)
                for c in range(2):
                    step(stt(d["x"][:, c, :], bank[7][:, c * H:c * H + H], rms_n[:, c:c + 1],
                             cst[:, C_DTB:C_DTB + H], op1=ALU.add))
                stt(d["abs"][:, :, :], d["x"][:, :, :], -1.0, d["x"][:, :, :], op1=ALU.max).then_inc(dt_x, 1)
                dve.wait_ge(dt_e, 2)
                nc.vector.tensor_scalar(d["u"][:, :, :], d["e"][:, :, :], 1.0, None, ALU.add).then_inc(dt_u, 1)
                dve.wait_ge(dt_u, 1)
                step(stt(d["c"][:, :, :], d["u"][:, :, :], -1.0, d["e"][:, :, :], op0=ALU.add, op1=ALU.subtract))
                step(nc.vector.reciprocal(d["inv"][:, :, :], d["u"][:, :, :]))
                step(tt(d["c"][:, :, :], d["c"][:, :, :], d["inv"][:, :, :]))
                dve.wait_ge(dt_ln, 1)
                step(tt(d["c"][:, :, :], d["ln"][:, :, :], d["c"][:, :, :], ALU.subtract))
                step(stt(d["sp"][:, :, :], d["x"][:, :, :], 0.0, d["c"][:, :, :], op0=ALU.max, op1=ALU.add))
                for c in range(2):
                    ins = stt(d["da"][:, c, :], d["sp"][:, c, :], -1.0, a_exp[:, :])
                ins.then_inc(da_val, 1)
                dve.wait_ge(dahi_ready, 1)
                rest_of(da_lo[:, :, :], d["da"][:, :, :], da_hi[:, :, :]).then_inc(da_ready, 1)

            def acum_chain():
                dve.wait_ge(acum_done, 1)
                nc.vector.tensor_scalar(d["nacum"][:, :, :], bank[7][:, 64:64 + 2 * H].rearrange("p (c h) -> p c h", c=2),
                                        -1.0, None, ALU.mult).then_inc(acum_ready, 1)
                dve.wait_ge(acum_ready, 1)
                tt(rest[:, :], bank[7][:, 128:128 + H], d["nacum"][:, 0, :], ALU.add).then_inc(acum_ready, 1)

            def ssd():
                nz = first["z"]
                for s in range(16):
                    split(nz + s + AHEAD)
                    if s == 0:
                        norm(NORM_MIX1)
                        nc.vector.tensor_scalar(var_n[:, :], bank[4][:, 256:260].rearrange("p (a b) -> p a b", a=2)[:, :, 0],
                                                1.0 / D_MODEL, EPS, ALU.mult, ALU.add).then_inc(small_var_ready, 1)
                        dve.wait_ge(small_root_ready, 1)
                        inverse_root(rms_n[:, :], var_n[:, :], root_n[:, :])
                    if s == 1:
                        dt_chain()
                    if s == 2:
                        acum_chain()
                    if s == 3:
                        dve.wait_ge(acum_exp, 2)
                        tt(dsd[:, :], dsd[:, :], d["sp"][:, 0, :]).then_inc(dsd_ready, 1)
                        dve.wait_ge(dsd_ready, 1)
                    if s >= 4 and s < 12:
                        k = s - 4
                        stt(normed[k], x[:, k, :], gain(NORM_MIX1, k), rms[:, :]).then_inc(normed_ready, 1)
                dve.wait_ge(unit_done, nz + 16)
                for k in range(KT):
                    dve.wait_ge(hhi_ready, H_EXTRA + k + 1)
                    rest_of(h_lo[:, k, :], normed[k], h_hi[:, k, :]).then_inc(h_ready, 1)
                nx = first["xbc"]
                for t in range(SSD_STEPS):
                    G, q = divmod(t, 4)
                    if t < 36:
                        split(nx + t + AHEAD)
                    if G < GROUPS:
                        dve.wait_ge(conv_begun, t + 1)
                        o = acc[t % 2]
                        for w in range(3):
                            late = 3 - w
                            ins = stt(o[:, late:SEQ], bank[q][:, 0:SEQ - late], col(C_SSDK, 4 * t + w), o[:, late:SEQ], op1=ALU.add)
                            if w < 2:
                                step(ins)
                            else:
                                ins.then_inc(evac[q], 1)
                    g = G - 4
                    if 0 <= g < GROUPS and q == 0:
                        dve.wait_ge(yhi_ready, 2 * g + 2)
                        for u in range(2):
                            j = 2 * g + u
                            stt(a_lo[:, j, :], bank[5][:, u * SEQ:u * SEQ + SEQ], col(C_GATE, j),
                                a_hi[:, j, :].bitcast(F32), op1=ALU.subtract).then_inc(yt_ready, 1)
                    g = G - 1
                    if 0 <= g < GROUPS:
                        if q == 0:
                            dve.wait_ge(bnhi_ready, g + 1)
                            rest_of(bn_lo, bank[6][:, 256:384], bn_hi).then_inc(bn_ready, 1)
                            dve.wait_ge(decay_ready, 2 * g + 2)
                            at_least(dve, mlo_ready, 2 * g)
                            for c in range(2):
                                for r in range(HPG):
                                    hd = g * HPG + r
                                    ins = stt(m[:, c * 512 + r * P:c * 512 + r * P + P], decay[:, g, c, r * P:r * P + P],
                                              d["sp"][:, c, hd:hd + 1], bank[6][:, c * P:c * P + P])
                                ins.then_inc(m_ready, 1)
                        if q == 2:
                            dve.wait_ge(xnhi_ready, g + 1)
                            at_least(dve, xslo_ready, g)
                            tt(xs.rearrange("p (r n) -> p r n", r=HPG),
                               bank[5][:, 0:GW].rearrange("p (r n) -> p r n", r=HPG), heads_over(dsd, g)).then_inc(xs_ready, 1)
                            at_least(dve, y_added, g)
                            for c in range(2):
                                ins = tt(xd[:, c, :].rearrange("p (r n) -> p r n", r=HPG),
                                         bank[5][:, c * GW:c * GW + GW].rearrange("p (r n) -> p r n", r=HPG),
                                         heads_over(cst[:, C_DSKIP:C_DSKIP + H], g))
                            ins.then_inc(xd_ready, 1)
                            rest_of(xn_lo[:, :, :], bank[5][:, :].rearrange("p (a n) -> p a n", a=2), xn_hi[:, :, :]).then_inc(xn_ready, 1)
                    g = G - 2
                    if 0 <= g < GROUPS:
                        if q == 1:
                            dve.wait_ge(sthi_ready, g + 1)
                            rest_of(st_lo, bank[4][:, 0:GW], st_hi).then_inc(st_ready, 1)
                            dve.wait_ge(xd_ready, g + 1)
                            at_least(dve, yt_done, g - 1)
                            dve.wait_ge(y_done, g + 1)
                            tt(y[g % 2][:, :, :], bank[7][:, :].rearrange("p (a n) -> p a n", a=2), xd[:, :, :], ALU.add).then_inc(y_added, 1)
                        if q == 3:
                            dve.wait_ge(yo_done, g + 1)
                            at_least(dve, y_ready, g)
                            tt(y_off.rearrange("p (r n) -> p r n", r=HPG),
                               bank[4][:, 256:512].rearrange("p (r n) -> p r n", r=HPG), heads_over(e_acum, g)).then_inc(yoff_ready, 1)
                    g = G - 3
                    if 0 <= g < GROUPS:
                        if q == 1:
                            dve.wait_ge(ysq_ready, 2 * g + 2)
                            nc.vector.tensor_scalar(var_y[:, :], sum_y[:, :], 1.0 / GW, EPS, ALU.mult, ALU.add).then_inc(small_var_ready, 1)
                        if q == 2:
                            dve.wait_ge(small_root_ready, g + 2)
                            inverse_root(rms_y[:, :], var_y[:, :], root_n[:, :])
                            for c in range(2):
                                nc.vector.tensor_scalar(y[g % 2][:, c, :], y[g % 2][:, c, :], rms_y[:, c:c + 1], None,
                                                        ALU.mult).then_inc(yn_ready, 1)
                for k in range(KT):
                    splits = ssd_out_splits(k)
                    dve.wait_ge(unit_done, ssd_out_unit(k) + 1)
                    b, use = bank_use("ssd_out", k)
                    tt(x[:, k, :], bank[b][:, 0:SEQ], x[:, k, :], ALU.add).then_inc(evac[b], 1)
                    for n in splits:
                        split(n)
                    new_h(OUT_NORM["ssd_out"], k)

            nc.vector.memset(ones[:, :], 1.0).then_inc(ones_set, 1)
            step(nc.vector.memset(padded[:, 0:4], 0.0))
            dve.wait_ge(cst_in, 16)
            for k in range(KT):
                new_h(0, k)
            for n in range(AHEAD):
                split(n)
            ffn(0)
            norm("mem", rms_mem)
            conv()
            attention(0)
            ffn(1)
            dve.wait_ge(wdt_hi_ready, 1)
            rest_of(wdt_lo[:, :, :], wdt[:, :, :], wdt_hi[:, :, :]).then_inc(wdt_ready, 1)
            ffn(2)
            ssd()
            attention(1)
            ffn(3)
            norm(NORM_FINAL)
            for k in range(KT):
                stt(a_out(k), x[:, k, :], gain(NORM_FINAL, k), rms[:, :]).then_inc(out_ready, 1)

        @block.gpsimd
        def _(pool):
            steps = [0]

            def square_sum(src, k):
                if k == 0:
                    nc.gpsimd.tensor_tensor(ssq[:, :], src, src, ALU.mult).then_inc(ssq_step, 1)
                    steps[0] += 1
                    return
                nc.gpsimd.tensor_tensor(sq[:, :], src, src, ALU.mult).then_inc(ssq_step, 1)
                steps[0] += 1
                pool.wait_ge(ssq_step, steps[0])
                nc.gpsimd.tensor_tensor(ssq[:, :], ssq[:, :], sq[:, :], ALU.add).then_inc(ssq_step, 1)
                steps[0] += 1
                pool.wait_ge(ssq_step, steps[0])

            def a_part(j, count, src):
                pool.wait_ge(ahi_ready, count + 1)
                nc.gpsimd.tensor_tensor(j(a_lo), src, j(a_hi).bitcast(F32), ALU.subtract).then_inc(a_ready, 1)

            def ffn(f):
                for j in range(2):
                    a_part(lambda t, j=j: t[:, j, :], FFN_A[f] + j, t2[j][:, :])
                with pool.Fori(1, FT // 2) as i:
                    for q in range(2):
                        a_part(lambda t, q=q: t[:, bass.ds(2 * i + q, 1), :].rearrange("p a n -> p (a n)"),
                               FFN_A[f] + 2 * i + q, t2[q][:, :])
                if f == 0:
                    pool.wait_ge(mem_in, 16)
                    pool.wait_ge(ss_done, 1)
                    for k in range(KT):
                        square_sum(mem[:, k, :], k)
                    pool.wait_ge(ss_done, 2)
                project_out(f"down{f}")

            def project_out(phase):
                for k in range(KT):
                    pool.wait_ge(*x_signal(phase, k))
                    square_sum(x[:, k, :], k)

            def attention(layer):
                for k in range(KT):
                    a_part(lambda t, k=k: t[:, KT + k, :], Q_A[layer] + k, t2[k % 2][:, :])
                project_out(f"o{layer}")

            def ssd():
                for t in range(SSD_STEPS):
                    G, q = divmod(t, 4)
                    if G < GROUPS and q == 1:
                        pool.wait_ge(bhi_ready, 2 * G + 1)
                        at_least(pool, cb_done, 2 * G)
                        nc.gpsimd.tensor_tensor(b_lo, act_xbc[0], b_hi.bitcast(F32), ALU.subtract).then_inc(b_ready, 1)
                    if G < GROUPS and q == 2:
                        pool.wait_ge(bhi_ready, 2 * G + 2)
                        at_least(pool, yo_done, G - 1)
                        nc.gpsimd.tensor_tensor(c_lo[:, G % 2, :], act_xbc[1], c_hi[:, G % 2, :].bitcast(F32),
                                                ALU.subtract).then_inc(b_ready, 1)
                    g = G - 1
                    if 0 <= g < GROUPS:
                        if q == 1:
                            at_least(pool, y_done, g)
                            for c in range(2):
                                pool.wait_ge(mhi_ready, 2 * g + c + 1)
                                cols = slice(c * 512, c * 512 + 512)
                                nc.gpsimd.tensor_tensor(m_lo[:, cols], m[:, cols], m_hi[:, cols].bitcast(F32), ALU.subtract).then_inc(mlo_ready, 1)
                        if q == 3:
                            pool.wait_ge(xshi_ready, g + 1)
                            at_least(pool, state_done, g)
                            nc.gpsimd.tensor_tensor(xs_lo, xs, xs_hi.bitcast(F32), ALU.subtract).then_inc(xslo_ready, 1)
                    g = G - 2
                    if 0 <= g < GROUPS and q == 3:
                        pool.wait_ge(yoff_ready, g + 1)
                        pool.wait_ge(y_added, g + 1)
                        nc.gpsimd.tensor_tensor(y[g % 2][:, 1, :], y[g % 2][:, 1, :], y_off, ALU.add).then_inc(ysum_ready, 1)
                        pool.wait_ge(ysum_ready, g + 1)
                        pool.wait_ge(zs_ready, g + 1)
                        nc.gpsimd.tensor_tensor(y[g % 2][:, :, :], y[g % 2][:, :, :], zs[:, :, :], ALU.mult).then_inc(y_ready, 1)
                project_out("ssd_out")

            pool.wait_ge(x_in, 16)
            for k in range(KT):
                square_sum(x[:, k, :], k)
            ffn(0)
            for k in range(KT):
                a_part(lambda t, k=k: t[:, k, :], CONV_A + k, t2[k % 2][:, :])
            project_out("conv_out")
            attention(0)
            ffn(1)
            ffn(2)
            ssd()
            attention(1)
            ffn(3)

        @block.tensor
        def _(pe):
            def mm(out, lhs, rhs, start, stop, check=False):
                return nc.tensor.matmul(out, lhs, rhs, start=start, stop=stop, skip_group_check=check)

            def three(out, lh, ll, rh, rl, start, stop, check=False):
                mm(out, lh, rh, start, False, check)
                mm(out, lh, rl, False, False, check)
                return mm(out, ll, rh, False, stop, check)

            def unit(n, out, blocks, k0, r_hi, r_lo, start, stop, i=0, ready=None):
                s = n % SLOTS
                pe.wait_ge(lo_ready, n + 1 + SLOTS * i)
                for k in range(blocks):
                    if ready:
                        pe.wait_ge(ready[0], ready[1] + k0 + k + 1)
                    w = slice(k * P, k * P + P)
                    ins = three(out[:, 0:SEQ], w_hi[s][:, w], w_lo[s][:, w], r_hi[:, k0 + k, :], r_lo[:, k0 + k, :],
                                start and k == 0, stop and k == blocks - 1)
                ins.then_inc(unit_done, 1)

            def norm(b):
                pe.wait_ge(ssq_step, ssq_count(b))
                at_least(pe, var_ready, SS_INDEX[b])
                ins = mm(bank[4][:, 0:SEQ], ones[:, :], ssq[:, :], True, True)
                if b == NORM_MIX1:
                    for t in range(2):
                        ins = mm(bank[4][:, 256 + 2 * t:258 + 2 * t], ssq[:, t * P:t * P + P], ones[:, 0:2], True, True)
                ins.then_inc(ss_done, 1)

            def free(phase, t, banks=4, i=0):
                b, use = bank_use(phase, t, banks)
                at_least(pe, evac[b], use + i)
                return bank[b]

            def ffn(f):
                b = {0: 0, 1: 3, 2: 4, 3: 7}[f]
                n0, name = first[f"gu{f}"], f"gu{f}"
                for s in range(4):
                    unit(n0 + s, free(name, s), KT, 0, h_hi, h_lo, True, True, ready=(h_ready, H_FIRST[b]) if s == 0 else None)
                    if s == 0:
                        norm(b)
                with pe.Fori(1, FT // 2) as i:
                    for s in range(4):
                        unit(n0 + s, free(name, s, i=i), KT, 0, h_hi, h_lo, True, True, i)
                name = f"down{f}"
                n0 = first[name]
                half = FT // 2

                def pair(i, ready):
                    for t in range(2):
                        out = free(name, t, 2, i)
                        for u in range(2):
                            unit(n0 + 2 * t + u, out, half, u * half, a_hi, a_lo, u == 0, u == 1, i, ready if t == 0 else None)

                pair(0, (a_ready, FFN_A[f]))
                if f == 0:
                    norm("mem")
                with pe.Fori(1, KT // 2) as i:
                    pair(i, None)

            def project(name, b, tiles=KT, extra=None):
                for t in range(tiles):
                    unit(first[name] + t, free(name, t), KT, 0, h_hi, h_lo, True, True, ready=(h_ready, H_FIRST[b]) if t == 0 else None)
                    if t == 0:
                        norm(b)

            def scores(h):
                for t in range(2):
                    for k in range(2):
                        lq = slice(t * P, t * P + P)
                        ins = three(bank[5][:, t * 256:t * 256 + 256], a_hi[:, KT + 2 * h + k, lq], a_lo[:, KT + 2 * h + k, lq],
                                    k_hi[:, 2 * h + k, :], k_lo[:, 2 * h + k, :], k == 0, k == 1)
                ins.then_inc(s_done, 1)

            def turn(layer, h):
                pe.wait_ge(probs_ready, 2 * (HEADS * layer + h) + 2)
                at_least(pe, pt_ready, HEADS * layer + h)
                for mt in range(2):
                    for t in range(2):
                        ins = nc.tensor.transpose(bank[6][:, mt * 256 + t * P:mt * 256 + t * P + P],
                                                  probs[h][:, t, mt * P:mt * P + P], cst[:, C_EYE:C_EYE + P])
                ins.then_inc(pt_done, 1)

            def values(layer, h):
                pe.wait_ge(pt_ready, HEADS * layer + h + 1)
                at_least(pe, o_ready, HEADS * layer + h)
                for t in range(2):
                    cols = slice(h * HEAD_W + t * P, h * HEAD_W + t * P + P)
                    for mt in range(2):
                        ins = three(bank[7][:, t * SEQ:t * SEQ + SEQ], v_hi[:, mt, cols], v_lo[:, mt, cols],
                                    pt_hi[:, mt, :], pt_lo[:, mt, :], mt == 0, mt == 1)
                ins.then_inc(o_done, 1)

            def natural_unit(n, outs, k0, l_hi, l_lo, start, stop):
                s = n % SLOTS
                pe.wait_ge(lo_ready, n + 1)
                for k in range(4):
                    w = slice(k * 256, k * 256 + 256)
                    for t in range(2):
                        lt = slice(t * P, t * P + P)
                        ins = three(outs[t][:, 0:256], l_hi[:, k0 + k, lt], l_lo[:, k0 + k, lt], w_hi[s][:, w], w_lo[s][:, w],
                                    start and k == 0, stop and k == 3)
                ins.then_inc(unit_done, 1)

            def attention(layer):
                n0 = first[f"q{layer}"]
                b = 2 if layer == 0 else 6
                project(f"q{layer}", b)
                for s in range(KT, 24):
                    if s < 2 * KT:
                        t = s - KT
                        unit(n0 + s, free(f"k{layer}", t), KT, 0, mn_hi, mn_lo, True, True,
                             ready=(mem_lo, KT * layer) if t == 0 else None)
                    else:
                        c, u = divmod(s - 2 * KT, 2)
                        if u == 0:
                            outs = [free(f"v{layer}", 2 * c + t) for t in range(2)]
                        natural_unit(n0 + s, outs, 4 * u, mn_hi, mn_lo, u == 0, u == 1)
                    for h in range(HEADS):
                        if s == 10 + 2 * h:
                            pe.wait_ge(a_ready, Q_A[layer] + 2 * h + 2)
                            for t in range(2 * h, 2 * h + 2):
                                kb, use = bank_use(f"k{layer}", t)
                                pe.wait_ge(evac[kb], use + 1)
                            at_least(pe, exp_ready, 2 * (HEADS * layer + h))
                            scores(h)
                        if s == 17 + 2 * h:
                            turn(layer, h)
                        if s == 18 + 2 * h:
                            wait_v(layer, h)
                            values(layer, h)
                wait_v(layer, 3)
                values(layer, 3)
                for t in range(KT):
                    out = free(f"o{layer}", t)
                    s = (first[f"o{layer}"] + t) % SLOTS
                    pe.wait_ge(lo_ready, first[f"o{layer}"] + t + 1)
                    for k in range(KT):
                        if t == 0 and k % 2 == 0:
                            pe.wait_ge(o_ready, HEADS * layer + k // 2 + 1)
                        w = slice(k * P, k * P + P)
                        ins = three(out[:, 0:SEQ], w_hi[s][:, w], w_lo[s][:, w], a_hi[:, k, :], a_lo[:, k, :], k == 0, k == KT - 1)
                    ins.then_inc(unit_done, 1)

            def wait_v(layer, h):
                for mt in range(2):
                    vb, use = bank_use(f"v{layer}", 2 * h + mt)
                    pe.wait_ge(evac[vb], use + 1)

            def decays(l):
                g, c = l // 2, l % 2
                at_least(pe, decay_ready, l - 1)
                out = bank[5 + l % 2]
                mm(out[:, :].rearrange("p (r n) -> p r n", r=HPG), eye_r[:, :], mask_r[:, :].unsqueeze(1).broadcast_to((P, HPG, CHUNK)), True, False, True)
                for r in range(HPG):
                    hd = g * HPG + r
                    for part in (da_hi, da_lo):
                        ins = mm(out[:, r * P:r * P + P], part[:, c, hd:hd + 1].broadcast_to((P, P)), tri_r[:, :],
                                 False, r == HPG - 1 and part is da_lo, True)
                ins.then_inc(l_done, 1)

            def ssd():
                nz = first["z"]
                lcount = 0
                for s in range(16):
                    c, u = divmod(s, 2)
                    if u == 0:
                        outs = [free("z", 2 * c + t) for t in range(2)]
                    if s == 0:
                        for k in range(KT):
                            pe.wait_ge(h_ready, H_FIRST[NORM_MIX1] + k + 1)
                    natural_unit(nz + s, outs, 4 * u, h_hi, h_lo, u == 0, u == 1)
                    if s == 0:
                        norm(NORM_MIX1)
                        pe.wait_ge(wdt_ready, 1)
                        for t in range(2):
                            lt = slice(t * P, t * P + P)
                            for k in range(KT):
                                ins = three(bank[7][:, t * H:t * H + H], h_hi[:, k, lt], h_lo[:, k, lt], wdt_hi[:, k, :], wdt_lo[:, k, :],
                                            k == 0, k == KT - 1)
                        ins.then_inc(dt_done, 1)
                    if s == 2:
                        pe.wait_ge(da_ready, 1)
                        for cc in range(2):
                            mm(bank[7][:, 64 + cc * H:64 + cc * H + H], tri_r[:, :], da_hi[:, cc, :], True, False)
                            mm(bank[7][:, 64 + cc * H:64 + cc * H + H], tri_r[:, :], da_lo[:, cc, :], False, True)
                        mm(bank[7][:, 128:128 + H], ones_r[:, :], da_hi[:, 0, :], True, False)
                        mm(bank[7][:, 128:128 + H], ones_r[:, :], da_lo[:, 0, :], False, True).then_inc(acum_done, 1)
                    if s >= 3:
                        while lcount < min(16, (s - 2) * 16 // 12):
                            decays(lcount)
                            lcount += 1
                nx = first["xbc"]
                for t in range(SSD_STEPS):
                    G, q = divmod(t, 4)
                    if G < GROUPS:
                        unit(nx + t, free("xbc", t), KT, 0, h_hi, h_lo, True, True, ready=(h_ready, H_EXTRA) if t == 0 else None)
                    elif t < 36:
                        unit(nx + t, free("ssd_out", q), KT, 0, a_hi, a_lo, True, False, ready=(yt_ready, 0) if q == 0 else None)
                    g = G - 2
                    if 0 <= g < GROUPS and q == 0:
                        at_least(pe, y_added, g)
                        pe.wait_ge(bn_ready, g + 1)
                        pe.wait_ge(xslo_ready, g + 1)
                        at_least(pe, yoff_ready, g)
                        pe.wait_ge(small_var_ready, 1)
                        three(bank[4][:, 0:GW], bn_hi, bn_lo, xs_hi, xs_lo, True, True).then_inc(state_done, 1)
                        pe.wait_ge(mlo_ready, 2 * g + 2)
                        pe.wait_ge(xn_ready, g + 1)
                        for c in range(2):
                            for r in range(HPG):
                                mc = slice(c * 512 + r * P, c * 512 + r * P + P)
                                xc = slice(r * HD, r * HD + HD)
                                ins = three(bank[7][:, c * GW + r * HD:c * GW + r * HD + HD], m_hi[:, mc], m_lo[:, mc],
                                            xn_hi[:, c, xc], xn_lo[:, c, xc], True, True)
                        ins.then_inc(y_done, 1)
                    if 0 <= g < GROUPS and q == 2:
                        pe.wait_ge(st_ready, g + 1)
                        three(bank[4][:, 256:512], c_hi[:, g % 2, P:2 * P], c_lo[:, g % 2, P:2 * P], st_hi, st_lo,
                              True, True).then_inc(yo_done, 1)
                    g = G - 1
                    if 0 <= g < GROUPS and q == 1:
                        pe.wait_ge(xbc_ready, 4 * g + 4)
                        if g == 0:
                            pe.wait_ge(decay_ready, 16)
                        at_least(pe, yt_ready, 2 * (g - 2))
                        for c in range(2):
                            for u in range(2):
                                ins = nc.tensor.transpose(bank[5][:, c * 256 + u * P:c * 256 + u * P + P],
                                                          act_xbc[2 + u][:, c * P:c * P + P], cst[:, C_EYE:C_EYE + P])
                        ins.then_inc(xt_done, 1)
                    if G < GROUPS and q == 3:
                        pe.wait_ge(b_ready, 2 * G + 2)
                        at_least(pe, m_ready, 2 * G)
                        at_least(pe, bn_ready, G)
                        if G == 0:
                            pe.wait_ge(decay_ready, 16)
                        for c in range(2):
                            lc = slice(c * P, c * P + P)
                            ins = three(bank[6][:, c * P:c * P + P], b_hi[:, lc], b_lo[:, lc], c_hi[:, G % 2, lc], c_lo[:, G % 2, lc],
                                        True, True)
                        ins.then_inc(cb_done, 1)
                        nc.tensor.transpose(bank[6][:, 256:384], act_xbc[0][:, 0:P], cst[:, C_EYE:C_EYE + P]).then_inc(cb_done, 1)
                    g = G - 3
                    if 0 <= g < GROUPS and q == 3:
                        pe.wait_ge(yn_ready, 2 * g + 2)
                        pe.wait_ge(xn_ready, min(g + 3, GROUPS))
                        for u in range(2):
                            for c in range(2):
                                ins = nc.tensor.transpose(bank[5][:, u * SEQ + c * P:u * SEQ + c * P + P],
                                                          y[g % 2][:, c, u * P:u * P + P], cst[:, C_EYE:C_EYE + P])
                        ins.then_inc(yt_done, 1)
                for k in range(KT):
                    if k < 4:
                        unit(ssd_out_unit(k), bank[k], KT, KT, a_hi, a_lo, False, True, ready=(yt_ready, 0) if k == 0 else None)
                    else:
                        out = free("ssd_out", k)
                        for u in range(2):
                            unit(ssd_out_unit(k) - 1 + u, out, KT, KT * u, a_hi, a_lo, u == 0, u == 1)

            pe.wait_ge(cst_in, 16)
            pe.wait_ge(ones_set, 1)
            ffn(0)
            pe.wait_ge(consts, 4)
            project_conv = first["conv_in"]
            project("conv_in", NORM_MIX0, 3 * KT)
            for t in range(KT):
                unit(first["conv_out"] + t, free("conv_out", t), KT, 0, a_hi, a_lo, True, True,
                     ready=(a_ready, CONV_A) if t == 0 else None)
            attention(0)
            ffn(1)
            ffn(2)
            ssd()
            attention(1)
            ffn(3)
            norm(NORM_FINAL)


def _units(w):
    k, m = w.shape
    return w.reshape(k // P, P, m // P, P).transpose(2, 1, 0, 3).reshape(m // P, P, k)


def _halves(w, parts):
    u = _units(w)
    m, _, k = u.shape
    return u.reshape(m, P, parts, k // parts).transpose(0, 2, 1, 3).reshape(m * parts, P, k // parts)


def _natural(w):
    k, m = w.shape
    return w.reshape(2, 4, P, m // 256, 256).transpose(3, 0, 2, 1, 4).reshape(m // 128, P, 1024)


def _tiles(v):
    return v.reshape(-1, P).T


def _rows(v):
    return np.broadcast_to(v.reshape(1, -1), (P, v.size))


def kernel(**inputs):
    import concourse.bacc as bacc
    from concourse.bass_utils import run_bass_kernel_spmd

    t = {k: np.asarray(v) for k, v in inputs.items()}
    gu = t["ffn_w_gate_up"].reshape(4, D_MODEL, 2, FT, P).transpose(0, 1, 3, 2, 4).reshape(4, D_MODEL, 2 * D_FF)
    conv_in = t["conv_w_in"][0].reshape(D_MODEL, 3, KT, P)[:, [1, 2, 0]].transpose(0, 2, 1, 3).reshape(D_MODEL, 3 * D_MODEL)
    ssd_in = t["ssd_w_in"][0]
    xbc = ssd_in[:, D_INNER:D_INNER + 4096].reshape(D_MODEL, 32, P)
    order = [i for g in range(GROUPS) for i in (16 + g, 24 + g, 2 * g, 2 * g + 1)]
    ones = np.ones((P, P), np.float32)
    upper = np.triu(ones)
    gains = [t["ffn_norm"][0, 0], t["mix_norm"][0], t["xa_norm"][0], t["ffn_norm"][0, 1], t["ffn_norm"][1, 0],
             t["mix_norm"][1], t["xa_norm"][1], t["ffn_norm"][1, 1], t["final_norm"], t["xa_mem_norm"][0], t["xa_mem_norm"][1]]
    small = np.concatenate([
        *[_tiles(g) for g in gains],
        t["conv_kernel"][0].reshape(3, KT, P).transpose(2, 1, 0).reshape(P, KT * 3),
        t["ssd_conv_kernel"][0].reshape(4, 32, P)[:, order].transpose(2, 1, 0).reshape(P, 128),
        t["ssd_conv_bias"][0].reshape(32, P)[order].T,
        _tiles(t["ssd_gate_norm"][0]),
        _rows(t["ssd_dt_bias"][0]), _rows(t["ssd_a_log"][0]), _rows(t["ssd_d_skip"][0]),
        np.eye(P, dtype=np.float32), upper, np.tril(np.full((P, P), MASKED, np.float32), -1)], axis=1)
    arrays = {
        "x_t": t["x"][0].T.reshape(KT, P, SEQ).transpose(1, 0, 2),
        "mem_t": t["mem"][0].T.reshape(KT, P, N_MEM).transpose(1, 0, 2),
        "small": small,
        "w_gu": np.stack([_units(w) for w in gu]),
        "w_down": np.stack([_halves(w, 2) for w in t["ffn_w_down"].reshape(4, D_FF, D_MODEL)]),
        "w_conv_in": _units(conv_in),
        "w_conv_out": _units(t["conv_w_out"][0]),
        "w_z": _natural(ssd_in[:, :D_INNER]),
        "w_xbc": _units(xbc[:, order].reshape(D_MODEL, 4096)),
        "w_dt": ssd_in[:, D_INNER + 4096:].reshape(KT, P, SSD_HEADS).transpose(1, 0, 2),
        "w_ssd_out": _halves(t["ssd_w_out"][0], 2)[[0, 2, 4, 6, 1, 3, 5, 7, *range(8, 16)]],
        "w_q": np.stack([_units(w) for w in t["xa_w_q"]]),
        "w_k": np.stack([_units(w[:, :D_MODEL]) for w in t["xa_w_kv"]]),
        "w_v": np.stack([_natural(w[:, D_MODEL:]) for w in t["xa_w_kv"]]),
        "w_o": np.stack([_units(w) for w in t["xa_w_o"]]),
    }
    arrays = {k: np.ascontiguousarray(v) for k, v in arrays.items()}
    nc = bacc.Bacc("TRN2", target_bir_lowering=False, num_devices=1, dynamic_dma_scratch_size=1024)
    args = [nc.dram_tensor(k, v.shape, F32, kind="ExternalInput").ap() for k, v in arrays.items()]
    out = nc.dram_tensor("out_t", (P, KT, SEQ), F32, kind="ExternalOutput").ap()
    trunk(nc, *args, out)
    got = run_bass_kernel_spmd(nc, [arrays], core_ids=[0]).results[0]["out_t"]
    return np.asarray(got).transpose(2, 1, 0).reshape(1, SEQ, D_MODEL)
```

```python
from contextlib import ExitStack

import numpy as np

import concourse.bass as bass
from concourse import mybir

F32 = mybir.dt.float32
F32R = mybir.dt.float32r
ALU = mybir.AluOpType
ACT = mybir.ActivationFunctionType
AX = mybir.AxisListType

P = 128
SEQ = 256
D_MODEL = 1024
KT = D_MODEL // P
D_FF = 2816
FT = D_FF // P
N_MEM = 256
HEADS = 4
HEAD_W = D_MODEL // HEADS
GROUPS = 8
HPG = 4
HD = 64
SSD_HEADS = GROUPS * HPG
CHUNK = 128
D_INNER = SSD_HEADS * HD
IT = D_INNER // P
GW = D_INNER // GROUPS
EPS = 1e-6
MASKED = -1e30

UNIT_W = KT * P
DOWN_W = FT // 2 * P
SLOTS = 4
AHEAD = 3

N_NORMS = 11
C_GAIN = 0
C_CONVK = C_GAIN + N_NORMS * KT
C_SSDK = C_CONVK + KT * 3
C_SSDB = C_SSDK + 32 * 4
C_GATE = C_SSDB + 32
C_DTB = C_GATE + IT
C_ALOG = C_DTB + SSD_HEADS
C_DSKIP = C_ALOG + SSD_HEADS
C_EYE = C_DSKIP + SSD_HEADS
C_TRI = C_EYE + P
C_MASK = C_TRI + P
C_ALL = C_MASK + P
NORM_MIX0, NORM_XA0, NORM_MIX1, NORM_XA1, NORM_FINAL, NORM_MEM = 1, 2, 5, 6, 8, 9

PHASES = [
    ("gu0", 44, UNIT_W), ("down0", 16, DOWN_W), ("conv_in", 24, UNIT_W), ("conv_out", 8, UNIT_W),
    ("q0", 8, UNIT_W), ("k0", 8, UNIT_W), ("v0", 8, UNIT_W), ("o0", 8, UNIT_W),
    ("gu1", 44, UNIT_W), ("down1", 16, DOWN_W), ("gu2", 44, UNIT_W), ("down2", 16, DOWN_W),
    ("z", 16, UNIT_W), ("xbc", 32, UNIT_W), ("ssd_out", 16, UNIT_W),
    ("q1", 8, UNIT_W), ("k1", 8, UNIT_W), ("v1", 8, UNIT_W), ("o1", 8, UNIT_W),
    ("gu3", 44, UNIT_W), ("down3", 16, DOWN_W),
]
LAST_NORM = 8


def plan():
    first, uses, n, used = {}, {}, 0, [0] * 4
    for name, units, _ in PHASES:
        first[name], uses[name] = n, list(used)
        n += units
        tiles = units // 2 if name[:4] == "down" or name == "ssd_out" else units
        banks = 2 if name[:4] == "down" else 4
        for b in range(banks):
            used[b] += tiles // banks
    return first, uses, n


def trunk(nc, x_t, mem_t, small, w_gu, w_down, w_conv_in, w_conv_out, w_z, w_xbc, w_dt, w_ssd_out,
          w_q, w_k, w_v, w_o, out_t):
    first, uses, n_units = plan()
    width = []
    for _, units, w in PHASES:
        width += [w] * units

    with ExitStack() as ctx:
        def sb(name, shape, dt=F32):
            return ctx.enter_context(nc.sbuf_tensor(name, shape, dt))

        def sb_at(name, shape, dt=F32):
            mark = nc.sbuf_base
            return sb(name, shape, dt), mark + (-mark) % 32

        def f32_at(name, cols, offset):
            return nc.alloc_sbuf_tensor_at(name, [P, cols], F32, offset=offset)[:, :]

        def sem(name):
            return ctx.enter_context(nc.semaphore(name))

        x = sb("x", [P, KT, SEQ])
        h_hi, h_lo = sb("h_hi", [P, KT, SEQ], F32R), sb("h_lo", [P, KT, SEQ], F32R)
        (a_hi, a_hi_at), (a_lo, a_lo_at) = (sb_at(n, [P, FT, SEQ], F32R) for n in ("a_hi", "a_lo"))
        raw = sb("raw", [P, SLOTS, DOWN_W])
        w_hi, w_hi_at = zip(*(sb_at(f"w_hi{s}", [P, DOWN_W], F32R) for s in range(SLOTS)))
        w_lo, w_lo_at = zip(*(sb_at(f"w_lo{s}", [P, DOWN_W], F32R) for s in range(SLOTS)))
        mark = nc.sbuf_base
        mn_hi, mn_lo = sb("mn_hi", [P, KT, N_MEM], F32R), sb("mn_lo", [P, KT, N_MEM], F32R)
        z = nc.alloc_sbuf_tensor_at("z", [P, 2, D_INNER], F32, offset=mark + (-mark) % 32)
        mark = nc.sbuf_base
        k_hi, k_lo = sb("k_hi", [P, KT, N_MEM], F32R), sb("k_lo", [P, KT, N_MEM], F32R)
        v_hi, v_lo = sb("v_hi", [P, 2, D_MODEL], F32R), sb("v_lo", [P, 2, D_MODEL], F32R)
        decay = nc.alloc_sbuf_tensor_at("decay", [P, GROUPS, 2, HPG * CHUNK], F32, offset=mark + (-mark) % 32)
        mark = nc.sbuf_base
        mem = sb("mem", [P, KT, N_MEM])
        at = [mark + (-mark) % 32]

        def over(name, shape, dt=F32):
            t = nc.alloc_sbuf_tensor_at(name, shape, dt, offset=at[0])
            at[0] += 4 * int(np.prod(shape[1:]))
            return t

        probs_all = nc.alloc_sbuf_tensor_at("probs", [P, HEADS, 2, N_MEM], F32, offset=at[0])
        probs = [probs_all[:, h] for h in range(HEADS)]
        m = over("m", [P, 2 * HPG * CHUNK])
        wdt = over("wdt", [P, KT, SSD_HEADS])
        assert at[0] <= nc.sbuf_base
        cst = sb("cst", [P, C_ALL])
        ones = sb("ones", [P, P])
        eye_r, mask_r = (sb(n, [P, P], F32R) for n in ("eye_r", "mask_r"))
        ssq, sq = sb("ssq", [P, SEQ]), sb("sq", [P, SEQ])
        root, var, rms, rms_k, rms_mem = sb("root", [P, SEQ]), sb("var", [P, SEQ]), sb("rms", [P, SEQ]), sb("rms_k", [P, SEQ]), sb("rms_mem", [P, SEQ])
        t1_all, t2_all, gate_all = (sb(n, [P, 2, SEQ]) for n in ("t1", "t2", "gate"))
        t1, t2, gate = ([t[:, i] for i in range(2)] for t in (t1_all, t2_all, gate_all))
        padded = sb("padded", [P, 4 + SEQ])
        acc = [sb(f"acc{i}", [P, SEQ]) for i in range(2)]
        pt_hi, pt_lo = a_hi[:, 16:18, :], a_lo[:, 16:18, :]
        tile = 4 * SEQ
        m = [m[:, :], f32_at("m1", 2 * HPG * CHUNK, a_hi_at + 16 * tile)]
        c_t = [f32_at(f"c_t{i}", SEQ, at_) for i, at_ in enumerate((a_hi_at + 20 * tile, a_hi_at + 21 * tile, a_lo_at + 20 * tile))]
        mx, neg_mx, tot, inv_tot = (sb(n, [P, 2]) for n in ("mx", "neg_mx", "tot", "inv_tot"))
        act_xbc = [raw[:, s, UNIT_W:UNIT_W + SEQ] for s in range(4)]
        b_nat = [f32_at(f"b_nat{i}", P, at_ + 4 * UNIT_W) for i, at_ in enumerate((w_hi_at[0], w_lo_at[0]))]
        state = f32_at("state", GW, w_hi_at[2] + 4 * UNIT_W)
        xn = sb("xn", [P, 2, GW])
        xd = sb("xd", [P, 2, GW])
        normed = [t[:, i] for t in (t1_all, t2_all, gate_all, xd) for i in range(2)]
        first_squares = [t[:, i] for t in (t1_all, t2_all) for i in range(2)]
        y_off, xs = t1
        y = [t2_all, sb("y1", [P, 2, GW])]
        sq_y, zs = sq, gate_all
        var_y, rms_y = sb("var_y", [P, 2]), sb("rms_y", [P, 2])
        rms_n, var_n, root_n, sum_y, root_y = (sb(n, [P, 2]) for n in ("rms_n", "var_n", "root_n", "sum_y", "root_y"))
        H = SSD_HEADS
        d = {n: sb("dt_" + n, [P, 2, H]) for n in ("sp", "nacum")}
        for i, n in enumerate(("x", "abs", "e", "u", "ln", "c", "inv", "da")):
            c0 = UNIT_W + SEQ + i % 2 * 2 * H
            d[n] = raw[:, i // 2, c0:c0 + 2 * H].rearrange("p (c h) -> p c h", c=2)
        a_exp, e_acum, dsd, rest = (sb(n, [P, H]) for n in ("a_exp", "e_acum", "dsd", "rest"))

        tri = cst[:, C_TRI:C_TRI + P]

        bank = [ctx.enter_context(nc.psum_tensor(f"bank{i}", [P, 512], F32)) for i in range(8)]

        mem_in, gain_in, cst_in, dt_in = sem("mem_in"), sem("gain_in"), sem("cst_in"), sem("dt_in")
        x_in = [sem(f"x_in{c}") for c in range(KT // 2)]
        square_ready = sem("square_ready")
        landed = [sem(f"landed{s}") for s in range(SLOTS)]
        hi_ready, lo_ready = sem("hi_ready"), sem("lo_ready")
        unit_done = sem("unit_done")
        evac = [sem(f"evac{b}") for b in range(4)]
        silu_ready = sem("silu_ready")
        ahi_ready, a_ready = sem("ahi_ready"), sem("a_ready")
        x_ready = sem("x_ready")
        hhi_ready, h_ready = sem("hhi_ready"), sem("h_ready")
        ssq_step, ss_done = sem("ssq_step"), sem("ss_done")
        consts = sem("consts")
        var_ready, root_ready = sem("var_ready"), sem("root_ready")
        small_var_ready, small_root_ready = sem("small_var_ready"), sem("small_root_ready")
        ones_set, pads_set = sem("ones_set"), sem("pads_set")
        dve_step, pool_step = sem("dve_step"), sem("pool_step")
        mem_val, mem_hi, mem_lo = sem("mem_val"), sem("mem_hi"), sem("mem_lo")
        kv_hi = sem("kv_hi")
        s_done, max_ready, exp_ready, probs_ready = sem("s_done"), sem("max_ready"), sem("exp_ready"), sem("probs_ready")
        pt_done, pthi_ready, pt_ready = sem("pt_done"), sem("pthi_ready"), sem("pt_ready")
        o_done, ohi_ready, o_ready = sem("o_done"), sem("ohi_ready"), sem("o_ready")
        dt_done, dt_x, dt_e, dt_u, dt_ln, dt_a = (sem(n) for n in ("dt_done", "dt_x", "dt_e", "dt_u", "dt_ln", "dt_a"))
        da_ready = sem("da_ready")
        acum_done, acum_ready, acum_exp, dsd_ready = sem("acum_done"), sem("acum_ready"), sem("acum_exp"), sem("dsd_ready")
        l_done, decay_ready = sem("l_done"), sem("decay_ready")
        normed_ready, conv_begun, xbc_ready, y_added = (sem(n) for n in ("normed_ready", "conv_begun", "xbc_ready", "y_added"))
        cb_done, bn_ready, m_ready = sem("cb_done"), sem("bn_ready"), sem("m_ready")
        xt_done, xn_ready, xd_ready, xs_ready = sem("xt_done"), sem("xn_ready"), sem("xd_ready"), sem("xs_ready")
        state_done, st_ready = sem("state_done"), sem("st_ready")
        yoff_ready, ysum_ready, rmsy_ready = sem("yoff_ready"), sem("ysum_ready"), sem("rmsy_ready")
        y_done, yo_done, zs_ready, y_ready, ysq_ready, yn_ready = (
            sem(n) for n in ("y_done", "yo_done", "zs_ready", "y_ready", "ysq_ready", "yn_ready"))
        yt_done, yhi_ready, yt_ready = sem("yt_done"), sem("yhi_ready"), sem("yt_ready")
        out_ready, out_landed = sem("out_ready"), sem("out_landed")

        def at_least(eng, s, value):
            if isinstance(value, int) and value <= 0:
                return
            eng.wait_ge(s, value)

        def gain(b, k):
            return cst[:, C_GAIN + b * KT + k:C_GAIN + b * KT + k + 1]

        def col(c0, i):
            return cst[:, c0 + i:c0 + i + 1]

        def bank_use(phase, t, banks=4):
            return t % banks, uses[phase][t % banks] + t // banks

        FFN_A = {0: 0, 1: FT + KT + KT, 2: 2 * FT + 2 * KT, 3: 3 * FT + 3 * KT}
        CONV_A, Q_A = FT, {0: FT + KT, 1: 3 * FT + 2 * KT}
        X_COUNT = {"down0": 0, "conv_out": KT, "down1": 2 * KT, "down2": 3 * KT, "down3": 4 * KT}
        OUT_NORM = {"down0": 1, "conv_out": 2, "o0": 3, "down1": 4, "down2": 5, "ssd_out": 6, "o1": 7, "down3": 8}
        SS_INDEX = {0: 0, "mem": 1, 1: 2, 2: 3, 3: 4, 4: 5, 5: 6, 6: 7, 7: 8, 8: 9}

        def ssq_count(b):
            return (SS_INDEX[b] + 1) * (2 * KT - 1) - KT // 2

        def x_signal(phase, k):
            if phase in X_COUNT:
                return x_ready, X_COUNT[phase] + k + 1
            b, use = bank_use(phase, k)
            return evac[b], use + 1

        def a_out(k):
            return mem[:, k, :]

        H_FIRST = [KT * (b + (b > NORM_MIX1)) for b in range(LAST_NORM)]
        H_EXTRA = KT * (NORM_MIX1 + 1)
        SSD_STEPS = 4 * (GROUPS + 3) + 2
        SSD_UNITS = 4 * GROUPS + KT

        block = ctx.enter_context(nc.Block())

        @block.sync
        def _(sp):
            sp.dma_start(cst[:, 0:C_CONVK], small[:, 0:C_CONVK]).then_inc(gain_in, 16)

            def load(n, src, i=0):
                at_least(sp, lo_ready, n - SLOTS + 1 + SLOTS * i)
                sp.dma_start(raw[:, n % SLOTS, 0:width[n]], src).then_inc(landed[n % SLOTS], 16)

            def load_x(c):
                sp.dma_start(x[:, 2 * c:2 * c + 2, :], x_t[:, 2 * c:2 * c + 2, :]).then_inc(x_in[c], 16)

            def load_phase(name, w, units):
                n0 = first[name]
                for s in range(SLOTS):
                    if name == "gu0" and s == 0:
                        load_x(0)
                    load(n0 + s, w[s])
                    if name == "gu0" and s == 0:
                        for c in range(1, KT // 2):
                            load_x(c)
                if name == "gu0":
                    sp.dma_start(cst[:, C_CONVK:C_ALL], small[:, C_CONVK:C_ALL]).then_inc(cst_in, 16)
                    sp.dma_start(mem[:, :, :], mem_t).then_inc(mem_in, 16)
                if units == 2 * SLOTS:
                    for s in range(SLOTS, units):
                        load(n0 + s, w[s])
                else:
                    with sp.Fori(1, units // SLOTS) as i:
                        for s in range(SLOTS):
                            load(n0 + s, w[bass.ds(i * SLOTS + s, 1)].rearrange("a p n -> p (a n)"), i)

            sources = {"gu": w_gu, "down": w_down, "q": w_q, "k": w_k, "v": w_v, "o": w_o}
            whole = {"conv_in": w_conv_in, "conv_out": w_conv_out, "z": w_z, "xbc": w_xbc, "ssd_out": w_ssd_out}
            for name, units, _ in PHASES:
                if name in whole:
                    load_phase(name, whole[name], units)
                else:
                    load_phase(name, sources[name[:-1]][int(name[-1])], units)
                if name == "ssd_out":
                    sp.dma_start(mem[:, :, :], mem_t).then_inc(mem_in, 16)
                if name == "down1":
                    sp.dma_start(wdt[:, :, :], w_dt).then_inc(dt_in, 16)
            for k in range(KT):
                sp.wait_ge(out_ready, k + 1)
                sp.dma_start(out_t[:, k, :], a_out(k)).then_inc(out_landed, 16)
            sp.wait_ge(out_landed, 16 * KT)

        @block.scalar
        def _(act):
            def copy(out, in_, scale=1.0):
                return nc.scalar.activation(out, in_, ACT.Copy, scale=scale)

            def split(n, i=0):
                if n >= n_units:
                    return
                s = n % SLOTS
                act.wait_ge(landed[s], 16 * (n // SLOTS + 1) + 16 * i)
                at_least(act, unit_done, n - SLOTS + 1 + SLOTS * i)
                copy(w_hi[s][:, 0:width[n]], raw[:, s, 0:width[n]]).then_inc(hi_ready, 1)

            def norm(b):
                act.wait_ge(var_ready, SS_INDEX[b] + 1)
                nc.scalar.activation(root[:, :], var[:, :], ACT.Sqrt).then_inc(root_ready, 1)

            def new_h(b, k):
                copy(h_hi[:, k, :], x[:, k, :], gain(b, k)).then_inc(hhi_ready, 1)

            def a_part(j, count, src, signal, i=None):
                act.wait_ge(*signal)
                copy(a_hi[:, j, :], src).then_inc(ahi_ready, 1)

            def ffn_unit(f, n, s, i, j_of, opening=False):
                split(n + AHEAD, i)
                q, up = s // 2, s % 2
                if opening:
                    norm({0: 0, 1: 3, 2: 4, 3: 7}[f])
                b, use = bank_use(f"gu{f}", n - first[f"gu{f}"])
                act.wait_ge(evac[b], use + 1 + i)
                if not up:
                    b_up, use_up = bank_use(f"gu{f}", n + 1 - first[f"gu{f}"])
                    at_least(act, evac[b_up], use_up + i)
                    nc.scalar.activation(gate[q][:, :], t1[q][:, :], ACT.Silu).then_inc(silu_ready, 1)
                else:
                    copy(j_of(a_hi), t2[q][:, :]).then_inc(ahi_ready, 1)

            def ffn(f):
                n0 = first[f"gu{f}"]
                turns = FT // 2
                for s in range(4):
                    ffn_unit(f, n0 + s, s, 0, lambda t, s=s: t[:, s // 2, :], opening=s == 0)
                with act.Fori(1, turns - 1) as i:
                    for s in range(4):
                        ffn_unit(f, n0 + s, s, i, lambda t, s=s: t[:, bass.ds(2 * i + s // 2, 1), :].rearrange("p a n -> p (a n)"))
                for s in range(4):
                    n = n0 + 4 * (turns - 1) + s
                    ffn_unit(f, n, s, 0, lambda t, s=s: t[:, 2 * (turns - 1) + s // 2, :])
                project_out(f"down{f}", 2)

            def project_out(phase, per_tile):
                n0 = first[phase]
                for k in range(KT):
                    for u in range(per_tile):
                        split(n0 + per_tile * k + u + AHEAD)
                    b = OUT_NORM[phase]
                    if b <= 7:
                        act.wait_ge(*x_signal(phase, k))
                        new_h(b, k)

            def conv():
                n0 = first["conv_in"]
                for t in range(3 * KT):
                    split(n0 + t + AHEAD)
                    if t == 0:
                        norm(NORM_MIX0)
                    if t % 3 == 2:
                        b, use = bank_use("conv_in", t)
                        act.wait_ge(evac[b], use + 1)
                        copy(a_hi[:, t // 3, :], t2[t // 3 % 2][:, :]).then_inc(ahi_ready, 1)
                project_out("conv_out", 1)

            def attention(layer):
                n0 = first[f"q{layer}"]
                for s in range(24):
                    split(n0 + s + AHEAD)
                    if s == 0:
                        norm(2 if layer == 0 else 6)
                    for h in range(HEADS):
                        if s == 11 + 2 * h:
                            act.wait_ge(max_ready, HEADS * layer + h + 1)
                            for tt in range(2):
                                nc.scalar.activation(probs[h][:, tt, :], bank[5][:, tt * 256:tt * 256 + 256], ACT.Exp,
                                                     bias=neg_mx[:, tt:tt + 1], accum_out=tot[:, tt:tt + 1]).then_inc(exp_ready, 1)
                        if s == 19 + 2 * h:
                            o_part(layer, h)
                    if s < KT:
                        act.wait_ge(mem_val, KT * layer + s + 1)
                        copy(mn_hi[:, s, :], gate[s % 2][:, :]).then_inc(mem_hi, 1)
                        b, use = bank_use(f"q{layer}", s)
                        act.wait_ge(evac[b], use + 1)
                        copy(a_hi[:, KT + s, :], t2[s % 2][:, :]).then_inc(ahi_ready, 1)
                    elif s < 2 * KT:
                        act.wait_ge(unit_done, n0 + s + 1)
                        copy(k_hi[:, s - KT, :], bank[s % 4][:, 0:N_MEM]).then_inc(kv_hi, 1)
                    elif s % 2:
                        act.wait_ge(unit_done, n0 + s + 1)
                        c = (s - 2 * KT) // 2
                        for mt in range(2):
                            copy(v_hi[:, mt, c * 256:c * 256 + 256], bank[2 * (c % 2) + mt][:, 0:256]).then_inc(kv_hi, 1)
                    for h in range(HEADS):
                        if s == 17 + 2 * h:
                            pt_part(layer, h)
                o_part(layer, 3)
                project_out(f"o{layer}", 1)

            def pt_part(layer, h):
                act.wait_ge(pt_done, HEADS * layer + h + 1)
                at_least(act, o_done, HEADS * layer + h)
                copy(pt_hi[:, :, :], bank[6][:, 0:512].rearrange("p (a n) -> p a n", a=2)).then_inc(pthi_ready, 1)

            def o_part(layer, h):
                act.wait_ge(o_done, HEADS * layer + h + 1)
                copy(a_hi[:, 2 * h:2 * h + 2, :], bank[7][:, 0:512].rearrange("p (a n) -> p a n", a=2)).then_inc(ohi_ready, 1)

            def decays(l):
                g, c = l // 2, l % 2
                act.wait_ge(l_done, l + 1)
                for r in range(HPG):
                    hd = g * HPG + r
                    ins = nc.scalar.activation(decay[:, g, c, r * P:r * P + P], bank[5 + l % 2][:, r * P:r * P + P],
                                               ACT.Exp, bias=d["nacum"][:, c, hd:hd + 1])
                ins.then_inc(decay_ready, 1)

            def ssd():
                nz = first["z"]
                lcount = 0
                for s in range(16):
                    split(nz + s + AHEAD)
                    if s == 0:
                        norm(NORM_MIX1)
                        act.wait_ge(small_var_ready, 1)
                        nc.scalar.activation(root_n[:, :], var_n[:, :], ACT.Sqrt).then_inc(small_root_ready, 1)
                    if s == 1:
                        act.wait_ge(dt_x, 1)
                        nc.scalar.activation(d["e"][:, :, :], d["abs"][:, :, :], ACT.Exp, scale=-1.0).then_inc(dt_e, 1)
                        nc.scalar.activation(a_exp[:, :], cst[:, C_ALOG:C_ALOG + H], ACT.Exp).then_inc(dt_e, 1)
                        act.wait_ge(dt_u, 1)
                        nc.scalar.activation(d["ln"][:, :, :], d["u"][:, :, :], ACT.Ln).then_inc(dt_ln, 1)
                    if s % 2:
                        act.wait_ge(unit_done, nz + s + 1)
                        g = s // 2
                        for tt in range(2):
                            b = 2 * (g % 2) + tt
                            copy(z[:, tt, g * GW:g * GW + GW], bank[b][:, 0:GW], rms_n[:, tt:tt + 1]).then_inc(evac[b], 1)
                    if s == 2:
                        act.wait_ge(acum_ready, 2)
                        nc.scalar.activation(e_acum[:, :], d["nacum"][:, 1, :], ACT.Exp, scale=-1.0).then_inc(acum_exp, 1)
                        nc.scalar.activation(dsd[:, :], rest[:, :], ACT.Exp).then_inc(acum_exp, 1)
                    if s >= 3:
                        while lcount < min(16, (s - 2) * 16 // 12):
                            decays(lcount)
                            lcount += 1
                act.wait_ge(unit_done, nz + 16)
                for k in range(KT):
                    act.wait_ge(normed_ready, k + 1)
                    copy(h_hi[:, k, :], normed[k]).then_inc(hhi_ready, 1)
                nx = first["xbc"]
                for t in range(SSD_STEPS):
                    G, q = divmod(t, 4)
                    if t < SSD_UNITS:
                        split(nx + t + AHEAD)
                    g = G - 4
                    if 0 <= g < GROUPS and q == 1:
                        act.wait_ge(yt_done, g + 1)
                        for u in range(2):
                            j = 2 * g + u
                            copy(a_hi[:, j, :], bank[5][:, u * SEQ:u * SEQ + SEQ], col(C_GATE, j)).then_inc(yhi_ready, 1)
                    if G < GROUPS:
                        act.wait_ge(unit_done, nx + t + 1)
                        at_least(act, xbc_ready, t - 1)
                        nc.scalar.activation(acc[t % 2][:, :], bank[q][:, 0:SEQ], ACT.Identity, bias=col(C_SSDB, t),
                                             scale=col(C_SSDK, 4 * t + 3)).then_inc(conv_begun, 1)
                    if 0 < t <= 4 * GROUPS:
                        silu_xbc(*divmod(t - 1, 4))
                    g = G - 2
                    if 0 <= g < GROUPS and q == 2:
                        act.wait_ge(state_done, g + 1)
                        at_least(act, yo_done, g)
                        copy(state, bank[4][:, 0:GW]).then_inc(st_ready, 1)
                    g = G - 1
                    if 0 <= g < GROUPS:
                        if q == 1:
                            act.wait_ge(cb_done, 2 * g + 2)
                            at_least(act, state_done, g - 1)
                            copy(b_nat[g % 2], bank[6][:, 256:384]).then_inc(bn_ready, 1)
                        if q == 2:
                            act.wait_ge(xt_done, g + 1)
                            at_least(act, y_done, g)
                            at_least(act, xs_ready, g)
                            copy(xn[:, :, :], bank[5][:, :].rearrange("p (a n) -> p a n", a=2)).then_inc(xn_ready, 1)
                            at_least(act, y_added, g)
                            for r in range(HPG):
                                ins = copy(xd[:, :, r * HD:r * HD + HD], bank[5][:, :].rearrange("p (a n) -> p a n", a=2)[:, :, r * HD:r * HD + HD],
                                           col(C_DSKIP, g * HPG + r))
                            ins.then_inc(xd_ready, 1)
                    g = G - 2
                    if 0 <= g < GROUPS:
                        if q == 1:
                            at_least(act, y_ready, g)
                            nc.scalar.activation(zs[:, :, :], z[:, :, g * GW:g * GW + GW], ACT.Silu).then_inc(zs_ready, 1)
                    g = G - 3
                    if 0 <= g < GROUPS and q == 1:
                        act.wait_ge(y_ready, g + 1)
                        for c in range(2):
                            if g or c:
                                act.wait_ge(ysq_ready, 2 * g + c)
                            nc.scalar.activation(sq_y[:, :], y[g % 2][:, c, :], ACT.Square,
                                                 accum_out=sum_y[:, c:c + 1]).then_inc(ysq_ready, 1)
                for k in range(KT):
                    split(nx + SSD_UNITS + k + AHEAD)
                    act.wait_ge(*x_signal("ssd_out", k))
                    new_h(OUT_NORM["ssd_out"], k)

            def silu_xbc(G, q):
                b, use = bank_use("xbc", q)
                act.wait_ge(evac[b], use + G + 1)
                if q == 0:
                    at_least(act, cb_done, 2 * G)
                elif q == 1:
                    at_least(act, yo_done, G - 2)
                else:
                    at_least(act, xt_done, G)
                out = c_t[G % 3] if q == 1 else act_xbc[q]
                nc.scalar.activation(out, acc[q % 2][:, :], ACT.Silu).then_inc(xbc_ready, 1)

            act.wait_ge(gain_in, 16)
            for k in range(KT):
                if k == 2:
                    split(0)
                if k % 2 == 0:
                    act.wait_ge(x_in[k // 2], 16)
                new_h(0, k)
                if k >= KT // 2:
                    nc.scalar.activation(first_squares[k - KT // 2], x[:, k, :], ACT.Square).then_inc(square_ready, 1)
            for n in range(1, AHEAD):
                split(n)
            ffn(0)
            act.wait_ge(cst_in, 16)
            copy(eye_r[:, :], cst[:, C_EYE:C_EYE + P]).then_inc(consts, 1)
            copy(mask_r[:, :], cst[:, C_MASK:C_MASK + P]).then_inc(consts, 1)
            norm("mem")
            conv()
            attention(0)
            ffn(1)
            ffn(2)
            ssd()
            attention(1)
            ffn(3)
            norm(NORM_FINAL)

        @block.vector
        def _(dve):
            chain = [0]

            def step(ins):
                chain[0] += 1
                ins.then_inc(dve_step, 1)
                dve.wait_ge(dve_step, chain[0])

            def tt(out, a, b, op=ALU.mult):
                return nc.vector.tensor_tensor(out, a, b, op)

            def stt(out, a, scalar, b, op0=ALU.mult, op1=ALU.mult):
                return nc.vector.scalar_tensor_tensor(out=out, in0=a, scalar=scalar, in1=b, op0=op0, op1=op1)

            def rest_of(lo, value, hi):
                return tt(lo, value, hi.bitcast(F32), ALU.subtract)

            def split(n, i=0):
                if n >= n_units:
                    return
                s = n % SLOTS
                dve.wait_ge(hi_ready, n + 1 + SLOTS * i)
                rest_of(w_lo[s][:, 0:width[n]], raw[:, s, 0:width[n]], w_hi[s][:, 0:width[n]]).then_inc(lo_ready, 1)

            def new_h(b, k):
                dve.wait_ge(hhi_ready, H_FIRST[b] + k + 1)
                stt(h_lo[:, k, :], x[:, k, :], gain(b, k), h_hi[:, k, :].bitcast(F32), op1=ALU.subtract).then_inc(h_ready, 1)

            def norm(b, out=None):
                dve.wait_ge(ss_done, SS_INDEX[b] + 1)
                out = (rms if out is None else out)[:, :]
                nc.vector.tensor_scalar(var[:, :], bank[4][:, 0:SEQ], 1.0 / D_MODEL, EPS, ALU.mult, ALU.add).then_inc(var_ready, 1)
                dve.wait_ge(root_ready, SS_INDEX[b] + 1)
                inverse_root(out, var[:, :], root[:, :])

            def inverse_root(out, v, root_v):
                step(nc.vector.reciprocal(out, root_v))
                step(tt(root_v, v, out))
                step(tt(root_v, root_v, out))
                step(nc.vector.tensor_scalar(root_v, root_v, -0.5, 1.5, ALU.mult, ALU.add))
                step(tt(out, out, root_v))

            def scaled(factor):
                step(nc.vector.tensor_scalar(rms_k[:, :], rms[:, :], factor, None, ALU.mult))

            def ffn_unit(f, n, s, i, j, opening=False):
                if opening:
                    split(n + AHEAD)
                    norm({0: 0, 1: 3, 2: 4, 3: 7}[f])
                    scaled(0.5)
                q, up = s // 2, s % 2
                b, use = bank_use(f"gu{f}", n - first[f"gu{f}"])
                dve.wait_ge(unit_done, n + 1 + 4 * i)
                if not up:
                    at_least(dve, silu_ready, FT * f + j - 1)
                    tt(t1[q][:, :], bank[b][:, 0:SEQ], rms[:, :]).then_inc(evac[b], 1)
                else:
                    dve.wait_ge(silu_ready, FT * f + j + 1)
                    at_least(dve, a_ready, FFN_A[f] + j - 1)
                    tt(t2[q][:, :], bank[b][:, 0:SEQ], gate[q][:, :]).then_inc(evac[b], 1)
                if not opening:
                    split(n + AHEAD, i)

            def ffn(f):
                n0 = first[f"gu{f}"]
                turns = FT // 2
                for s in range(4):
                    ffn_unit(f, n0 + s, s, 0, s // 2, opening=s == 0)
                with dve.Fori(1, turns - 1) as i:
                    for s in range(4):
                        ffn_unit(f, n0 + s, s, i, 2 * i + s // 2)
                for s in range(4):
                    ffn_unit(f, n0 + 4 * (turns - 1) + s, s, 0, 2 * (turns - 1) + s // 2)
                project_out(f"down{f}", 2, 2, True)

            def project_out(phase, per_tile, banks, with_scale):
                n0 = first[phase]
                for k in range(KT):
                    if per_tile == 2:
                        split(n0 + 2 * k + AHEAD)
                    dve.wait_ge(unit_done, n0 + per_tile * (k + 1))
                    b, use = bank_use(phase, k, banks)
                    if with_scale:
                        tt(acc[k % 2][:, :], bank[b][:, 0:SEQ], rms_k[:, :]).then_inc(evac[b], 1)
                        dve.wait_ge(evac[b], use + 1)
                        tt(x[:, k, :], x[:, k, :], acc[k % 2][:, :], ALU.add).then_inc(x_ready, 1)
                    else:
                        tt(x[:, k, :], bank[b][:, 0:SEQ], x[:, k, :], ALU.add).then_inc(evac[b], 1)
                    if k < KT - 1 or OUT_NORM[phase] > 7:
                        split(n0 + per_tile * (k + 1) - 1 + AHEAD)
                    if OUT_NORM[phase] <= 7:
                        new_h(OUT_NORM[phase], k)
                    if k == KT - 1 and OUT_NORM[phase] <= 7:
                        split(n0 + per_tile * (k + 1) - 1 + AHEAD)

            def conv():
                n0 = first["conv_in"]
                for t in range(3 * KT):
                    if t == 0:
                        split(n0 + t + AHEAD)
                        norm(NORM_MIX0)
                        step(tt(rms_k[:, :], rms[:, :], rms[:, :]))
                    j, q = t // 3, t % 3
                    b, use = bank_use("conv_in", t)
                    dve.wait_ge(unit_done, n0 + t + 1)
                    if q == 0:
                        tt(t1[0][:, :], bank[b][:, 0:SEQ], rms_k[:, :]).then_inc(evac[b], 1)
                        if t:
                            split(n0 + t + AHEAD)
                        dve.wait_ge(evac[b], use + 1)
                    elif q == 1:
                        tt(padded[:, 2:2 + SEQ], bank[b][:, 0:SEQ], t1[0][:, :]).then_inc(evac[b], 1)
                        split(n0 + t + AHEAD)
                        dve.wait_ge(evac[b], use + 1)
                        step(nc.vector.tensor_scalar(acc[0][:, :], padded[:, 0:SEQ], col(C_CONVK, 3 * j), None, ALU.mult))
                        for w in range(1, 3):
                            step(stt(acc[0][:, :], padded[:, w:w + SEQ], col(C_CONVK, 3 * j + w), acc[0][:, :], op1=ALU.add))
                    else:
                        at_least(dve, a_ready, CONV_A + j - 1)
                        tt(t2[j % 2][:, :], bank[b][:, 0:SEQ], acc[0][:, :]).then_inc(evac[b], 1)
                        split(n0 + t + AHEAD)
                step(nc.vector.tensor_copy(rms_k[:, :], rms[:, :]))
                project_out("conv_out", 1, 4, True)

            def softmax_max(layer, h):
                dve.wait_ge(s_done, HEADS * layer + h + 1)
                if h:
                    dve.wait_ge(exp_ready, 2 * (HEADS * layer + h))
                step(nc.vector.tensor_reduce(mx[:, :], bank[5][:, :].rearrange("p (a n) -> p a n", a=2), AX.X, ALU.max))
                nc.vector.tensor_scalar(neg_mx[:, :], mx[:, :], -1.0, None, ALU.mult).then_inc(max_ready, 1)

            def softmax_norm(layer, h):
                dve.wait_ge(exp_ready, 2 * (HEADS * layer + h) + 2)
                step(nc.vector.reciprocal(inv_tot[:, :], tot[:, :]))
                for t in range(2):
                    nc.vector.tensor_scalar(probs[h][:, t, :], probs[h][:, t, :], inv_tot[:, t:t + 1], None,
                                            ALU.mult).then_inc(probs_ready, 1)

            def pt_part(layer, h):
                dve.wait_ge(pthi_ready, HEADS * layer + h + 1)
                rest_of(pt_lo[:, :, :], bank[6][:, :].rearrange("p (a n) -> p a n", a=2), pt_hi[:, :, :]).then_inc(pt_ready, 1)

            def o_part(layer, h):
                dve.wait_ge(ohi_ready, HEADS * layer + h + 1)
                rest_of(a_lo[:, 2 * h:2 * h + 2, :], bank[7][:, :].rearrange("p (a n) -> p a n", a=2),
                        a_hi[:, 2 * h:2 * h + 2, :]).then_inc(o_ready, 1)

            def attention(layer):
                n0 = first[f"q{layer}"]
                for s in range(24):
                    if s == 0:
                        split(n0 + s + AHEAD)
                        norm(2 if layer == 0 else 6)
                        scaled(HEAD_W ** -0.5)
                    for h in range(HEADS):
                        if s == 11 + 2 * h:
                            softmax_max(layer, h)
                        if s == 19 + 2 * h:
                            o_part(layer, h)
                    if s < KT:
                        if s == 0:
                            dve.wait_ge(mem_in, 16 * layer + 16)
                        if s >= 2:
                            dve.wait_ge(mem_hi, KT * layer + s - 1)
                        stt(gate[s % 2][:, :], mem[:, s, :], gain(NORM_MEM + layer, s), rms_mem[:, :]).then_inc(mem_val, 1)
                        dve.wait_ge(unit_done, n0 + s + 1)
                        b, use = bank_use(f"q{layer}", s)
                        at_least(dve, a_ready, Q_A[layer] + s - 1)
                        tt(t2[s % 2][:, :], bank[b][:, 0:SEQ], rms_k[:, :]).then_inc(evac[b], 1)
                        if s:
                            split(n0 + s + AHEAD)
                        dve.wait_ge(mem_hi, KT * layer + s + 1)
                        rest_of(mn_lo[:, s, :], gate[s % 2][:, :], mn_hi[:, s, :]).then_inc(mem_lo, 1)
                    elif s < 2 * KT:
                        dve.wait_ge(kv_hi, 16 * layer + s - KT + 1)
                        b = s % 4
                        rest_of(k_lo[:, s - KT, :], bank[b][:, 0:N_MEM], k_hi[:, s - KT, :]).then_inc(evac[b], 1)
                        split(n0 + s + AHEAD)
                    elif s % 2 == 0:
                        split(n0 + s + AHEAD)
                    else:
                        c = (s - 2 * KT) // 2
                        for mt in range(2):
                            dve.wait_ge(kv_hi, 16 * layer + KT + 2 * c + mt + 1)
                            b = 2 * (c % 2) + mt
                            cols = slice(c * 256, c * 256 + 256)
                            rest_of(v_lo[:, mt, cols], bank[b][:, 0:256], v_hi[:, mt, cols]).then_inc(evac[b], 1)
                        if s > 16:
                            pt_part(layer, (s - 17) // 2)
                        split(n0 + s + AHEAD)
                    for h in range(HEADS):
                        if s == 11 + 2 * h:
                            softmax_norm(layer, h)
                o_part(layer, 3)
                project_out(f"o{layer}", 1, 4, False)

            def heads_over(t, g):
                return t[:, g * HPG:g * HPG + HPG].unsqueeze(2).broadcast_to((P, HPG, HD))

            def dt_chain():
                dve.wait_ge(dt_done, 1)
                for c in range(2):
                    step(stt(d["x"][:, c, :], bank[7][:, c * H:c * H + H], rms_n[:, c:c + 1],
                             cst[:, C_DTB:C_DTB + H], op1=ALU.add))
                stt(d["abs"][:, :, :], d["x"][:, :, :], -1.0, d["x"][:, :, :], op1=ALU.max).then_inc(dt_x, 1)
                dve.wait_ge(dt_e, 2)
                nc.vector.tensor_scalar(d["u"][:, :, :], d["e"][:, :, :], 1.0, None, ALU.add).then_inc(dt_u, 1)
                dve.wait_ge(dt_u, 1)
                step(stt(d["c"][:, :, :], d["u"][:, :, :], -1.0, d["e"][:, :, :], op0=ALU.add, op1=ALU.subtract))
                step(nc.vector.reciprocal(d["inv"][:, :, :], d["u"][:, :, :]))
                step(tt(d["c"][:, :, :], d["c"][:, :, :], d["inv"][:, :, :]))
                dve.wait_ge(dt_ln, 1)
                step(tt(d["c"][:, :, :], d["ln"][:, :, :], d["c"][:, :, :], ALU.subtract))
                step(stt(d["sp"][:, :, :], d["x"][:, :, :], 0.0, d["c"][:, :, :], op0=ALU.max, op1=ALU.add))
                for c in range(2):
                    ins = stt(d["da"][:, c, :], d["sp"][:, c, :], -1.0, a_exp[:, :])
                ins.then_inc(da_ready, 1)

            def acum_chain():
                dve.wait_ge(acum_done, 1)
                nc.vector.tensor_scalar(d["nacum"][:, :, :], bank[7][:, 64:64 + 2 * H].rearrange("p (c h) -> p c h", c=2),
                                        -1.0, None, ALU.mult).then_inc(acum_ready, 1)
                dve.wait_ge(acum_ready, 1)
                tt(rest[:, :], bank[7][:, 128:128 + H], d["nacum"][:, 0, :], ALU.add).then_inc(acum_ready, 1)

            def ssd():
                nz = first["z"]
                for s in range(16):
                    split(nz + s + AHEAD)
                    if s == 0:
                        norm(NORM_MIX1)
                        nc.vector.tensor_scalar(var_n[:, :], bank[4][:, 256:260].rearrange("p (a b) -> p a b", a=2)[:, :, 0],
                                                1.0 / D_MODEL, EPS, ALU.mult, ALU.add).then_inc(small_var_ready, 1)
                        dve.wait_ge(small_root_ready, 1)
                        inverse_root(rms_n[:, :], var_n[:, :], root_n[:, :])
                    if s == 1:
                        dt_chain()
                    if s == 2:
                        acum_chain()
                    if s == 3:
                        dve.wait_ge(acum_exp, 2)
                        tt(dsd[:, :], dsd[:, :], d["sp"][:, 0, :]).then_inc(dsd_ready, 1)
                        dve.wait_ge(dsd_ready, 1)
                    if s >= 4 and s < 12:
                        k = s - 4
                        stt(normed[k], x[:, k, :], gain(NORM_MIX1, k), rms[:, :]).then_inc(normed_ready, 1)
                dve.wait_ge(unit_done, nz + 16)
                for k in range(KT):
                    dve.wait_ge(hhi_ready, H_EXTRA + k + 1)
                    rest_of(h_lo[:, k, :], normed[k], h_hi[:, k, :]).then_inc(h_ready, 1)
                nx = first["xbc"]
                for t in range(SSD_STEPS):
                    G, q = divmod(t, 4)
                    g = G - 4
                    if 0 <= g < GROUPS and q == 1:
                        dve.wait_ge(yhi_ready, 2 * g + 2)
                        for u in range(2):
                            j = 2 * g + u
                            stt(a_lo[:, j, :], bank[5][:, u * SEQ:u * SEQ + SEQ], col(C_GATE, j),
                                a_hi[:, j, :].bitcast(F32), op1=ALU.subtract).then_inc(yt_ready, 1)
                    g = G - 3
                    if 0 <= g < GROUPS and q == 0:
                        dve.wait_ge(yo_done, g + 1)
                        at_least(dve, y_ready, g)
                        tt(y_off.rearrange("p (r n) -> p r n", r=HPG),
                           bank[4][:, 256:512].rearrange("p (r n) -> p r n", r=HPG), heads_over(e_acum, g)).then_inc(yoff_ready, 1)
                    if t < SSD_UNITS and q != 3:
                        split(nx + t + AHEAD)
                    g = G - 3
                    if 0 <= g < GROUPS and q == 3:
                        dve.wait_ge(rmsy_ready, g + 1)
                        for c in range(2):
                            nc.vector.tensor_scalar(y[g % 2][:, c, :], y[g % 2][:, c, :], rms_y[:, c:c + 1], None,
                                                    ALU.mult).then_inc(yn_ready, 1)
                    if G < GROUPS:
                        dve.wait_ge(conv_begun, t + 1)
                        o = acc[t % 2]
                        for w in range(3):
                            late = 3 - w
                            ins = stt(o[:, late:SEQ], bank[q][:, 0:SEQ - late], col(C_SSDK, 4 * t + w), o[:, late:SEQ], op1=ALU.add)
                            if w < 2:
                                step(ins)
                            else:
                                ins.then_inc(evac[q], 1)
                    if t < SSD_UNITS and q == 3:
                        split(nx + t + AHEAD)
                    g = G - 2
                    if 0 <= g < GROUPS and q == 2:
                        dve.wait_ge(xd_ready, g + 1)
                        at_least(dve, yt_done, g - 1)
                        dve.wait_ge(y_done, g + 1)
                        tt(y[g % 2][:, :, :], bank[7][:, :].rearrange("p (a n) -> p a n", a=2), xd[:, :, :], ALU.add).then_inc(y_added, 1)
                    g = G - 1
                    if 0 <= g < GROUPS:
                        if q == 1:
                            dve.wait_ge(bn_ready, g + 1)
                        if q in (1, 2):
                            c = q - 1
                            dve.wait_ge(decay_ready, 2 * g + 2)
                            at_least(dve, y_done, g - 1)
                            for r in range(HPG):
                                hd = g * HPG + r
                                ins = stt(m[g % 2][:, c * 512 + r * P:c * 512 + r * P + P], decay[:, g, c, r * P:r * P + P],
                                          d["sp"][:, c, hd:hd + 1], bank[6][:, c * P:c * P + P])
                            ins.then_inc(m_ready, 1)
                        if q == 2:
                            dve.wait_ge(xn_ready, g + 1)
                            at_least(dve, state_done, g)
                            tt(xs.rearrange("p (r n) -> p r n", r=HPG),
                               xn[:, 0, :].rearrange("p (r n) -> p r n", r=HPG), heads_over(dsd, g)).then_inc(xs_ready, 1)
                for k in range(KT):
                    dve.wait_ge(unit_done, nx + SSD_UNITS + k + 1)
                    b, use = bank_use("ssd_out", k)
                    tt(x[:, k, :], bank[b][:, k // 4 * SEQ:k // 4 * SEQ + SEQ], x[:, k, :], ALU.add).then_inc(evac[b], 1)
                    split(nx + SSD_UNITS + k + AHEAD)
                    new_h(OUT_NORM["ssd_out"], k)

            nc.vector.memset(ones[:, :], 1.0).then_inc(ones_set, 1)
            step(nc.vector.memset(padded[:, 0:4], 0.0))
            dve.wait_ge(gain_in, 16)
            for k in range(KT):
                if k == 2:
                    split(0)
                if k % 2 == 0:
                    dve.wait_ge(x_in[k // 2], 16)
                new_h(0, k)
            for n in range(1, AHEAD):
                split(n)
            ffn(0)
            dve.wait_ge(cst_in, 16)
            norm("mem", rms_mem)
            conv()
            attention(0)
            ffn(1)
            ffn(2)
            ssd()
            attention(1)
            ffn(3)
            norm(NORM_FINAL)
            for k in range(KT):
                stt(a_out(k), x[:, k, :], gain(NORM_FINAL, k), rms[:, :]).then_inc(out_ready, 1)

        @block.gpsimd
        def _(pool):
            steps = [0]
            chain = [0]

            def square_sum(src, k):
                if k == 0:
                    nc.gpsimd.tensor_tensor(ssq[:, :], src, src, ALU.mult).then_inc(ssq_step, 1)
                    steps[0] += 1
                    return
                nc.gpsimd.tensor_tensor(sq[:, :], src, src, ALU.mult).then_inc(ssq_step, 1)
                steps[0] += 1
                pool.wait_ge(ssq_step, steps[0])
                nc.gpsimd.tensor_tensor(ssq[:, :], ssq[:, :], sq[:, :], ALU.add).then_inc(ssq_step, 1)
                steps[0] += 1
                pool.wait_ge(ssq_step, steps[0])

            def a_part(j, count, src):
                pool.wait_ge(ahi_ready, count + 1)
                nc.gpsimd.tensor_tensor(j(a_lo), src, j(a_hi).bitcast(F32), ALU.subtract).then_inc(a_ready, 1)

            def ffn(f):
                for j in range(2):
                    a_part(lambda t, j=j: t[:, j, :], FFN_A[f] + j, t2[j][:, :])
                with pool.Fori(1, FT // 2) as i:
                    for q in range(2):
                        a_part(lambda t, q=q: t[:, bass.ds(2 * i + q, 1), :].rearrange("p a n -> p (a n)"),
                               FFN_A[f] + 2 * i + q, t2[q][:, :])
                if f == 0:
                    pool.wait_ge(mem_in, 16)
                    pool.wait_ge(ss_done, 1)
                    for k in range(KT):
                        square_sum(mem[:, k, :], k)
                    pool.wait_ge(ss_done, 2)
                project_out(f"down{f}")

            def project_out(phase):
                for k in range(KT):
                    pool.wait_ge(*x_signal(phase, k))
                    square_sum(x[:, k, :], k)

            def attention(layer):
                for k in range(KT):
                    a_part(lambda t, k=k: t[:, KT + k, :], Q_A[layer] + k, t2[k % 2][:, :])
                project_out(f"o{layer}")

            def inverse_root_y():
                def step(ins, done=pool_step):
                    ins.then_inc(done, 1)
                    if done is pool_step:
                        chain[0] += 1
                        pool.wait_ge(pool_step, chain[0])
                r, v, w = rms_y[:, :], var_y[:, :], root_y[:, :]
                step(nc.gpsimd.tensor_scalar(v, sum_y[:, :], 1.0 / GW, EPS, ALU.mult, ALU.add))
                step(nc.gpsimd.tensor_scalar(r.bitcast(mybir.dt.int32), v.bitcast(mybir.dt.int32), -0.5, float(0x5f3759df), ALU.mult, ALU.add))
                for i in range(3):
                    step(nc.gpsimd.tensor_tensor(w, v, r, ALU.mult))
                    step(nc.gpsimd.tensor_tensor(w, w, r, ALU.mult))
                    step(nc.gpsimd.tensor_scalar(w, w, -0.5, 1.5, ALU.mult, ALU.add))
                    step(nc.gpsimd.tensor_tensor(r, w, r, ALU.mult), rmsy_ready if i == 2 else pool_step)

            def ssd():
                for t in range(SSD_STEPS):
                    G, q = divmod(t, 4)
                    g = G - 3
                    if 0 <= g < GROUPS and q == 2:
                        pool.wait_ge(ysq_ready, 2 * g + 2)
                        at_least(pool, yn_ready, 2 * g)
                        inverse_root_y()
                    g = G - 3
                    if 0 <= g < GROUPS and q == 0:
                        pool.wait_ge(yoff_ready, g + 1)
                        pool.wait_ge(y_added, g + 1)
                        nc.gpsimd.tensor_tensor(y[g % 2][:, 1, :], y[g % 2][:, 1, :], y_off, ALU.add).then_inc(ysum_ready, 1)
                        pool.wait_ge(ysum_ready, g + 1)
                        pool.wait_ge(zs_ready, g + 1)
                        nc.gpsimd.tensor_tensor(y[g % 2][:, :, :], y[g % 2][:, :, :], zs[:, :, :], ALU.mult).then_inc(y_ready, 1)
                project_out("ssd_out")

            for k in range(KT // 2):
                if k % 2 == 0:
                    pool.wait_ge(x_in[k // 2], 16)
                square_sum(x[:, k, :], k)
            for k in range(KT // 2):
                pool.wait_ge(square_ready, k + 1)
                nc.gpsimd.tensor_tensor(ssq[:, :], ssq[:, :], first_squares[k], ALU.add).then_inc(ssq_step, 1)
                steps[0] += 1
                pool.wait_ge(ssq_step, steps[0])
            ffn(0)
            for k in range(KT):
                a_part(lambda t, k=k: t[:, k, :], CONV_A + k, t2[k % 2][:, :])
            project_out("conv_out")
            attention(0)
            ffn(1)
            ffn(2)
            ssd()
            attention(1)
            ffn(3)

        @block.tensor
        def _(pe):
            def mm(out, lhs, rhs, start, stop, check=False):
                return nc.tensor.matmul(out, lhs, rhs, start=start, stop=stop, skip_group_check=check)

            def three(out, lh, ll, rh, rl, start, stop, check=False):
                mm(out, lh, rh, start, False, check)
                mm(out, lh, rl, False, False, check)
                return mm(out, ll, rh, False, stop, check)

            def half(out, k):
                return out[:, k // 4 * SEQ:k // 4 * SEQ + SEQ]

            def unit(n, out, blocks, k0, r_hi, r_lo, start, stop, i=0, ready=None, check=False):
                s = n % SLOTS
                pe.wait_ge(lo_ready, n + 1 + SLOTS * i)
                for k in range(blocks):
                    if ready:
                        pe.wait_ge(ready[0], ready[1] + k0 + k + 1)
                    w = slice(k * P, k * P + P)
                    ins = three(out[:, 0:SEQ], w_hi[s][:, w], w_lo[s][:, w], r_hi[:, k0 + k, :], r_lo[:, k0 + k, :],
                                start and k == 0, stop and k == blocks - 1, check)
                ins.then_inc(unit_done, 1)

            def norm(b):
                pe.wait_ge(ssq_step, ssq_count(b))
                at_least(pe, var_ready, SS_INDEX[b])
                ins = mm(bank[4][:, 0:SEQ], ones[:, :], ssq[:, :], True, True)
                if b == NORM_MIX1:
                    for t in range(2):
                        ins = mm(bank[4][:, 256 + 2 * t:258 + 2 * t], ssq[:, t * P:t * P + P], ones[:, 0:2], True, True)
                ins.then_inc(ss_done, 1)

            def free(phase, t, banks=4, i=0):
                b, use = bank_use(phase, t, banks)
                at_least(pe, evac[b], use + i)
                return bank[b]

            def ffn(f):
                b = {0: 0, 1: 3, 2: 4, 3: 7}[f]
                n0, name = first[f"gu{f}"], f"gu{f}"
                for s in range(4):
                    unit(n0 + s, free(name, s), KT, 0, h_hi, h_lo, True, True, ready=(h_ready, H_FIRST[b]) if s == 0 else None)
                    if s == 0:
                        norm(b)
                with pe.Fori(1, FT // 2) as i:
                    for s in range(4):
                        unit(n0 + s, free(name, s, i=i), KT, 0, h_hi, h_lo, True, True, i)
                name = f"down{f}"
                n0 = first[name]
                half = FT // 2

                def pair(i, ready):
                    for t in range(2):
                        out = free(name, t, 2, i)
                        for u in range(2):
                            unit(n0 + 2 * t + u, out, half, u * half, a_hi, a_lo, u == 0, u == 1, i, ready if t == 0 else None)

                pair(0, (a_ready, FFN_A[f]))
                if f == 0:
                    norm("mem")
                with pe.Fori(1, KT // 2) as i:
                    pair(i, None)

            def project(name, b, tiles=KT, extra=None):
                for t in range(tiles):
                    unit(first[name] + t, free(name, t), KT, 0, h_hi, h_lo, True, True, ready=(h_ready, H_FIRST[b]) if t == 0 else None)
                    if t == 0:
                        norm(b)

            def scores(h):
                for t in range(2):
                    for k in range(2):
                        lq = slice(t * P, t * P + P)
                        ins = three(bank[5][:, t * 256:t * 256 + 256], a_hi[:, KT + 2 * h + k, lq], a_lo[:, KT + 2 * h + k, lq],
                                    k_hi[:, 2 * h + k, :], k_lo[:, 2 * h + k, :], k == 0, k == 1)
                ins.then_inc(s_done, 1)

            def turn(layer, h):
                pe.wait_ge(probs_ready, 2 * (HEADS * layer + h) + 2)
                at_least(pe, pt_ready, HEADS * layer + h)
                for mt in range(2):
                    for t in range(2):
                        ins = nc.tensor.transpose(bank[6][:, mt * 256 + t * P:mt * 256 + t * P + P],
                                                  probs[h][:, t, mt * P:mt * P + P], cst[:, C_EYE:C_EYE + P])
                ins.then_inc(pt_done, 1)

            def values(layer, h):
                pe.wait_ge(pt_ready, HEADS * layer + h + 1)
                at_least(pe, o_ready, HEADS * layer + h)
                for t in range(2):
                    cols = slice(h * HEAD_W + t * P, h * HEAD_W + t * P + P)
                    for mt in range(2):
                        ins = three(bank[7][:, t * SEQ:t * SEQ + SEQ], v_hi[:, mt, cols], v_lo[:, mt, cols],
                                    pt_hi[:, mt, :], pt_lo[:, mt, :], mt == 0, mt == 1)
                ins.then_inc(o_done, 1)

            def natural_unit(n, outs, k0, l_hi, l_lo, start, stop):
                s = n % SLOTS
                pe.wait_ge(lo_ready, n + 1)
                for k in range(4):
                    w = slice(k * 256, k * 256 + 256)
                    for t in range(2):
                        lt = slice(t * P, t * P + P)
                        ins = three(outs[t][:, 0:256], l_hi[:, k0 + k, lt], l_lo[:, k0 + k, lt], w_hi[s][:, w], w_lo[s][:, w],
                                    start and k == 0, stop and k == 3)
                ins.then_inc(unit_done, 1)

            def attention(layer):
                n0 = first[f"q{layer}"]
                b = 2 if layer == 0 else 6
                project(f"q{layer}", b)
                for s in range(KT, 24):
                    if s < 2 * KT:
                        t = s - KT
                        unit(n0 + s, free(f"k{layer}", t), KT, 0, mn_hi, mn_lo, True, True,
                             ready=(mem_lo, KT * layer) if t == 0 else None)
                    else:
                        c, u = divmod(s - 2 * KT, 2)
                        if u == 0:
                            outs = [free(f"v{layer}", 2 * c + t) for t in range(2)]
                        natural_unit(n0 + s, outs, 4 * u, mn_hi, mn_lo, u == 0, u == 1)
                    for h in range(HEADS):
                        if s == 10 + 2 * h:
                            pe.wait_ge(a_ready, Q_A[layer] + 2 * h + 2)
                            for t in range(2 * h, 2 * h + 2):
                                kb, use = bank_use(f"k{layer}", t)
                                pe.wait_ge(evac[kb], use + 1)
                            at_least(pe, exp_ready, 2 * (HEADS * layer + h))
                            scores(h)
                        if s == 17 + 2 * h:
                            turn(layer, h)
                        if s == 18 + 2 * h:
                            wait_v(layer, h)
                            values(layer, h)
                early = 2 * HEADS - 2
                output_tile(layer, 0, 0, early)
                wait_v(layer, 3)
                values(layer, 3)
                output_tile(layer, 1, 0, early)
                for t in range(KT):
                    output_tile(layer, t, early if t < 2 else 0, KT)

            def output_tile(layer, t, k0, k1):
                n = first[f"o{layer}"] + t
                if k0 == 0:
                    free(f"o{layer}", t)
                    pe.wait_ge(lo_ready, n + 1)
                for k in range(k0, k1):
                    if t == 0 and k % 2 == 0:
                        pe.wait_ge(o_ready, HEADS * layer + k // 2 + 1)
                    w = slice(k * P, k * P + P)
                    ins = three(bank[t % 4][:, 0:SEQ], w_hi[n % SLOTS][:, w], w_lo[n % SLOTS][:, w], a_hi[:, k, :], a_lo[:, k, :],
                                k == 0, k == KT - 1)
                if k1 == KT:
                    ins.then_inc(unit_done, 1)

            def wait_v(layer, h):
                for mt in range(2):
                    vb, use = bank_use(f"v{layer}", 2 * h + mt)
                    pe.wait_ge(evac[vb], use + 1)

            def decays(l):
                g, c = l // 2, l % 2
                at_least(pe, decay_ready, l - 1)
                out = bank[5 + l % 2]
                mm(out[:, :].rearrange("p (r n) -> p r n", r=HPG), eye_r[:, :], mask_r[:, :].unsqueeze(1).broadcast_to((P, HPG, CHUNK)), True, False, True)
                for r in range(HPG):
                    hd = g * HPG + r
                    ins = mm(out[:, r * P:r * P + P], d["da"][:, c, hd:hd + 1].broadcast_to((P, P)), tri, False, r == HPG - 1, True)
                ins.then_inc(l_done, 1)

            def ssd():
                nz = first["z"]
                lcount = 0
                for s in range(16):
                    c, u = divmod(s, 2)
                    if u == 0:
                        outs = [free("z", 2 * c + t) for t in range(2)]
                    if s == 0:
                        for k in range(KT):
                            pe.wait_ge(h_ready, H_FIRST[NORM_MIX1] + k + 1)
                    natural_unit(nz + s, outs, 4 * u, h_hi, h_lo, u == 0, u == 1)
                    if s == 0:
                        norm(NORM_MIX1)
                        pe.wait_ge(dt_in, 16)
                        for t in range(2):
                            lt = slice(t * P, t * P + P)
                            for k in range(KT):
                                for part in (h_hi, h_lo):
                                    ins = mm(bank[7][:, t * H:t * H + H], part[:, k, lt].bitcast(F32), wdt[:, k, :],
                                             k == 0 and part is h_hi, k == KT - 1 and part is h_lo)
                        ins.then_inc(dt_done, 1)
                    if s == 2:
                        pe.wait_ge(da_ready, 1)
                        for cc in range(2):
                            mm(bank[7][:, 64 + cc * H:64 + cc * H + H], tri, d["da"][:, cc, :], True, True)
                        mm(bank[7][:, 128:128 + H], ones[:, :], d["da"][:, 0, :], True, True).then_inc(acum_done, 1)
                    if s >= 3:
                        while lcount < min(16, (s - 2) * 16 // 12):
                            decays(lcount)
                            lcount += 1
                nx = first["xbc"]
                for t in range(SSD_STEPS):
                    G, q = divmod(t, 4)
                    if G < GROUPS:
                        unit(nx + t, free("xbc", t), KT, 0, h_hi, h_lo, True, True, ready=(h_ready, H_EXTRA) if t == 0 else None)
                    elif t < SSD_UNITS:
                        k = t - 4 * GROUPS
                        out = free("ssd_out", k) if k < 4 else bank[k % 4]
                        unit(nx + t, half(out, k), KT, 0, a_hi, a_lo, k < 4, False,
                             ready=(yt_ready, 0) if k == 0 else None, check=True)
                    g = G - 1
                    if 0 <= g < GROUPS and q == 0:
                        pe.wait_ge(xbc_ready, 4 * g + 2)
                        at_least(pe, m_ready, 2 * g)
                        at_least(pe, bn_ready, g)
                        if g == 0:
                            pe.wait_ge(decay_ready, 16)
                        for c in range(2):
                            lc = slice(c * P, c * P + P)
                            ins = mm(bank[6][:, c * P:c * P + P], act_xbc[0][:, lc], c_t[g % 3][:, lc], True, True)
                        ins.then_inc(cb_done, 1)
                        nc.tensor.transpose(bank[6][:, 256:384], act_xbc[0][:, 0:P], cst[:, C_EYE:C_EYE + P]).then_inc(cb_done, 1)
                    g = G - 4
                    if 0 <= g < GROUPS and q == 0:
                        pe.wait_ge(yn_ready, 2 * g + 2)
                        pe.wait_ge(xn_ready, min(g + 3, GROUPS))
                        pe.wait_ge(xd_ready, min(g + 3, GROUPS))
                        for u in range(2):
                            for c in range(2):
                                ins = nc.tensor.transpose(bank[5][:, u * SEQ + c * P:u * SEQ + c * P + P],
                                                          y[g % 2][:, c, u * P:u * P + P], cst[:, C_EYE:C_EYE + P])
                        ins.then_inc(yt_done, 1)
                    g = G - 2
                    if 0 <= g < GROUPS and q == 1:
                        at_least(pe, y_added, g)
                        pe.wait_ge(bn_ready, g + 1)
                        pe.wait_ge(xs_ready, g + 1)
                        at_least(pe, yoff_ready, g)
                        pe.wait_ge(small_var_ready, 1)
                        mm(bank[4][:, 0:GW], b_nat[g % 2], xs, True, True).then_inc(state_done, 1)
                        pe.wait_ge(m_ready, 2 * g + 2)
                        pe.wait_ge(xn_ready, g + 1)
                        for c in range(2):
                            for r in range(HPG):
                                mc = slice(c * 512 + r * P, c * 512 + r * P + P)
                                xc = slice(r * HD, r * HD + HD)
                                ins = mm(bank[7][:, c * GW + r * HD:c * GW + r * HD + HD], m[g % 2][:, mc], xn[:, c, xc], True, True)
                        ins.then_inc(y_done, 1)
                    if 0 <= g < GROUPS and q == 3:
                        pe.wait_ge(st_ready, g + 1)
                        mm(bank[4][:, 256:512], c_t[g % 3][:, P:2 * P], state, True, True).then_inc(yo_done, 1)
                    g = G - 1
                    if 0 <= g < GROUPS and q == 1:
                        pe.wait_ge(xbc_ready, 4 * g + 4)
                        if g == 0:
                            pe.wait_ge(decay_ready, 16)
                        at_least(pe, yt_ready, 2 * (g - 2))
                        for c in range(2):
                            for u in range(2):
                                ins = nc.tensor.transpose(bank[5][:, c * 256 + u * P:c * 256 + u * P + P],
                                                          act_xbc[2 + u][:, c * P:c * P + P], cst[:, C_EYE:C_EYE + P])
                        ins.then_inc(xt_done, 1)
                for k in range(KT):
                    out = bank[k] if k < 4 else free("ssd_out", k)
                    unit(nx + SSD_UNITS + k, half(out, k), KT, KT, a_hi, a_lo, False, True,
                         ready=(yt_ready, 0) if k == 0 else None, check=True)

            pe.wait_ge(ones_set, 1)
            ffn(0)
            pe.wait_ge(cst_in, 16)
            pe.wait_ge(consts, 2)
            project("conv_in", NORM_MIX0, 3 * KT)
            for t in range(KT):
                unit(first["conv_out"] + t, free("conv_out", t), KT, 0, a_hi, a_lo, True, True,
                     ready=(a_ready, CONV_A) if t == 0 else None)
            attention(0)
            ffn(1)
            ffn(2)
            ssd()
            attention(1)
            ffn(3)
            norm(NORM_FINAL)


def _units(w):
    k, m = w.shape
    return w.reshape(k // P, P, m // P, P).transpose(2, 1, 0, 3).reshape(m // P, P, k)


def _halves(w, parts):
    u = _units(w)
    m, _, k = u.shape
    return u.reshape(m, P, parts, k // parts).transpose(0, 2, 1, 3).reshape(m * parts, P, k // parts)


def _natural(w):
    k, m = w.shape
    return w.reshape(2, 4, P, m // 256, 256).transpose(3, 0, 2, 1, 4).reshape(m // 128, P, 1024)


def _tiles(v):
    return v.reshape(-1, P).T


def _rows(v):
    return np.broadcast_to(v.reshape(1, -1), (P, v.size))


def kernel(**inputs):
    import concourse.bacc as bacc
    from concourse.bass_utils import run_bass_kernel_spmd

    t = {k: np.asarray(v) for k, v in inputs.items()}
    gu = t["ffn_w_gate_up"].reshape(4, D_MODEL, 2, FT, P).transpose(0, 1, 3, 2, 4).reshape(4, D_MODEL, 2 * D_FF)
    conv_in = t["conv_w_in"][0].reshape(D_MODEL, 3, KT, P)[:, [1, 2, 0]].transpose(0, 2, 1, 3).reshape(D_MODEL, 3 * D_MODEL)
    ssd_in = t["ssd_w_in"][0]
    xbc = ssd_in[:, D_INNER:D_INNER + 4096].reshape(D_MODEL, 32, P)
    order = [i for g in range(GROUPS) for i in (16 + g, 24 + g, 2 * g, 2 * g + 1)]
    ones = np.ones((P, P), np.float32)
    upper = np.triu(ones)
    gains = [t["ffn_norm"][0, 0], t["mix_norm"][0], t["xa_norm"][0], t["ffn_norm"][0, 1], t["ffn_norm"][1, 0],
             t["mix_norm"][1], t["xa_norm"][1], t["ffn_norm"][1, 1], t["final_norm"], t["xa_mem_norm"][0], t["xa_mem_norm"][1]]
    small = np.concatenate([
        *[_tiles(g) for g in gains],
        t["conv_kernel"][0].reshape(3, KT, P).transpose(2, 1, 0).reshape(P, KT * 3),
        t["ssd_conv_kernel"][0].reshape(4, 32, P)[:, order].transpose(2, 1, 0).reshape(P, 128),
        t["ssd_conv_bias"][0].reshape(32, P)[order].T,
        _tiles(t["ssd_gate_norm"][0]),
        _rows(t["ssd_dt_bias"][0]), _rows(t["ssd_a_log"][0]), _rows(t["ssd_d_skip"][0]),
        np.eye(P, dtype=np.float32), upper, np.tril(np.full((P, P), MASKED, np.float32), -1)], axis=1)
    arrays = {
        "x_t": t["x"][0].T.reshape(KT, P, SEQ).transpose(1, 0, 2),
        "mem_t": t["mem"][0].T.reshape(KT, P, N_MEM).transpose(1, 0, 2),
        "small": small,
        "w_gu": np.stack([_units(w) for w in gu]),
        "w_down": np.stack([_halves(w, 2) for w in t["ffn_w_down"].reshape(4, D_FF, D_MODEL)]),
        "w_conv_in": _units(conv_in),
        "w_conv_out": _units(t["conv_w_out"][0]),
        "w_z": _natural(ssd_in[:, :D_INNER]),
        "w_xbc": _units(xbc[:, order].reshape(D_MODEL, 4096)),
        "w_dt": ssd_in[:, D_INNER + 4096:].reshape(KT, P, SSD_HEADS).transpose(1, 0, 2),
        "w_ssd_out": _halves(t["ssd_w_out"][0], 2)[[*range(0, 16, 2), *range(1, 16, 2)]],
        "w_q": np.stack([_units(w) for w in t["xa_w_q"]]),
        "w_k": np.stack([_units(w[:, :D_MODEL]) for w in t["xa_w_kv"]]),
        "w_v": np.stack([_natural(w[:, D_MODEL:]) for w in t["xa_w_kv"]]),
        "w_o": np.stack([_units(w) for w in t["xa_w_o"]]),
    }
    arrays = {k: np.ascontiguousarray(v) for k, v in arrays.items()}
    nc = bacc.Bacc("TRN2", target_bir_lowering=False, num_devices=1, dynamic_dma_scratch_size=1024)
    args = [nc.dram_tensor(k, v.shape, F32, kind="ExternalInput").ap() for k, v in arrays.items()]
    out = nc.dram_tensor("out_t", (P, KT, SEQ), F32, kind="ExternalOutput").ap()
    trunk(nc, *args, out)
    got = run_bass_kernel_spmd(nc, [arrays], core_ids=[0]).results[0]["out_t"]
    return np.asarray(got).transpose(2, 1, 0).reshape(1, SEQ, D_MODEL)
```
